# Optimizing a Trainium2 kernel written in Bass

```python
import math
import jax, jax.numpy as jnp
from jax import lax
import numpy as np

D_MODEL = 1024
BATCH = 1
SEQ = 512
DEPTH = 2

GRID_W = 64
CTX_LEN = 256
D_MIX = D_MODEL
D_RWKV = D_MIX // 4
RWKV_HEAD_DIM = 64
RWKV_HEADS = D_RWKV // RWKV_HEAD_DIM
DECAY_LORA = 64
ICL_LORA = 64
D_CONV = D_MIX // 4
CONV_WIDTH = 3
D_ATTN = D_MIX // 2
DIFF_HEAD_DIM = 64
DIFF_V_DIM = 2 * DIFF_HEAD_DIM
DIFF_HEADS = D_ATTN // DIFF_V_DIM
Q_BLOCK = 128
ROPE_THETA = 10000.0
ROPE_AXIS_DIM = DIFF_HEAD_DIM // 2
NORM_EPS = 1e-6
RWKV_GN_EPS = 64e-5
IN_SPLITS = (D_RWKV, D_RWKV, D_RWKV, DECAY_LORA, DECAY_LORA, ICL_LORA, ICL_LORA, D_RWKV,
             D_CONV, D_CONV, D_CONV, D_CONV,
             D_ATTN, D_ATTN, D_ATTN, D_ATTN)
D_IN = 4 * D_RWKV + 2 * DECAY_LORA + 2 * ICL_LORA + 4 * D_CONV + 4 * D_ATTN


def rms_norm(x, g):
    xf = x.astype(jnp.float32)
    y = xf * lax.rsqrt(jnp.mean(xf * xf, axis=-1, keepdims=True) + NORM_EPS)
    return (y * g.astype(jnp.float32)).astype(x.dtype)

def modulation(cond, mod_w, mod_b):
    m = jax.nn.silu(cond) @ mod_w + mod_b
    return jnp.split(m, 3, axis=-1)

def split_projection(u):
    idx = np.cumsum(IN_SPLITS)[:-1].tolist()
    return jnp.split(u, idx, axis=-1)

def axial_rope_tables(seq_len):
    rows = seq_len // GRID_W
    row = jnp.repeat(jnp.arange(rows, dtype=jnp.float32), GRID_W)
    col = jnp.tile(jnp.arange(GRID_W, dtype=jnp.float32), rows)
    inv_freq = ROPE_THETA ** (-jnp.arange(0, ROPE_AXIS_DIM, 2, dtype=jnp.float32) / ROPE_AXIS_DIM)
    ang_r = row[:, None] * inv_freq
    ang_c = col[:, None] * inv_freq
    return (jnp.cos(ang_r), jnp.sin(ang_r), jnp.cos(ang_c), jnp.sin(ang_c))

def rotate(x, cos, sin):
    half = x.shape[-1] // 2
    x1, x2 = x[..., :half], x[..., half:]
    return jnp.concatenate([x1 * cos - x2 * sin, x2 * cos + x1 * sin], axis=-1)

def apply_axial_rope(x, tables):
    cos_r, sin_r, cos_c, sin_c = (t[None, :, None, None, :] for t in tables)
    xf = x.astype(jnp.float32)
    out = jnp.concatenate([rotate(xf[..., :ROPE_AXIS_DIM], cos_r, sin_r),
                           rotate(xf[..., ROPE_AXIS_DIM:], cos_c, sin_c)], axis=-1)
    return out.astype(x.dtype)

def to_heads(t):
    return t.reshape(t.shape[0], t.shape[1], RWKV_HEADS, RWKV_HEAD_DIM)

def rwkv_direction_inputs(parts, d, w0, w_up, a0, a_up, k_k, k_a):
    r, k, v, lw_f, lw_b, la_f, la_b, _ = parts
    lw = lw_f if d == 0 else lw_b
    la = la_f if d == 0 else la_b
    w = -jax.nn.softplus(-(w0[d] + jnp.tanh(lw) @ w_up[d])) - 0.5
    decay = jnp.exp(-jnp.exp(w))
    a = jax.nn.sigmoid(a0[d] + la @ a_up[d])
    kk = to_heads(k * k_k)
    kk = kk / jnp.maximum(jnp.linalg.norm(kk, axis=-1, keepdims=True), 1e-12)
    k_mod = k * (1.0 + (a - 1.0) * k_a)
    return (to_heads(r), to_heads(decay), to_heads(k_mod), to_heads(v), -kk, kk * to_heads(a))

def rwkv_scan(state0, terms, reverse, with_output):
    seq_terms = terms if with_output else terms[1:]
    xs = tuple(jnp.moveaxis(t, 1, 0) for t in seq_terms)

    def step(S, inp):
        w_t, k_t, v_t, a_t, b_t = inp[-5:]
        sa = jnp.einsum('bhvk,bhk->bhv', S, a_t)
        S = S * w_t[:, :, None, :] + sa[..., None] * b_t[:, :, None, :] + v_t[..., None] * k_t[:, :, None, :]
        y_t = jnp.einsum('bhvk,bhk->bhv', S, inp[0]) if with_output else None
        return S, y_t

    S, ys = lax.scan(step, state0, xs, reverse=reverse)
    return S, (jnp.moveaxis(ys, 0, 1) if with_output else None)

def rwkv_readout(ys, ks, parts, r_k, ln_g, ln_b):
    r, v, z = to_heads(parts[0]), to_heads(parts[2]), parts[7]
    y = ys[0] + ys[1]
    mu = jnp.mean(y, axis=-1, keepdims=True)
    var = jnp.mean(jnp.square(y - mu), axis=-1, keepdims=True)
    y = (y - mu) * lax.rsqrt(var + RWKV_GN_EPS)
    B, T = y.shape[0], y.shape[1]
    y = y.reshape(B, T, D_RWKV) * ln_g + ln_b
    bonus = jnp.sum(r * (ks[0] + ks[1]) * r_k, axis=-1, keepdims=True) * v
    y = y + bonus.reshape(B, T, D_RWKV)
    return y * jax.nn.silu(z)

def rwkv_mixer(lat, ctx, w0, w_up, a0, a_up, k_k, k_a, r_k, ln_g, ln_b, need_ctx_out):
    f32 = jnp.float32
    lat = [t.astype(f32) for t in lat]
    ctx = [t.astype(f32) for t in ctx]
    w0, w_up, a0, a_up, k_k, k_a, r_k, ln_g, ln_b = (
        p.astype(f32) for p in (w0, w_up, a0, a_up, k_k, k_a, r_k, ln_g, ln_b))
    B = lat[0].shape[0]
    state0 = jnp.zeros((B, RWKV_HEADS, RWKV_HEAD_DIM, RWKV_HEAD_DIM), f32)
    ys_l, ks_l, ys_c, ks_c = [], [], [], []
    for d, reverse in ((0, False), (1, True)):
        tc = rwkv_direction_inputs(ctx, d, w0, w_up, a0, a_up, k_k, k_a)
        tl = rwkv_direction_inputs(lat, d, w0, w_up, a0, a_up, k_k, k_a)
        s_ctx, y_c = rwkv_scan(state0, tc, reverse, need_ctx_out)
        _, y_l = rwkv_scan(s_ctx, tl, reverse, True)
        ys_l.append(y_l)
        ks_l.append(tl[2])
        ys_c.append(y_c)
        ks_c.append(tc[2])
    out_l = rwkv_readout(ys_l, ks_l, lat, r_k, ln_g, ln_b)
    out_c = rwkv_readout(ys_c, ks_c, ctx, r_k, ln_g, ln_b) if need_ctx_out else None
    return out_l, out_c

def short_conv_mixer(b_gate, c_gate, h, z, conv_w):
    u = c_gate * h
    T = u.shape[1]
    up = jnp.pad(u, ((0, 0), (CONV_WIDTH // 2, CONV_WIDTH // 2), (0, 0)))
    y = up[:, 0:T] * conv_w[0]
    for j in range(1, CONV_WIDTH):
        y = y + up[:, j:j + T] * conv_w[j]
    return b_gate * y * jax.nn.silu(z)

def diff_attend(q, k, v, lam, scale):
    s = jnp.einsum('bqhjd,bkhjd->bhjqk', q, k).astype(jnp.float32) * scale
    p = jax.nn.softmax(s, axis=-1)
    attn = p[:, :, 0] - lam * p[:, :, 1]
    return jnp.einsum('bhqk,bkhe->bqhe', attn.astype(v.dtype), v)

def diff_attention_mixer(lat, ctx, diff_lambda, subln_g, rope, layer_idx, need_ctx_out):
    q_l, k_l, v_l, z_l = lat
    q_c, k_c, v_c, z_c = ctx
    B, T = q_l.shape[0], q_l.shape[1]

    def qk_heads(t):
        return t.reshape(t.shape[0], t.shape[1], DIFF_HEADS, 2, DIFF_HEAD_DIM)

    def v_heads(t):
        return t.reshape(t.shape[0], t.shape[1], DIFF_HEADS, DIFF_V_DIM)

    q_l = apply_axial_rope(qk_heads(q_l), rope)
    k_l = apply_axial_rope(qk_heads(k_l), rope)
    v_l = v_heads(v_l)
    q_c, k_c, v_c = qk_heads(q_c), qk_heads(k_c), v_heads(v_c)

    lam_init = 0.8 - 0.6 * math.exp(-0.3 * layer_idx)
    lf = diff_lambda.astype(jnp.float32)
    lam = jnp.exp(jnp.sum(lf[0] * lf[1])) - jnp.exp(jnp.sum(lf[2] * lf[3])) + lam_init
    scale = DIFF_HEAD_DIM ** -0.5

    def finish(o, z):
        o = rms_norm(o, subln_g) * (1.0 - lam_init)
        return o.reshape(o.shape[0], o.shape[1], D_ATTN) * jax.nn.silu(z)

    k_all = jnp.concatenate([k_l, k_c], axis=1)
    v_all = jnp.concatenate([v_l, v_c], axis=1)
    nb = T // Q_BLOCK
    qb = jnp.moveaxis(q_l.reshape(B, nb, Q_BLOCK, DIFF_HEADS, 2, DIFF_HEAD_DIM), 1, 0)
    o = lax.map(lambda qblk: diff_attend(qblk, k_all, v_all, lam, scale), qb)
    o = jnp.moveaxis(o, 0, 1).reshape(B, T, DIFF_HEADS, DIFF_V_DIM)
    out_l = finish(o, z_l)
    out_c = finish(diff_attend(q_c, k_c, v_c, lam, scale), z_c) if need_ctx_out else None
    return out_l, out_c

def hybrid_layer(x, xc, c, c_ctx, mod_w, mod_b, pre_g, post_g, w_in, w_out,
                 rwkv_w0, rwkv_w_up, rwkv_a0, rwkv_a_up, rwkv_k_k, rwkv_k_a, rwkv_r_k,
                 rwkv_ln_g, rwkv_ln_b, conv_w, diff_lambda, diff_subln_g,
                 rope, layer_idx, need_ctx_out):
    shift, scale, gate = modulation(c, mod_w, mod_b)
    shift_c, scale_c, gate_c = modulation(c_ctx, mod_w, mod_b)
    h = rms_norm(x, pre_g) * (1.0 + scale[:, None, :]) + shift[:, None, :]
    hc = rms_norm(xc, pre_g) * (1.0 + scale_c) + shift_c
    p_l = split_projection(h @ w_in)
    p_c = split_projection(hc @ w_in)

    y_rwkv_l, y_rwkv_c = rwkv_mixer(p_l[0:8], p_c[0:8], rwkv_w0, rwkv_w_up, rwkv_a0, rwkv_a_up,
                                    rwkv_k_k, rwkv_k_a, rwkv_r_k, rwkv_ln_g, rwkv_ln_b, need_ctx_out)
    y_conv_l = short_conv_mixer(*p_l[8:12], conv_w)
    y_attn_l, y_attn_c = diff_attention_mixer(p_l[12:16], p_c[12:16], diff_lambda, diff_subln_g,
                                              rope, layer_idx, need_ctx_out)

    y_l = jnp.concatenate([y_rwkv_l.astype(x.dtype), y_conv_l, y_attn_l], axis=-1) @ w_out
    x = x + gate[:, None, :] * rms_norm(y_l, post_g)
    if need_ctx_out:
        y_conv_c = short_conv_mixer(*p_c[8:12], conv_w)
        y_c = jnp.concatenate([y_rwkv_c.astype(xc.dtype), y_conv_c, y_attn_c], axis=-1) @ w_out
        xc = xc + gate_c * rms_norm(y_c, post_g)
    return x, xc

def first_inputs(seed: int = 0) -> dict:
    key = jax.random.key(seed)
    ks = jax.random.split(key, 24)
    f32 = jnp.float32
    L = DEPTH

    def nrm(k, shape, s):
        return jax.random.normal(k, shape, f32) * s

    return {
        'x': nrm(ks[0], (BATCH, SEQ, D_MODEL), 1.0),
        'c': nrm(ks[1], (BATCH, D_MODEL), 1.0),
        'ctx': nrm(ks[2], (BATCH, CTX_LEN, D_MODEL), 1.0),
        'c_ctx': nrm(ks[3], (D_MODEL,), 1.0),
        'mod_w': nrm(ks[4], (L, D_MODEL, 3 * D_MODEL), 0.5 * D_MODEL ** -0.5),
        'mod_b': nrm(ks[5], (L, 3 * D_MODEL), 0.01),
        'norm_pre_g': 1.0 + nrm(ks[6], (L, D_MODEL), 0.05),
        'norm_post_g': 1.0 + nrm(ks[7], (L, D_MODEL), 0.05),
        'w_in': nrm(ks[8], (L, D_MODEL, D_IN), D_MODEL ** -0.5),
        'w_out': nrm(ks[9], (L, D_MIX, D_MODEL), D_MIX ** -0.5),
        'rwkv_w0': jax.random.uniform(ks[10], (L, 2, D_RWKV), f32, -6.0, -1.0),
        'rwkv_w_up': nrm(ks[11], (L, 2, DECAY_LORA, D_RWKV), 0.05),
        'rwkv_a0': nrm(ks[12], (L, 2, D_RWKV), 0.5),
        'rwkv_a_up': nrm(ks[13], (L, 2, ICL_LORA, D_RWKV), 0.3 * ICL_LORA ** -0.5),
        'rwkv_k_k': 0.85 + nrm(ks[14], (L, D_RWKV), 0.05),
        'rwkv_k_a': 1.0 + nrm(ks[15], (L, D_RWKV), 0.05),
        'rwkv_r_k': nrm(ks[16], (L, RWKV_HEADS, RWKV_HEAD_DIM), 0.1),
        'rwkv_ln_g': 1.0 + nrm(ks[17], (L, D_RWKV), 0.05),
        'rwkv_ln_b': nrm(ks[18], (L, D_RWKV), 0.01),
        'conv_w': nrm(ks[19], (L, CONV_WIDTH, D_CONV), CONV_WIDTH ** -0.5),
        'diff_lambda': nrm(ks[20], (L, 4, DIFF_HEAD_DIM), 0.1),
        'diff_subln_g': 1.0 + nrm(ks[21], (L, DIFF_V_DIM), 0.05),
    }

def first_block(x, c, ctx, c_ctx, mod_w, mod_b, norm_pre_g, norm_post_g, w_in, w_out,
              rwkv_w0, rwkv_w_up, rwkv_a0, rwkv_a_up, rwkv_k_k, rwkv_k_a, rwkv_r_k,
              rwkv_ln_g, rwkv_ln_b, conv_w, diff_lambda, diff_subln_g):
    rope = axial_rope_tables(x.shape[1])
    xc = ctx
    for l in range(DEPTH):
        x, xc = hybrid_layer(x, xc, c, c_ctx, mod_w[l], mod_b[l], norm_pre_g[l], norm_post_g[l],
                             w_in[l], w_out[l], rwkv_w0[l], rwkv_w_up[l], rwkv_a0[l], rwkv_a_up[l],
                             rwkv_k_k[l], rwkv_k_a[l], rwkv_r_k[l], rwkv_ln_g[l], rwkv_ln_b[l],
                             conv_w[l], diff_lambda[l], diff_subln_g[l],
                             rope, l, l < DEPTH - 1)
    return x


CHUNK = 64
N_LEFT_CHUNKS = 8
BAND = (N_LEFT_CHUNKS + 1) * CHUNK
HEAD_DIM = 64
N_HEADS_A = 8
N_HEADS_B = 8
A_W = N_HEADS_A * HEAD_DIM
B_W = N_HEADS_B * HEAD_DIM
MIX_W = A_W + B_W
REL_CLIP = 256
LRU_WIDTH = D_MODEL
LRU_BLOCKS = 4
LRU_BLOCK_W = LRU_WIDTH // LRU_BLOCKS
CONV_WIDTH_2 = 4
LRU_C = 8.0
D_FF = -(-(8 * D_MODEL) // (3 * 256)) * 256
RMS_EPS = 1e-6
N_ATTN_LAYERS = (DEPTH + 1) // 2
N_REC_LAYERS = DEPTH // 2


def rmsnorm(x, g):
    xf = x.astype(jnp.float32)
    y = xf * lax.rsqrt(jnp.mean(xf * xf, axis=-1, keepdims=True) + RMS_EPS)
    return (y * g.astype(jnp.float32)).astype(x.dtype)

def chunked_relpos_attention(q, k, v, rel_bias):
    b, s, h, dh = q.shape
    nc = s // CHUNK
    qc = q.reshape(b, nc, CHUNK, h, dh)

    def gather_band(t):
        tc = t.reshape(b, nc, CHUNK, h, dh)
        tp = jnp.pad(tc, ((0, 0), (N_LEFT_CHUNKS, 0), (0, 0), (0, 0), (0, 0)))
        return jnp.concatenate([tp[:, j:j + nc] for j in range(N_LEFT_CHUNKS + 1)], axis=2)

    kb, vb = gather_band(k), gather_band(v)
    scores = jnp.einsum('bcqhd,bckhd->bhcqk', qc, kb).astype(jnp.float32) * (dh ** -0.5)
    qpos = N_LEFT_CHUNKS * CHUNK + jnp.arange(CHUNK)
    kpos = jnp.arange(BAND)
    rel = jnp.clip(qpos[:, None] - kpos[None, :], -REL_CLIP, REL_CLIP) + REL_CLIP
    bias = rel_bias[:, rel].astype(jnp.float32)
    key_chunk = jnp.arange(nc)[:, None] - N_LEFT_CHUNKS + (kpos // CHUNK)[None, :]
    valid = key_chunk >= 0
    scores = scores + bias[None, :, None, :, :]
    scores = jnp.where(valid[None, None, :, None, :], scores, -jnp.inf)
    p = jax.nn.softmax(scores, axis=-1).astype(v.dtype)
    o = jnp.einsum('bhcqk,bckhd->bcqhd', p, vb)
    return o.reshape(b, s, h * dh)

def stick_breaking_attention(q, k, v):
    b, s, h, dh = q.shape
    nb = s // Q_BLOCK
    scale = dh ** -0.5
    kpos = jnp.arange(s)
    q_blocks = q.reshape(b, nb, Q_BLOCK, h, dh).transpose(1, 0, 2, 3, 4)

    def one_block(args):
        q_blk, blk = args
        z = jnp.einsum('bqhd,bkhd->bhqk', q_blk, k).astype(jnp.float32) * scale
        qpos = blk * Q_BLOCK + jnp.arange(Q_BLOCK)
        causal = kpos[None, :] < qpos[:, None]
        log_beta = jax.nn.log_sigmoid(z)
        log_1m_beta = jnp.where(causal, jax.nn.log_sigmoid(-z), 0.0)
        after = lax.cumsum(log_1m_beta, axis=3, reverse=True) - log_1m_beta
        w = jnp.where(causal, jnp.exp(log_beta + after), 0.0).astype(v.dtype)
        return jnp.einsum('bhqk,bkhd->bqhd', w, v)

    o = lax.map(one_block, (q_blocks, jnp.arange(nb)))
    return o.transpose(1, 0, 2, 3, 4).reshape(b, s, h * dh)

def attention_mixer(h, w_in, rel_bias, w_out):
    b, s, _ = h.shape
    proj = h @ w_in
    part_a, part_b = proj[..., :3 * A_W], proj[..., 3 * A_W:]
    qa, ka, va = [t.reshape(b, s, N_HEADS_A, HEAD_DIM) for t in jnp.split(part_a, 3, axis=-1)]
    qs, ks, vs = [t.reshape(b, s, N_HEADS_B, HEAD_DIM) for t in jnp.split(part_b, 3, axis=-1)]
    out_a = chunked_relpos_attention(qa, ka, va, rel_bias)
    out_b = stick_breaking_attention(qs, ks, vs)
    return jnp.concatenate([out_a, out_b], axis=-1) @ w_out

def recurrent_mixer(h, w_in, conv_w, conv_b, w_a, b_a, w_i, b_i, lam, w_out):
    b, s, _ = h.shape
    proj = h @ w_in
    gate, xr = jnp.split(proj, 2, axis=-1)
    gate = jax.nn.gelu(gate, approximate=True)
    xc = lax.conv_general_dilated(
        xr, conv_w, window_strides=(1,), padding=[(CONV_WIDTH_2 - 1, 0)],
        dimension_numbers=('NWC', 'WIO', 'NWC'), feature_group_count=LRU_WIDTH) + conv_b
    xg = xc.reshape(b, s, LRU_BLOCKS, LRU_BLOCK_W)
    r = jax.nn.sigmoid(jnp.einsum('bsni,nij->bsnj', xg, w_a) + b_a).reshape(b, s, LRU_WIDTH)
    i = jax.nn.sigmoid(jnp.einsum('bsni,nij->bsnj', xg, w_i) + b_i).reshape(b, s, LRU_WIDTH)
    log_a = -LRU_C * r.astype(jnp.float32) * jax.nn.softplus(-lam.astype(jnp.float32))
    a = jnp.exp(log_a)
    mult = jnp.sqrt(-jnp.expm1(2.0 * log_a))
    u = mult * (i * xc).astype(jnp.float32)

    def combine(left, right):
        a1, b1 = left
        a2, b2 = right
        return a1 * a2, a2 * b1 + b2

    _, hs = lax.associative_scan(combine, (a, u), axis=1)
    return (hs.astype(h.dtype) * gate) @ w_out

def swiglu(h, w_gate, w_up, w_down):
    return (jax.nn.silu(h @ w_gate) * (h @ w_up)) @ w_down

def second_inputs(seed: int = 0) -> dict:
    key = jax.random.key(seed)
    ks = jax.random.split(key, 24)
    f32 = jnp.float32

    def nrm(k, shape, fan_in):
        return jax.random.normal(k, shape, f32) * (fan_in ** -0.5)

    def gain(k, shape):
        return 1.0 + 0.05 * jax.random.normal(k, shape, f32)

    u = jax.random.uniform(ks[12], (N_REC_LAYERS, LRU_WIDTH), f32, 0.9, 0.999)
    base = u ** (1.0 / LRU_C)
    lam = jnp.log(base) - jnp.log1p(-base)
    return {
        'x': jax.random.normal(ks[0], (BATCH, SEQ, D_MODEL), f32),
        'attn_w_in': nrm(ks[1], (N_ATTN_LAYERS, D_MODEL, 3 * MIX_W), D_MODEL),
        'attn_rel_bias': 0.2 * jax.random.normal(ks[2], (N_ATTN_LAYERS, N_HEADS_A, 2 * REL_CLIP + 1), f32),
        'attn_w_out': nrm(ks[3], (N_ATTN_LAYERS, MIX_W, D_MODEL), MIX_W),
        'rg_w_in': nrm(ks[4], (N_REC_LAYERS, D_MODEL, 2 * LRU_WIDTH), D_MODEL),
        'rg_conv_w': nrm(ks[5], (N_REC_LAYERS, CONV_WIDTH_2, 1, LRU_WIDTH), CONV_WIDTH_2),
        'rg_conv_b': 0.01 * jax.random.normal(ks[6], (N_REC_LAYERS, LRU_WIDTH), f32),
        'rg_w_a': nrm(ks[7], (N_REC_LAYERS, LRU_BLOCKS, LRU_BLOCK_W, LRU_BLOCK_W), LRU_BLOCK_W),
        'rg_b_a': 0.01 * jax.random.normal(ks[8], (N_REC_LAYERS, LRU_BLOCKS, LRU_BLOCK_W), f32),
        'rg_w_i': nrm(ks[9], (N_REC_LAYERS, LRU_BLOCKS, LRU_BLOCK_W, LRU_BLOCK_W), LRU_BLOCK_W),
        'rg_b_i': 0.01 * jax.random.normal(ks[10], (N_REC_LAYERS, LRU_BLOCKS, LRU_BLOCK_W), f32),
        'rg_lambda': lam,
        'rg_w_out': nrm(ks[11], (N_REC_LAYERS, LRU_WIDTH, D_MODEL), LRU_WIDTH),
        'norm_mix_pre': gain(ks[13], (DEPTH, D_MODEL)),
        'norm_mix_post': gain(ks[14], (DEPTH, D_MODEL)),
        'norm_ffn_pre': gain(ks[15], (DEPTH, D_MODEL)),
        'norm_ffn_post': gain(ks[16], (DEPTH, D_MODEL)),
        'ffn_w_gate': nrm(ks[17], (DEPTH, D_MODEL, D_FF), D_MODEL),
        'ffn_w_up': nrm(ks[18], (DEPTH, D_MODEL, D_FF), D_MODEL),
        'ffn_w_down': nrm(ks[19], (DEPTH, D_FF, D_MODEL), D_FF),
    }

def second_block(x, attn_w_in, attn_rel_bias, attn_w_out, rg_w_in, rg_conv_w, rg_conv_b,
              rg_w_a, rg_b_a, rg_w_i, rg_b_i, rg_lambda, rg_w_out,
              norm_mix_pre, norm_mix_post, norm_ffn_pre, norm_ffn_post,
              ffn_w_gate, ffn_w_up, ffn_w_down):
    for layer in range(DEPTH):
        j = layer // 2
        h = rmsnorm(x, norm_mix_pre[layer])
        if layer % 2 == 0:
            m = attention_mixer(h, attn_w_in[j], attn_rel_bias[j], attn_w_out[j])
        else:
            m = recurrent_mixer(h, rg_w_in[j], rg_conv_w[j], rg_conv_b[j], rg_w_a[j], rg_b_a[j],
                                rg_w_i[j], rg_b_i[j], rg_lambda[j], rg_w_out[j])
        x = x + rmsnorm(m, norm_mix_post[layer])
        h = rmsnorm(x, norm_ffn_pre[layer])
        f = swiglu(h, ffn_w_gate[layer], ffn_w_up[layer], ffn_w_down[layer])
        x = x + rmsnorm(f, norm_ffn_post[layer])
    return x


def setup_inputs(seed=0):
    out = dict(first_inputs(seed))
    for name, value in second_inputs(seed + 1).items():
        if name != "x":
            out[name + "_2"] = value
    return out


def reference(
    x, c, ctx, c_ctx, mod_w, mod_b, norm_pre_g, norm_post_g, w_in, w_out, rwkv_w0, rwkv_w_up,
    rwkv_a0, rwkv_a_up, rwkv_k_k, rwkv_k_a, rwkv_r_k, rwkv_ln_g, rwkv_ln_b, conv_w, diff_lambda,
    diff_subln_g, attn_w_in_2, attn_rel_bias_2, attn_w_out_2, rg_w_in_2, rg_conv_w_2,
    rg_conv_b_2, rg_w_a_2, rg_b_a_2, rg_w_i_2, rg_b_i_2, rg_lambda_2, rg_w_out_2,
    norm_mix_pre_2, norm_mix_post_2, norm_ffn_pre_2, norm_ffn_post_2, ffn_w_gate_2, ffn_w_up_2,
    ffn_w_down_2,
):
    x = first_block(
        x, c, ctx, c_ctx, mod_w, mod_b, norm_pre_g, norm_post_g, w_in, w_out, rwkv_w0,
        rwkv_w_up, rwkv_a0, rwkv_a_up, rwkv_k_k, rwkv_k_a, rwkv_r_k, rwkv_ln_g, rwkv_ln_b,
        conv_w, diff_lambda, diff_subln_g,
    )
    return second_block(
        x, attn_w_in_2, attn_rel_bias_2, attn_w_out_2, rg_w_in_2, rg_conv_w_2, rg_conv_b_2,
        rg_w_a_2, rg_b_a_2, rg_w_i_2, rg_b_i_2, rg_lambda_2, rg_w_out_2, norm_mix_pre_2,
        norm_mix_post_2, norm_ffn_pre_2, norm_ffn_post_2, ffn_w_gate_2, ffn_w_up_2,
        ffn_w_down_2,
    )


_drawn_inputs = setup_inputs


def setup_inputs(seed=0):
    import zlib

    import numpy as np

    out = dict(_drawn_inputs(seed))
    spreads = {}
    factors = {'rwkv_w_up': 5.761,
     'rwkv_ln_g': 3.906,
     'rwkv_ln_b': 30.235,
     'diff_subln_g': 2.734,
     'rg_b_a_2': 58.555,
     'rg_b_i_2': 27.394}
    for name, (base, spread) in spreads.items():
        noise = np.random.default_rng([zlib.crc32(name.encode()), seed]).standard_normal(out[name].shape)
        drawn = base * np.exp(spread * noise) if base else spread * noise
        out[name] = __import__('jax').numpy.asarray(drawn.astype(out[name].dtype))
    for name, factor in factors.items():
        out[name] = (out[name] * factor).astype(out[name].dtype)
    return out
```

```python
import math
from contextlib import ExitStack

import numpy as np

import concourse.bass as bass
from concourse import mybir

ALU = mybir.AluOpType
ACT = mybir.ActivationFunctionType
AXX = mybir.AxisListType.X
F32 = mybir.dt.float32
F32R = mybir.dt.float32r

P = 128
D = 1024
NB = D // P
SEQ, CTX = 512, 256
TOK = SEQ + CTX
NT = TOK // P
DEPTH = 2
CH = 64
DFF = 2816
FB = DFF // P
GRID_W = 64
EPS = 1e-6
GN_EPS = 64e-5
C_R, C_K, C_V, C_LORA, C_Z = 0, 256, 512, 768, 1024
C_CONV = 1280
C_AQ, C_AK, C_AV, C_AZ = 2304, 2816, 3328, 3840

LAYER_VECS = [("mod_b", 24), ("pre_g", 8), ("post_g", 8), ("w0", 4), ("a0", 4), ("k_k", 2), ("k_a", 2),
              ("r_k", 2), ("ln_g", 2), ("ln_b", 2), ("conv_w", 6), ("subln", 1)]
BLOCK2_VECS = [("rg_conv_w", 32), ("rg_conv_b", 8), ("b_a", 8), ("b_i", 8), ("lam", 8),
               ("mix_pre", 16), ("mix_post", 16), ("ffn_pre", 16), ("ffn_post", 16)]


def row_table(vecs, start=0):
    at, out = start, {}
    for name, n in vecs:
        out[name] = at
        at += n
    return out, at


LROW, LROWS = row_table(LAYER_VECS)
B2ROW, B2ROWS = row_table(BLOCK2_VECS)
CROW = LROWS


def constant_columns():
    cols, parts = {}, []

    def put(name, a):
        cols[name] = (sum(p.shape[1] for p in parts), a.shape[1])
        parts.append(a.astype(np.float32))

    p = np.arange(P)
    put("ident", np.eye(P))
    put("headones", (p[:, None] // CH == p[None, :] // CH))
    put("ones", np.ones((P, P)))
    t = p % CH
    s = np.arange(CH)
    put("ident2", t[:, None] == s[None, :])
    for d in range(2):
        before = t[:, None] < s[None, :] if d == 0 else t[:, None] > s[None, :]
        put(f"seen{d}", np.concatenate([before, before | (t[:, None] == s[None, :])], 1))
    lev = []
    for j in range(6):
        for d in range(2):
            r, c = t[:, None] >> j, s[None, :] >> j
            same = (r >> 1) == (c >> 1)
            lev.append(same & ((r & 1) == 1) & ((c & 1) == 0) if d == 0 else same & ((r & 1) == 0) & ((c & 1) == 1))
    put("level", np.concatenate(lev, 1))
    put("reset", np.tile((np.arange(TOK) % CH != 0), (P, 1)))
    inv = 10000.0 ** (-np.arange(0, 32, 2, dtype=np.float32) / np.float32(32))
    tok = np.arange(SEQ)
    ch = p % 64
    pos = np.where(ch[:, None] < 32, tok[None, :] // GRID_W, tok[None, :] % GRID_W).astype(np.float32)
    ang = pos * inv[ch % 16].astype(np.float32)[:, None]
    put("cos", np.cos(ang))
    put("sin", np.where((ch % 32)[:, None] < 16, -1.0, 1.0) * np.sin(ang))
    put("strict", p[None, :] < p[:, None])
    return cols, np.concatenate(parts, 1)


CONST_AT, _CONST = constant_columns()
NCONST = _CONST.shape[1]


def build_program(nc, t, out):
    with ExitStack() as ctx:
        base = (nc.sbuf_base + 63) // 64 * 64
        here = [base]

        def place(name, shape, dt=F32, at=None):
            size = int(np.prod(shape[1:])) * 4
            off = here[0] if at is None else at
            if at is None:
                here[0] += (size + 63) // 64 * 64
            return nc.alloc_sbuf_tensor_at(name, [int(x) for x in shape], dt, offset=off)

        xT = place("xT", [P, NB, TOK])
        at_h = here[0]
        hhi = place("hhi", [P, NB, TOK], F32R)
        hlo = place("hlo", [P, NB, TOK], F32R)
        wraw = place("wraw", [P, 2, 8, P])
        whi = place("whi", [P, 2, 8, P], F32R)
        wlo = place("wlo", [P, 2, 8, P], F32R)
        const = place("const", [P, NCONST])
        VC = place("VC", [P, 3, P])
        modT = place("modT", [P, 2, 24, 2])
        chi = place("chi", [P, NB, 2], F32R)
        clo = place("clo", [P, NB, 2], F32R)
        cs = place("cs", [P, NB, 2])
        scl = place("scl", [P, 8, 16])
        sm = place("sm", [P, 64])
        epsc = place("epsc", [P, 2])
        ltmp = place("ltmp", [P, 8, 8])
        at_mix = here[0]
        mix = place("mix", [P, NB, TOK])
        at_a = here[0]
        arena_size = nc.sbuf_usable_end - at_a

        def arena(name, shape, dt=F32, off=0):
            size = int(np.prod(shape[1:])) * 4
            assert off + size <= arena_size, (name, off + size, arena_size)
            return place(name, shape, dt, at=at_a + off)

        def arena2(name, shape, dt=F32, off=0):
            size = int(np.prod(shape[1:])) * 4
            assert off + size <= 2 * NB * TOK * 4, (name, off + size)
            return place(name, shape, dt, at=at_h + off)

        K1 = 1024

        def cc(name):
            a, n = CONST_AT[name]
            return const[:, a:a + n]

        ident, headones, ones, ident2 = cc("ident"), cc("headones"), cc("ones"), cc("ident2")
        PW = [ctx.enter_context(nc.psum_tensor(f"PW{i}", [P, 1024], F32)) for i in range(4)]

        def bank(i):
            return PW[i // 2][:, (i % 2) * 512:(i % 2) * 512 + 512]

        sems = {}

        def S(name):
            if name not in sems:
                sems[name] = ctx.enter_context(nc.semaphore(name))
            return sems[name]

        totals = {}

        class Signal:
            def __init__(self, name, total):
                self.sem, self.base = S(name), totals.get(name, 0)
                totals[name] = self.base + total

            def at(self, n):
                return self.base + n

        SEGS = {TOK: [(0, 512), (512, TOK)], SEQ: [(0, 512)], 2: [(0, 2)]}
        stages = []

        def add_stage(name, body, iters, ntok, rhs, outs):
            st = dict(name=name, body=body, iters=iters, ntok=ntok, rhs=rhs, outs=outs, U=len(body), no=len(outs))
            if stages:
                l = stages[-1]
                st["g0"], st["o0"] = l["g0"] + l["U"] * l["iters"], l["o0"] + l["no"] * l["iters"]
                l["next"] = body[0]
            else:
                st["g0"], st["o0"] = 0, 0
            st["next"] = None
            assert st["U"] % 2 == 0 and st["no"] % 2 == 0
            stages.append(st)
            return st

        def kview(w):
            return w.rearrange("(k p) n -> p k n", p=P)

        def plain(name, w, col, nblk, ntok, rhs, evac):
            v = kview(w)
            body = [(v, 0, 8, col + P * j, 2 * P, j, True, True) for j in range(2)]
            return add_stage(name, body, nblk // 2, ntok, rhs, [("act", evac)] * 2)

        def turns(st):
            n, lo = st["iters"], 1 if st["g0"] == 0 else 0
            return lo, n - 1

        def run_turns(eng, st, do):
            lo, hi = turns(st)
            if lo == 1 and st["iters"] > 1:
                do(0, False)
            if hi - lo >= 2:
                with eng.Fori(lo, hi) as i:
                    do(i, False)
            else:
                for i in range(lo, hi):
                    do(i, False)
            do(st["iters"] - 1, True)

        def wait_pos(eng, sem, value):
            if not isinstance(value, int) or value > 0:
                eng.wait_ge(sem, value)

        def sp_stage(sp, st):
            def do(i, last):
                for u, (v, k0, kb, c0, cstep, o, first, fin) in enumerate(st["body"]):
                    g = i * st["U"] + (st["g0"] + u)
                    wait_pos(sp, S("w_split"), g - 1)
                    sp.dma_start(wraw[:, u % 2, 0:kb, :], v[:, k0:k0 + kb, bass.ds(i * cstep + c0, P)]) \
                        .then_inc(S(f"w_landed{u % 2}"), 16)
            run_turns(sp, st, do)

        def hi_part(act, i, st, u, desc):
            g = i * st["U"] + (st["g0"] + u)
            slot = u % 2
            act.wait_ge(S(f"w_landed{slot}"), (i * (st["U"] // 2) + (st["g0"] // 2 + u // 2)) * 16 + 16)
            wait_pos(act, S("w_used"), g - 1)
            kb = desc[2]
            act.activation(whi[:, slot, 0:kb, :], wraw[:, slot, 0:kb, :], ACT.Copy).then_inc(S("w_hi"), 1)

        def lo_part(dve, i, st, u, desc):
            g = i * st["U"] + (st["g0"] + u)
            slot = u % 2
            dve.wait_ge(S("w_hi"), g + 1)
            kb = desc[2]
            dve.tensor_tensor(wlo[:, slot, 0:kb, :], wraw[:, slot, 0:kb, :], whi[:, slot, 0:kb, :].bitcast(F32),
                              ALU.subtract).then_inc(S("w_split"), 1)

        def split_and_evac(eng, which, part, st):
            def do(i, last):
                for u, desc in enumerate(st["body"]):
                    nxt = st["body"][(u + 1) % st["U"]]
                    if u == st["U"] - 1 and last:
                        nxt = st["next"]
                    if nxt is not None:
                        part(eng, i, st, u + 1, nxt)
                    o = desc[5]
                    if desc[7] and st["outs"][o][0] == which:
                        eng.wait_ge(S("w_used"), i * st["U"] + (st["g0"] + u + 1))
                        st["outs"][o][1](eng, i, o, PW[o % 2][:, 0:st["ntok"]]) \
                            .then_inc(S(f"evac_done{o % 2}"), 1)
            run_turns(eng, st, do)

        def pe_stage(pe, st):
            def do(i, last):
                for u, (v, k0, kb, c0, cstep, o, first, fin) in enumerate(st["body"]):
                    g = i * st["U"] + (st["g0"] + u)
                    pe.wait_ge(S("w_split"), g + 1)
                    if first:
                        wait_pos(pe, S(f"evac_done{o % 2}"), i * (st["no"] // 2) + (st["o0"] // 2 + o // 2))
                    rhi, rlo = st["rhs"]
                    for s0, s1 in SEGS[st["ntok"]]:
                        acc = PW[o % 2][:, s0:s1]
                        for k in range(kb):
                            a, b = first and k == 0, fin and k == kb - 1
                            pe.matmul(acc, whi[:, u % 2, k, :], rhi[:, k0 + k, s0:s1], start=a, stop=False)
                            pe.matmul(acc, wlo[:, u % 2, k, :], rhi[:, k0 + k, s0:s1], start=False, stop=False)
                            last_mm = pe.matmul(acc, whi[:, u % 2, k, :], rlo[:, k0 + k, s0:s1], start=False, stop=b)
                    last_mm.then_inc(S("w_used"), 1)
            run_turns(pe, st, do)

        phases = []

        def phase(**engines):
            phases.append(engines)

        def to(dest, func=ACT.Copy, ntok=None):
            def ev(eng, i, o, acc):
                n = acc.shape[1]
                d = dest[:, bass.ds(i * 2 + o, 1), 0:n].rearrange("p a n -> p (a n)")
                return eng.activation(d, acc, func)
            return ev

        xtok = arena("xtok", [P, NT, D])
        VR = arena("VR", [P, 3, P], off=24 * K1)
        lamb = arena("lamb", [P, 2, 256], off=26 * K1)
        lamp = arena("lamp", [P, 2, 2, 64], off=28 * K1)
        n_in = [0]

        def sp_inputs(sp):
            def load(dst, src):
                sp.dma_start(dst, src).then_inc(S("inputs"), 16)
                n_in[0] += 16
            load(const[:, :], t["const"])
            load(xtok[:, 0:4, :], t["x"][0].rearrange("(a p) n -> p a n", p=P))
            load(xtok[:, 4:6, :], t["ctx"][0].rearrange("(a p) n -> p a n", p=P))

            def rows(i, at, ap, n):
                load(VR[at:at + n, i, :], ap)
            for l in range(DEPTH):
                r = LROW
                one = lambda name, a: rows(l, r[name], a.rearrange("(k p) -> k p", p=P), a.shape[0] // P)
                one("mod_b", t["mod_b"][l])
                one("pre_g", t["norm_pre_g"][l])
                one("post_g", t["norm_post_g"][l])
                one("w0", t["rwkv_w0"][l].rearrange("d n -> (d n)"))
                one("a0", t["rwkv_a0"][l].rearrange("d n -> (d n)"))
                one("k_k", t["rwkv_k_k"][l])
                one("k_a", t["rwkv_k_a"][l])
                one("r_k", t["rwkv_r_k"][l].rearrange("d n -> (d n)"))
                one("ln_g", t["rwkv_ln_g"][l])
                one("ln_b", t["rwkv_ln_b"][l])
                one("conv_w", t["conv_w"][l].rearrange("d n -> (d n)"))
                one("subln", t["diff_subln_g"][l])
            rows(0, CROW, t["c"][0].rearrange("(k p) -> k p", p=P), 8)
            rows(0, CROW + 8, t["c_ctx"].rearrange("(k p) -> k p", p=P), 8)
            b = B2ROW
            rows(2, b["rg_conv_w"], t["rg_conv_w_2"][0, :, 0].rearrange("j (k p) -> (j k) p", p=P), 32)
            rows(2, b["rg_conv_b"], t["rg_conv_b_2"][0].rearrange("(k p) -> k p", p=P), 8)
            rows(2, b["b_a"], t["rg_b_a_2"][0].rearrange("j (k p) -> (j k) p", p=P), 8)
            rows(2, b["b_i"], t["rg_b_i_2"][0].rearrange("j (k p) -> (j k) p", p=P), 8)
            rows(2, b["lam"], t["rg_lambda_2"][0].rearrange("(k p) -> k p", p=P), 8)
            for n, key in (("mix_pre", "norm_mix_pre_2"), ("mix_post", "norm_mix_post_2"),
                           ("ffn_pre", "norm_ffn_pre_2"), ("ffn_post", "norm_ffn_post_2")):
                rows(2, b[n], t[key].rearrange("l (k p) -> (l k) p", p=P), 16)
            for l in range(DEPTH):
                load(lamb[:, l, :], t["diff_lambda"][l].rearrange("a b -> (a b)").unsqueeze(0).to_broadcast([P, 256]))

        N_INPUTS = 3 + 12 * DEPTH + 2 + 9 + DEPTH

        def pe_inputs(pe):
            pe.wait_ge(S("inputs"), 16 * N_INPUTS)
            for i, n in ((0, CROW + 16), (1, LROWS), (2, B2ROWS)):
                ins = pe.transpose(bank(6)[:, i * P:i * P + n], VR[0:n, i, :], ident[0:n, 0:n])
            ins.then_inc(S("vec_cols"), 1)
            for T in range(NT):
                if T >= 2:
                    pe.wait_ge(S("xT_ready"), T - 1)
                for b in range(NB):
                    ins = pe.transpose(PW[T % 2][:, b * P:(b + 1) * P], xtok[:, T, b * P:(b + 1) * P], ident)
                ins.then_inc(S("xT_turned"), 1)

        def dve_inputs(dve):
            dve.memset(epsc[:, 0:1], EPS)
            dve.memset(epsc[:, 1:2], GN_EPS)
            dve.wait_ge(S("inputs"), 16 * N_INPUTS)
            dve.wait_ge(S("vec_cols"), 1)
            for i, n in ((0, CROW + 16), (1, LROWS), (2, B2ROWS)):
                ins = dve.tensor_copy(VC[:, i, 0:n], bank(6)[:, i * P:i * P + n])
            ins.then_inc(S("VC_ready"), 1)
            for T in range(NT):
                dve.wait_ge(S("xT_turned"), T + 1)
                dve.tensor_copy(xT[:, :, T * P:(T + 1) * P], PW[T % 2][:, :].rearrange("p (b n) -> p b n", b=NB)) \
                   .then_inc(S("xT_ready"), 1)
            dve.wait_ge(S("silu_c"), 1)
            dve.tensor_copy(chi[:], cs[:])
            dve.drain()
            dve.tensor_tensor(clo[:], cs[:], chi[:].bitcast(F32), ALU.subtract)
            lv = lamb[:].rearrange("p l (a c b) -> p l a c b", a=2, c=2)
            dve.tensor_tensor(lamp[:], lv[:, :, :, 0, :], lv[:, :, :, 1, :], ALU.mult)
            dve.drain()
            dve.tensor_reduce(sm[:, 0:4], lamp[:].rearrange("p l a b -> p (l a) b"), AXX, ALU.add) \
               .then_inc(S("lam_sums"), 1)
            dve.wait_ge(S("lam_exps"), 1)
            for l in range(DEPTH):
                init = 0.8 - 0.6 * math.exp(-0.3 * l)
                dve.tensor_tensor(sm[:, 8 + l:9 + l], sm[:, 4 + 2 * l + 1:4 + 2 * l + 2],
                                  sm[:, 4 + 2 * l:4 + 2 * l + 1], ALU.subtract)
                dve.drain()
                dve.tensor_scalar(sm[:, 8 + l:9 + l], sm[:, 8 + l:9 + l], init, None, ALU.subtract)
                dve.tensor_scalar(scl[:, 7, l:l + 1], VC[:, l, LROW["subln"]:LROW["subln"] + 1], 1.0 - init, None,
                                  ALU.mult)
            lcol = VC[:, 2, B2ROW["lam"]:B2ROW["lam"] + 8]
            E, A, Q, R, Z = (ltmp[:, i, :] for i in range(5))
            dve.wait_ge(S("lam_exps"), 2)
            dve.tensor_scalar(A, E, 2.0, None, ALU.add)
            dve.drain()
            dve.reciprocal(Q, A)
            dve.drain()
            dve.tensor_tensor(A, E, Q, ALU.mult)
            dve.drain()
            dve.tensor_tensor(Q, A, A, ALU.mult)
            dve.memset(R, 2.0 / 19)
            dve.drain()
            for n in range(17, 0, -2):
                dve.tensor_tensor(R, R, Q, ALU.mult)
                dve.drain()
                dve.tensor_scalar(R, R, 2.0 / n, None, ALU.add)
                dve.drain()
            dve.tensor_tensor(R, R, A, ALU.mult)
            dve.tensor_scalar(Z, lcol, -1.0, 0.0, ALU.mult, ALU.max)
            dve.drain()
            dve.tensor_tensor(R, R, Z, ALU.add)
            dve.drain()
            dve.tensor_scalar(scl[:, 6, 0:8], R, 8.0, None, ALU.mult)
            dve.tensor_scalar(scl[:, 6, 8:16], R, -8.0, None, ALU.mult)

        def act_inputs(act):
            act.wait_ge(S("VC_ready"), 1)
            act.activation(cs[:, :, 0], VC[:, 0, CROW:CROW + 8], ACT.Silu)
            act.activation(cs[:, :, 1], VC[:, 0, CROW + 8:CROW + 16], ACT.Silu).then_inc(S("silu_c"), 1)
            act.wait_ge(S("lam_sums"), 1)
            act.activation(sm[:, 4:8], sm[:, 0:4], ACT.Exp).then_inc(S("lam_exps"), 1)
            act.activation(ltmp[:, 1, :], VC[:, 2, B2ROW["lam"]:B2ROW["lam"] + 8], ACT.Abs)
            act.drain()
            act.activation(ltmp[:, 0, :], ltmp[:, 1, :], ACT.Exp, scale=-1.0).then_inc(S("lam_exps"), 1)

        phase(sp=sp_inputs, pe=pe_inputs, dve=dve_inputs, act=act_inputs)

        def stream_phase(*sts, pe=None, dve=None, act=None):
            def pe_(e):
                for st in sts:
                    pe_stage(e, st)
                if pe:
                    pe(e)

            def act_(e):
                for st in sts:
                    split_and_evac(e, "act", hi_part, st)
                if act:
                    act(e)

            def dve_(e):
                for st in sts:
                    split_and_evac(e, "dve", lo_part, st)
                if dve:
                    dve(e)
            phase(sp=lambda sp: [sp_stage(sp, st) for st in sts], pe=pe_, act=act_, dve=dve_)

        def to_mod(l):
            def ev(eng, i, o, acc):
                return eng.activation(modT[:, l, bass.ds(i * 2 + o, 1), :].rearrange("p a n -> p (a n)"), acc, ACT.Copy)
            return ev

        for l in range(DEPTH):
            stream_phase(plain(f"mod{l}", t["mod_w"][l], 0, 24, 2, (chi, clo), to_mod(l)))

        def dve_scales(dve):
            for l in range(DEPTH):
                for s in range(2):
                    dve.tensor_tensor(modT[:, l, :, s], modT[:, l, :, s], VC[:, l, 0:24], ALU.add)
            dve.drain()
            for l in range(DEPTH):
                for s in range(2):
                    g, pg = (VC[:, l, LROW[n]:LROW[n] + 8] for n in ("pre_g", "post_g"))
                    v = scl[:, 3 * l:3 * l + 3, :].rearrange("p a (b s) -> p a b s", s=2)
                    dve.scalar_tensor_tensor(out=v[:, 0, :, s], in0=modT[:, l, 8:16, s], scalar=1.0, in1=g,
                                             op0=ALU.add, op1=ALU.mult)
                    dve.tensor_copy(v[:, 1, :, s], modT[:, l, 0:8, s])
                    dve.tensor_tensor(v[:, 2, :, s], modT[:, l, 16:24, s], pg, ALU.mult)

        phase(dve=dve_scales)

        def norm_phase(name, src, ntok, finish_dve, finish_act=None, scratch=24 * K1):
            segs = SEGS[ntok]
            sq = arena(f"sq_{name}", [P, 4, TOK], off=scratch)
            root = arena(f"root_{name}", [P, TOK], off=scratch + 12 * K1)
            rstd = arena(f"rstd_{name}", [P, TOK], off=scratch + 15 * K1)
            tmp = arena(f"tmp_{name}", [P, 2, TOK], off=scratch + 18 * K1)
            sqr, sqm = Signal("squares", NB + 1), Signal("squares_summed", NB)

            def act(a):
                for b in range(NB):
                    if b >= 4:
                        a.wait_ge(sqm.sem, sqm.at(b - 3))
                    a.activation(sq[:, b % 4, 0:ntok], src[:, b, 0:ntok], ACT.Square).then_inc(sqr.sem, 1)
                a.wait_ge(sqm.sem, sqm.at(NB))
                a.activation(root[:, 0:ntok], PW[0][:, 0:ntok], ACT.Sqrt, scale=1.0 / D, bias=epsc[:, 0:1]) \
                 .then_inc(sqr.sem, 1)
                if finish_act:
                    finish_act(a, tmp)

            def pe(e):
                for b in range(NB):
                    e.wait_ge(sqr.sem, sqr.at(b + 1))
                    for s0, s1 in segs:
                        ins = e.matmul(PW[0][:, s0:s1], ones, sq[:, b % 4, s0:s1], start=b == 0, stop=b == NB - 1)
                    ins.then_inc(sqm.sem, 1)

            def dve(v):
                v.wait_ge(sqr.sem, sqr.at(NB + 1))
                v.reciprocal(rstd[:, 0:ntok], root[:, 0:ntok])
                v.drain()
                finish_dve(v, rstd, tmp)
            phase(pe=pe, act=act, dve=dve)

        def pre_norm(name, ntok, gcol, shift):
            segs = SEGS[ntok]
            tr, hr = Signal("scaled", len(segs) * NB), Signal("h_rounded", len(segs) * NB)

            def dve(v, rstd, tmp):
                def low(b):
                    v.wait_ge(hr.sem, hr.at(len(segs) * (b + 1)))
                    for s, (s0, s1) in enumerate(segs):
                        v.scalar_tensor_tensor(out=hlo[:, b, s0:s1], in0=tmp[:, b % 2, s0:s1], scalar=shift(b, s),
                                               in1=hhi[:, b, s0:s1].bitcast(F32), op0=ALU.add, op1=ALU.subtract)
                for b in range(NB):
                    v.drain()
                    for s, (s0, s1) in enumerate(segs):
                        v.scalar_tensor_tensor(out=tmp[:, b % 2, s0:s1], in0=xT[:, b, s0:s1], scalar=gcol(b, s),
                                               in1=rstd[:, s0:s1], op0=ALU.mult, op1=ALU.mult).then_inc(tr.sem, 1)
                    if b:
                        low(b - 1)
                low(NB - 1)

            def act(a, tmp):
                for b in range(NB):
                    a.wait_ge(tr.sem, tr.at(len(segs) * (b + 1)))
                    for s, (s0, s1) in enumerate(segs):
                        a.activation(hhi[:, b, s0:s1], tmp[:, b % 2, s0:s1], ACT.Identity, bias=shift(b, s)) \
                         .then_inc(hr.sem, 1)
            norm_phase(name, xT, ntok, dve, act)

        def post_norm(name, m, ntok, gcol, **kw):
            segs = SEGS[ntok]

            def dve(v, rstd, tmp):
                for b in range(NB):
                    for s, (s0, s1) in enumerate(segs):
                        v.scalar_tensor_tensor(out=tmp[:, b % 2, s0:s1], in0=m[:, b, s0:s1], scalar=gcol(b, s),
                                               in1=rstd[:, s0:s1], op0=ALU.mult, op1=ALU.mult)
                    v.drain()
                    v.tensor_tensor(xT[:, b, 0:ntok], xT[:, b, 0:ntok], tmp[:, b % 2, 0:ntok], ALU.add)
            norm_phase(name, m, ntok, dve, **kw)

        def split_mix(name, ntok):
            hr = Signal("mix_rounded", NB)

            def act(a):
                for b in range(NB):
                    a.activation(hhi[:, b, 0:ntok], mix[:, b, 0:ntok], ACT.Copy).then_inc(hr.sem, 1)

            def dve(v):
                for b in range(NB):
                    v.wait_ge(hr.sem, hr.at(b + 1))
                    v.tensor_tensor(hlo[:, b, 0:ntok], mix[:, b, 0:ntok], hhi[:, b, 0:ntok].bitcast(F32), ALU.subtract)
            phase(act=act, dve=dve)

        HALF = {TOK: 2, SEQ: 1}

        def conv_mixer(l, full):
            n = TOK if full else SEQ
            cb = arena(f"cb{l}", [P, 8, TOK])
            u = arena(f"cu{l}", [P, TOK], off=24 * K1)
            y = arena(f"cy{l}", [P, TOK], off=27 * K1)
            w = lambda j, hp: VC[:, l, LROW["conv_w"] + 2 * j + hp:LROW["conv_w"] + 2 * j + hp + 1]

            def dve(v):
                v.wait_ge(S("evac_done1"), conv_last[l])
                v.wait_ge(S("evac_done0"), conv_last[l])
                for hp in range(2):
                    v.tensor_tensor(u[:, 0:n], cb[:, 2 + hp, 0:n], cb[:, 4 + hp, 0:n], ALU.mult)
                    v.drain()
                    v.tensor_scalar(y[:, 0:n], u[:, 0:n], w(1, hp), None, ALU.mult)
                    v.drain()
                    for s0, s1 in SEGS[n]:
                        v.scalar_tensor_tensor(out=y[:, s0 + 1:s1], in0=u[:, s0:s1 - 1], scalar=w(0, hp),
                                               in1=y[:, s0 + 1:s1], op0=ALU.mult, op1=ALU.add)
                    v.drain()
                    for s0, s1 in SEGS[n]:
                        v.scalar_tensor_tensor(out=y[:, s0:s1 - 1], in0=u[:, s0 + 1:s1], scalar=w(2, hp),
                                               in1=y[:, s0:s1 - 1], op0=ALU.mult, op1=ALU.add)
                    v.drain()
                    v.tensor_tensor(y[:, 0:n], y[:, 0:n], cb[:, hp, 0:n], ALU.mult)
                    v.drain()
                    v.tensor_tensor(mix[:, 2 + hp, 0:n], y[:, 0:n], cb[:, 6 + hp, 0:n], ALU.mult)
                    v.drain()
            w_in = t["w_in"][l]
            a = plain(f"conv{l}", w_in, C_CONV, 6, n, (hhi, hlo), to(cb))
            b = plain(f"convz{l}", w_in, C_CONV + 768, 2, n, (hhi, hlo), to(cb[:, 6:8, :], ACT.Silu))
            conv_last[l] = (b["o0"] + 2) // 2
            stream_phase(a, b, dve=dve)

        conv_last = {}

        def attention(l, full):
            n = TOK if full else SEQ
            w_in = t["w_in"][l]
            q = arena(f"aq{l}", [P, 4, TOK])
            k = arena(f"ak{l}", [P, 4, TOK], off=12 * K1)
            z = arena(f"az{l}", [P, 4, TOK], off=24 * K1)
            vtok = arena(f"avt{l}", [P, NT, 512], off=36 * K1)
            vch = arena(f"avc{l}", [P, 4, TOK], off=48 * K1)
            AT = arena(f"aAT{l}", [P, NT, 512], off=48 * K1)
            prob = arena(f"apr{l}", [P, 2, TOK], off=60 * K1)
            rot = arena(f"arot{l}", [P, 2, SEQ], off=60 * K1)
            st = sm[:, 16:32]

            vtu, vts = Signal("v_turned", NT), Signal("v_tokens", NT)

            def pe_v(e):
                e.wait_ge(S("evac_done0"), (vs["o0"] + 4) // 2)
                e.wait_ge(S("evac_done1"), (vs["o0"] + 4) // 2)
                for T in range(NT):
                    if T >= 2:
                        e.wait_ge(vts.sem, vts.at(T - 1))
                    for h in range(4):
                        ins = e.transpose(bank(4 + T % 2)[:, h * P:(h + 1) * P], vch[:, h, T * P:(T + 1) * P], ident)
                    ins.then_inc(vtu.sem, 1)

            def act_v(a):
                for T in range(NT):
                    a.wait_ge(vtu.sem, vtu.at(T + 1))
                    a.activation(vtok[:, T, :], bank(4 + T % 2), ACT.Copy).then_inc(vts.sem, 1)
            vs = plain(f"av{l}", w_in, C_AV, 4, TOK, (hhi, hlo), to(vch))
            stream_phase(vs, pe=pe_v, act=act_v)

            def dve_rope(v):
                for i, sts in ((0, qs), (1, ks)):
                    v.wait_ge(S("evac_done0"), (sts["o0"] + 4) // 2)
                    v.wait_ge(S("evac_done1"), (sts["o0"] + 4) // 2)
                    x = (q, k)[i]
                    for h in range(4):
                        v.stream_shuffle(rot[:, 0, :], x[:, h, 0:SEQ], [j ^ 16 for j in range(32)])
                        v.tensor_tensor(rot[:, 1, :], x[:, h, 0:SEQ], cc("cos"), ALU.mult)
                        v.drain()
                        v.tensor_tensor(rot[:, 0, :], rot[:, 0, :], cc("sin"), ALU.mult)
                        v.drain()
                        v.tensor_tensor(x[:, h, 0:SEQ], rot[:, 0, :], rot[:, 1, :], ALU.add)
                        v.drain()
            qs = plain(f"aq{l}", w_in, C_AQ, 4, n, (hhi, hlo), to(q))
            ks = plain(f"ak{l}", w_in, C_AK, 4, TOK, (hhi, hlo), to(k))
            zs = plain(f"az{l}", w_in, C_AZ, 4, n, (hhi, hlo), to(z, ACT.Silu))
            stream_phase(qs, ks, zs, dve=dve_rope)

            steps = []
            for h in range(4):
                steps += [(h, qt, 0, 0, NT) for qt in range(4)]
                if full:
                    steps += [(h, qt, SEQ, 4, 2) for qt in (4, 5)]
            finals = []
            for i, (h, qt, c0, kt0, nk) in enumerate(steps):
                if qt in (3, 5):
                    finals.append((i, h, qt == 5))
            fin_at = {i: (f, h, c) for f, (i, h, c) in enumerate(finals)}
            ns, nf = len(steps), len(finals)
            sc_, mx, ex, cb_, tr, at, pv, osq, osum, ort, omix = (
                Signal(f"attn_{nm}", c) for nm, c in (
                    ("scores", 2 * ns), ("max", ns), ("exps", 2 * ns), ("combined", ns), ("turned", ns), ("AT", ns),
                    ("out", nf), ("out_read", 2 * nf), ("sums", nf), ("root", nf), ("mixed", nf)))
            scale = 64 ** -0.5
            osb = place(f"aosb{l}", [P, 3, 512], at=at_mix)

            def pe_scores(e, i):
                h, qt, c0, kt0, nk = steps[i]
                for j in range(2):
                    if i:
                        e.wait_ge(ex.sem, ex.at(2 * (i - 1) + j + 1))
                    width = nk * P
                    for s0 in range(0, width, 512):
                        s1 = min(width, s0 + 512)
                        ins = e.matmul(PW[j][:, s0:s1], q[64 * j:64 * j + 64, h, qt * P:(qt + 1) * P],
                                       k[64 * j:64 * j + 64, h, c0 + s0:c0 + s1], start=True, stop=True)
                    ins.then_inc(sc_.sem, 1)

            def pe_attn(e):
                pe_scores(e, 0)
                for i, (h, qt, c0, kt0, nk) in enumerate(steps):
                    if i + 1 < len(steps):
                        pe_scores(e, i + 1)
                    e.wait_ge(cb_.sem, cb_.at(i + 1))
                    if i:
                        e.wait_ge(at.sem, at.at(i))
                    for kt in range(nk):
                        ins = e.transpose(PW[2][:, kt * P:(kt + 1) * P], prob[:, 0, kt * P:(kt + 1) * P], ident)
                    ins.then_inc(tr.sem, 1)
                    if i in fin_at:
                        f, _, is_ctx = fin_at[i]
                        w = 256 if is_ctx else 512
                        e.wait_ge(at.sem, at.at(i + 1))
                        if f:
                            e.wait_ge(osq.sem, osq.at(2 * f))
                        for kt in range(nk):
                            ins = e.matmul(bank(6)[:, 0:w], vtok[:, kt0 + kt, h * P:(h + 1) * P],
                                           AT[:, kt, 0:w], start=kt == 0, stop=kt == nk - 1)
                        ins.then_inc(pv.sem, 1)
                        e.wait_ge(osq.sem, osq.at(2 * f + 2))
                        if f:
                            e.wait_ge(ort.sem, ort.at(f))
                        e.matmul(bank(7)[:, 0:w], ones, osb[:, 1, 0:w], start=True, stop=True).then_inc(osum.sem, 1)

            def act_attn(a):
                for i, (h, qt, c0, kt0, nk) in enumerate(steps):
                    a.wait_ge(mx.sem, mx.at(i + 1))
                    if i:
                        a.wait_ge(tr.sem, tr.at(i))
                    for j in range(2):
                        a.activation(prob[:, j, 0:nk * P], PW[j][:, 0:nk * P], ACT.Exp, scale=scale,
                                     bias=st[:, 2 + j:3 + j], accum_out=st[:, 4 + j:5 + j]).then_inc(ex.sem, 1)
                    a.wait_ge(tr.sem, tr.at(i + 1))
                    is_ctx = qt >= 4
                    if qt in (0, 4) and i:
                        a.wait_ge(pv.sem, pv.at(sum(1 for x in finals if x[0] < i)))
                    qq = (qt - 4 if is_ctx else qt) * P
                    a.activation(AT[:, 0:nk, qq:qq + P], PW[2][:, 0:nk * P].rearrange("p (a b) -> p a b", b=P),
                                 ACT.Copy).then_inc(at.sem, 1)
                    if i in fin_at:
                        f, _, is_ctx = fin_at[i]
                        w = 256 if is_ctx else 512
                        a.wait_ge(pv.sem, pv.at(f + 1))
                        if f:
                            a.wait_ge(omix.sem, omix.at(f))
                        a.activation(osb[:, 0, 0:w], bank(6)[:, 0:w], ACT.Copy).then_inc(osq.sem, 1)
                        a.activation(osb[:, 1, 0:w], bank(6)[:, 0:w], ACT.Square).then_inc(osq.sem, 1)
                        a.wait_ge(osum.sem, osum.at(f + 1))
                        a.activation(osb[:, 2, 0:w], bank(7)[:, 0:w], ACT.Sqrt, scale=1.0 / P, bias=epsc[:, 0:1]) \
                         .then_inc(ort.sem, 1)

            def dve_attn(v):
                def finish(f, h, is_ctx):
                    w, c = (256, SEQ) if is_ctx else (512, 0)
                    v.wait_ge(ort.sem, ort.at(f + 1))
                    v.reciprocal(osb[:, 2, 0:w], osb[:, 2, 0:w])
                    v.drain()
                    v.scalar_tensor_tensor(out=osb[:, 0, 0:w], in0=osb[:, 0, 0:w], scalar=scl[:, 7, l:l + 1],
                                           in1=osb[:, 2, 0:w], op0=ALU.mult, op1=ALU.mult)
                    v.drain()
                    v.tensor_tensor(mix[:, 4 + h, c:c + w], osb[:, 0, 0:w], z[:, h, c:c + w], ALU.mult) \
                     .then_inc(omix.sem, 1)
                for i, (h, qt, c0, kt0, nk) in enumerate(steps):
                    for j in range(2):
                        v.wait_ge(sc_.sem, sc_.at(2 * i + j + 1))
                        v.reduce_max(st[:, j:j + 1], PW[j][:, 0:nk * P], AXX)
                    v.drain()
                    v.tensor_scalar(st[:, 2:4], st[:, 0:2], -scale, None, ALU.mult).then_inc(mx.sem, 1)
                    v.wait_ge(ex.sem, ex.at(2 * i + 2))
                    v.reciprocal(st[:, 6:8], st[:, 4:6])
                    v.drain()
                    v.tensor_tensor(st[:, 8:9], st[:, 7:8], sm[:, 8 + l:9 + l], ALU.mult)
                    v.drain()
                    v.tensor_scalar(prob[:, 1, 0:nk * P], prob[:, 1, 0:nk * P], st[:, 8:9], None, ALU.mult)
                    v.drain()
                    v.scalar_tensor_tensor(out=prob[:, 0, 0:nk * P], in0=prob[:, 0, 0:nk * P], scalar=st[:, 6:7],
                                           in1=prob[:, 1, 0:nk * P], op0=ALU.mult, op1=ALU.add).then_inc(cb_.sem, 1)
                    if i in fin_at:
                        finish(*fin_at[i])
            phase(pe=pe_attn, act=act_attn, dve=dve_attn)

        def rwkv(l, full):
            n = TOK if full else SEQ
            w_in = t["w_in"][l]
            col = lambda name, i: VC[:, l, LROW[name] + i:LROW[name] + i + 1]
            r = arena(f"r{l}", [P, 2, TOK])
            k = arena(f"k{l}", [P, 2, TOK], off=6 * K1)
            v_ = arena(f"v{l}", [P, 2, TOK], off=12 * K1)
            z = arena(f"z{l}", [P, 2, TOK], off=18 * K1)
            lora = arena(f"lora{l}", [P, 2, TOK], off=24 * K1)
            kk = arena(f"kk{l}", [P, 2, TOK], off=30 * K1)
            icl = arena(f"icl{l}", [P, 2, 2, TOK], off=36 * K1)
            vtok = arena(f"rvt{l}", [P, NT, 256], off=48 * K1)
            wup = arena(f"wup{l}", [P, 2, 256], off=54 * K1)
            cm = arena2(f"cm{l}", [P, 2, 2, TOK])
            cum = arena2(f"cum{l}", [P, 2, 2, TOK], off=12 * K1)
            AR = arena2(f"AR{l}", [P, 2, 2, 2, P], off=24 * K1)
            BK = arena2(f"BK{l}", [P, 2, 2, 4, P], off=28 * K1)
            MB = arena2(f"MB{l}", [P, 8, 3, CH], off=36 * K1)
            MK = arena2(f"MK{l}", [P, 8, 2, CH], off=42 * K1)
            KhT = arena2(f"KhT{l}", [P, 8, CH], off=46 * K1)
            AW = arena(f"AW{l}", [P, 8, 2, CH], off=54 * K1)
            Tt = arena(f"Tt{l}", [P, 8, CH], off=58 * K1)
            X = arena(f"X{l}", [P, 8, CH], off=60 * K1)
            XT = arena(f"XT{l}", [P, 8, CH], off=62 * K1)
            G = arena(f"G{l}", [P, 8, CH], off=64 * K1)
            QT = arena(f"QT{l}", [P, 8, CH], off=66 * K1)
            ST = arena(f"ST{l}", [P, 4, CH], off=24 * K1)
            SH = arena(f"SH{l}", [P, 4, CH], off=25 * K1)
            t1 = arena2(f"t1{l}", [P, 2, TOK], off=24 * K1)
            t2 = arena2(f"t2{l}", [P, 2, TOK], off=30 * K1)

            r_st = plain(f"pr{l}", w_in, C_R, 2, n, (hhi, hlo), to(r))
            k_st = plain(f"pk{l}", w_in, C_K, 2, TOK, (hhi, hlo), to(k))
            v_st = plain(f"pv{l}", w_in, C_V, 2, TOK, (hhi, hlo), to(v_))

            def ev_lora(eng, i, o, acc):
                return eng.activation(lora[:, o, 0:TOK], acc, ACT.Tanh if o == 0 else ACT.Copy)
            l_st = plain(f"pl{l}", w_in, C_LORA, 2, TOK, (hhi, hlo), ev_lora)
            z_st = plain(f"pz{l}", w_in, C_Z, 2, n, (hhi, hlo), to(z, ACT.Silu))
            stream_phase(r_st, k_st, v_st, l_st, z_st)

            lnorm, s_wup, s_vtok, s_vturn = (Signal("kk_squares", 2), Signal("lora_weights", 32), Signal("rwkv_v_tokens", NT),
                                             Signal("rwkv_v_turned", NT))
            s_kksum, s_kkroot = Signal("kk_summed", 2), Signal("kk_root", 2)

            def pool_prep(pool):
                pool.wait_ge(S("phase_end"), 3 * phase_of[f"rprep{l}"])
                pool.dma_start(wup[:, 0, :], t["rwkv_w_up"][l].rearrange("d a n -> (d a) n")).then_inc(s_wup.sem, 16)
                pool.dma_start(wup[:, 1, :], t["rwkv_a_up"][l].rearrange("d a n -> (d a) n")).then_inc(s_wup.sem, 16)

            up, upe = Signal("lora_up", 8), Signal("lora_up_read", 8)

            def pe_prep(e):
                for T in range(NT):
                    if T >= 2:
                        e.wait_ge(s_vtok.sem, s_vtok.at(T - 1))
                    for hp in range(2):
                        ins = e.transpose(bank(6 + T % 2)[:, hp * P:(hp + 1) * P], v_[:, hp, T * P:(T + 1) * P], ident)
                    ins.then_inc(s_vturn.sem, 1)
                e.wait_ge(s_wup.sem, s_wup.at(32))
                i = 0
                for kind in range(2):
                    for d in range(2):
                        for hp in range(2):
                            if i >= 2:
                                e.wait_ge(upe.sem, upe.at(i - 1))
                            for s0, s1 in SEGS[TOK]:
                                ins = e.matmul(PW[i % 2][:, s0:s1], wup[64 * d:64 * d + 64, kind, hp * P:(hp + 1) * P],
                                               lora[64 * d:64 * d + 64, kind, s0:s1], start=True, stop=True)
                            ins.then_inc(up.sem, 1)
                            i += 1
                for hp in range(2):
                    e.wait_ge(lnorm.sem, lnorm.at(hp + 1))
                    if hp == 0:
                        e.wait_ge(upe.sem, upe.at(8))
                    for s0, s1 in SEGS[TOK]:
                        ins = e.matmul(PW[hp][:, s0:s1], headones, t1[:, hp, s0:s1], start=True, stop=True)
                    ins.then_inc(s_kksum.sem, 1)

            def act_prep(a):
                i = 0
                for kind in range(2):
                    for d in range(2):
                        for hp in range(2):
                            a.wait_ge(up.sem, up.at(i + 1))
                            dst = (cm, icl)[kind][:, d, hp, :]
                            a.activation(dst, PW[i % 2][:, 0:TOK], ACT.Sigmoid,
                                         bias=col(("w0", "a0")[kind], 2 * d + hp)).then_inc(upe.sem, 1)
                            i += 1
                for hp in range(2):
                    a.wait_ge(s_kksum.sem, s_kksum.at(hp + 1))
                    a.activation(t2[:, hp, :], PW[hp][:, 0:TOK], ACT.Sqrt).then_inc(s_kkroot.sem, 1)

            def dve_prep(v):
                v.memset(ST[:], 0.0) if False else None
                for hp in range(2):
                    v.tensor_scalar(kk[:, hp, :], k[:, hp, :], col("k_k", hp), None, ALU.mult)
                v.drain()
                for hp in range(2):
                    v.tensor_tensor(t1[:, hp, :], kk[:, hp, :], kk[:, hp, :], ALU.mult).then_inc(lnorm.sem, 1)
                v.memset(mix[:, 0:2, 0:n], 0.0)
                for T in range(NT):
                    v.wait_ge(s_vturn.sem, s_vturn.at(T + 1))
                    v.tensor_copy(vtok[:, T, :], bank(6 + T % 2)[:, 0:256]).then_inc(s_vtok.sem, 1)
                v.wait_ge(upe.sem, upe.at(4))
                v.tensor_scalar(cm[:], cm[:], -math.exp(-0.5), None, ALU.mult)
                v.drain()
                for hp in range(2):
                    v.tensor_tensor_scan(cum[:, 0, hp, :], cc("reset"), cm[:, 0, hp, :], 0.0, ALU.mult, ALU.add)
                    v.tensor_tensor_scan(cum[:, 1, hp, ::-1], cc("reset"), cm[:, 1, hp, ::-1], 0.0, ALU.mult, ALU.add)
                v.drain()
                v.tensor_tensor(cm[:], cum[:], cm[:], ALU.subtract)
                v.wait_ge(s_kkroot.sem, s_kkroot.at(2))
                v.tensor_scalar(t2[:], t2[:], 1e-12, None, ALU.max)
                v.drain()
                v.reciprocal(t2[:], t2[:])
                v.drain()
                v.tensor_tensor(kk[:], kk[:], t2[:], ALU.mult)
                v.tensor_scalar(scl_ka[:, 0:2], VC[:, l, LROW["k_a"]:LROW["k_a"] + 2], -1.0, 1.0, ALU.mult, ALU.add)
                v.tensor_scalar(scl_ka[:, 2:4], VC[:, l, LROW["k_a"]:LROW["k_a"] + 2], -2.0, 2.0, ALU.mult, ALU.add)
            scl_ka = sm[:, 40:44]
            phase_of[f"rprep{l}"] = len(phases)
            phase(pool=pool_prep, pe=pe_prep, act=act_prep, dve=dve_prep)

            order = [[4, 5, 0, 1, 2, 3], [5, 4, 3, 2, 1, 0]]
            NBATCH = NT

            def has_y(j):
                return full or j >= 2
            names = ("exps", "AR", "BK", "Lb", "Lk", "tA", "tB", "tK", "mb", "mk", "aw", "bh", "kh", "w1", "w1e",
                     "inv", "inve", "xa", "xae", "gq", "gqe", "chS", "hy", "che")
            q = {nm: S(f"rw_{nm}") for nm in names}
            base_j = l * NBATCH

            def tiles(j):
                return [slice(order[d][j] * P, order[d][j] * P + P) for d in range(2)]

            a0, a1 = CONST_AT["seen0"][0], CONST_AT["seen1"][0]
            assert a1 == a0 + 2 * CH
            seen_both = const[:, a0:a0 + 4 * CH]

            def act_batch(a, j):
                jj = base_j + j
                if jj:
                    a.wait_ge(q["che"], 6 * jj if False else 2 * jj)
                for d in range(2):
                    s = tiles(j)[d]
                    a.activation(AR[:, d, :, 0, :], cm[:, d, :, s], ACT.Exp)
                    a.activation(AR[:, d, :, 1, :], cum[:, d, :, s], ACT.Exp)
                    a.activation(BK[:, d, :, 0, :], cum[:, d, :, s], ACT.Exp, scale=-1.0).then_inc(q["exps"], 1)
                a.wait_ge(q["tA"], jj + 1)
                a.activation(AW[:, :, 0, :], bank(4).rearrange("p (a b) -> p a b", b=CH), ACT.Copy).then_inc(q["aw"], 1)
                a.wait_ge(q["tB"], jj + 1)
                a.activation(MB[:, :, 2, :], bank(5).rearrange("p (a b) -> p a b", b=CH), ACT.Copy).then_inc(q["bh"], 1)
                a.wait_ge(q["tK"], jj + 1)
                a.activation(KhT[:], bank(6).rearrange("p (a b) -> p a b", b=CH), ACT.Copy).then_inc(q["kh"], 1)
                a.wait_ge(q["w1"], jj + 1)
                a.activation(AW[:, :, 1, :], bank(7).rearrange("p (a b) -> p a b", b=CH), ACT.Copy).then_inc(q["w1e"], 1)
                for d in range(2):
                    a.wait_ge(q["xa"], 2 * jj + d + 1)
                    src = bank(6 + d).rearrange("p (a c b) -> p a c b", c=2, b=CH)
                    a.activation(AW[:, 4 * d:4 * d + 4, 1, :], src[:, :, 0, :], ACT.Copy)
                    a.activation(AW[:, 4 * d:4 * d + 4, 0, :], src[:, :, 1, :], ACT.Copy).then_inc(q["xae"], 1)

            def dve_batch(v, j):
                jj = base_j + j
                for d in range(2):
                    s = tiles(j)[d]
                    v.wait_ge(q["exps"], 2 * jj + d + 1)
                    A, R = AR[:, d, :, 0, :], AR[:, d, :, 1, :]
                    B, K, Bh, Kh = (BK[:, d, :, i, :] for i in range(4))
                    for hp in range(2):
                        v.tensor_scalar(K[:, hp, :], icl[:, d, hp, s], col("k_a", hp), scl_ka[:, hp:hp + 1],
                                        ALU.mult, ALU.add)
                    v.tensor_tensor(Bh, kk[:, :, s], icl[:, d, :, s], ALU.mult)
                    v.scalar_tensor_tensor(out=A, in0=kk[:, :, s], scalar=-1.0, in1=A, op0=ALU.mult, op1=ALU.mult)
                    v.drain()
                    v.tensor_tensor(K, K, k[:, :, s], ALU.mult)
                    if has_y(j):
                        pass
                    for pi in range(2):
                        at = s.start + pi * CH + (CH - 1 if d == 0 else 0)
                        v.tensor_copy(wc[:, 4 * d + 2 * pi:4 * d + 2 * pi + 2],
                                      R[:, :, (pi * CH + (CH - 1 if d == 0 else 0)):(pi * CH + (CH - 1 if d == 0 else 0)) + 1]
                                      .rearrange("p a b -> p (a b)"))
                    v.drain()
                    v.tensor_tensor(K, K, B, ALU.mult)
                    if has_y(j):
                        v.tensor_tensor(R, R, r[:, :, s], ALU.mult)
                    v.drain()
                    v.tensor_tensor(B, Bh, B, ALU.mult).then_inc(q["AR"], 1)
                    v.drain()
                    for hp in range(2):
                        for pi in range(2):
                            w = wc[:, 4 * d + 2 * pi + hp:4 * d + 2 * pi + hp + 1]
                            v.tensor_scalar(BK[:, d, hp, 2:4, pi * CH:(pi + 1) * CH],
                                            BK[:, d, hp, 0:2, pi * CH:(pi + 1) * CH], w, None, ALU.mult)
                    v.drain()
                    v.nop().then_inc(q["BK"], 1) if False else v.drain().then_inc(q["BK"], 1)
                for which, (bk, M, sg, sg2) in enumerate(((0, MB, "Lb", "mb"), (2, MK, "Lk", "mk"))):
                    seen = seen_both.rearrange("p (d n) -> p d n", d=2).unsqueeze(2).to_broadcast([P, 2, 2, 2 * CH])
                    for e_ in range(2):
                        v.wait_ge(q[sg], 2 * jj + e_ + 1)
                        dst = M[:, :, 0:2, :].rearrange("p (d h e) c b -> p e d h (c b)", d=2, e=2)[:, e_]
                        v.tensor_tensor(dst, bank(bk + e_).rearrange("p (d h n) -> p d h n", d=2, h=2), seen,
                                        ALU.mult).then_inc(q[sg2], 1)
                v.drain()
                lev = cc("level").rearrange("p (j d b) -> p j d b", j=6, d=2)
                I4 = ident2.unsqueeze(1).to_broadcast([P, 4, CH])
                for d in range(2):
                    sl = slice(4 * d, 4 * d + 4)
                    v.tensor_tensor(XT[:, sl, :], MB[:, sl, 0, :],
                                    lev[:, 0, 1 - d, :].unsqueeze(1).to_broadcast([P, 4, CH]), ALU.mult)
                v.drain()
                for d in range(2):
                    sl = slice(4 * d, 4 * d + 4)
                    v.tensor_tensor(XT[:, sl, :], XT[:, sl, :], I4, ALU.add)
                ninv = [jj * 22]
                for lv_ in range(6):
                    for d in range(2):
                        sl = slice(4 * d, 4 * d + 4)
                        v.wait_ge(q["inv"], inv_count(jj, lv_, "T", d))
                        v.tensor_tensor(Tt[:, sl, :], bank(d)[:, 0:256].rearrange("p (a b) -> p a b", b=CH),
                                        lev[:, lv_, d, :].unsqueeze(1).to_broadcast([P, 4, CH]), ALU.mult) \
                            .then_inc(q["inve"], 1)
                    if lv_ == 0:
                        v.drain()
                        for d in range(2):
                            sl = slice(4 * d, 4 * d + 4)
                            v.tensor_tensor(X[:, sl, :], Tt[:, sl, :], I4, ALU.add).then_inc(q["inve"], 1)
                        continue
                    for d in range(2):
                        sl = slice(4 * d, 4 * d + 4)
                        v.wait_ge(q["inv"], inv_count(jj, lv_, "X", d))
                        if lv_ < 5:
                            v.tensor_tensor(X[:, sl, :], X[:, sl, :],
                                            bank(2 + d)[:, 0:256].rearrange("p (a b) -> p a b", b=CH), ALU.add)
                        v.tensor_tensor(XT[:, sl, :], XT[:, sl, :],
                                        bank(4 + d)[:, 0:256].rearrange("p (a b) -> p a b", b=CH), ALU.add) \
                            .then_inc(q["inve"], 1)
                for pi in range(2):
                    v.wait_ge(q["gq"], 2 * jj + pi + 1)
                    src = bank(pi).rearrange("p (g c b) -> p g c b", g=4, b=CH)
                    v.tensor_copy(G[:].rearrange("p (g c) b -> p c g b", c=2)[:, pi], src[:, :, 0, :])
                    if has_y(j):
                        v.tensor_tensor(QT[:].rearrange("p (g c) b -> p c g b", c=2)[:, pi], src[:, :, 1, :],
                                        AR[:, :, :, 1, pi * CH:(pi + 1) * CH].rearrange("p d h b -> p (d h) b"),
                                        ALU.add)
                v.drain().then_inc(q["gqe"], 1)
                v.wait_ge(q["hy"], 2 * jj + 2)
                for step in range(2):
                    half = [step, 1 - step]
                    if step:
                        v.drain()
                    for d in range(2):
                        pi = half[d]
                        for hp in range(2):
                            g = 2 * d + hp
                            v.scalar_tensor_tensor(out=SH[:, g, :], in0=ST[:, g, :],
                                                   scalar=wc[:, 4 * d + 2 * pi + hp:4 * d + 2 * pi + hp + 1],
                                                   in1=bank(2 + pi)[:, g * CH:(g + 1) * CH],
                                                   op0=ALU.mult, op1=ALU.add)
                        if has_y(j):
                            c = tiles(j)[d].start + pi * CH
                            v.tensor_tensor(mix[:, 0:2, c:c + CH], mix[:, 0:2, c:c + CH],
                                            bank(2 + pi)[:, (4 + 2 * d) * CH:(6 + 2 * d) * CH]
                                            .rearrange("p (a b) -> p a b", b=CH), ALU.add)
                            v.drain()
                    v.drain()
                    v.wait_ge(q["chS"], 2 * jj + step + 1)
                    v.tensor_tensor(ST[:], SH[:], bank(4 + step)[:, 0:4 * CH].rearrange("p (a b) -> p a b", b=CH),
                                    ALU.add)
                    v.drain().then_inc(q["che"], 1)
                    if has_y(j):
                        for d in range(2):
                            c = tiles(j)[d].start + half[d] * CH
                            v.tensor_tensor(mix[:, 0:2, c:c + CH], mix[:, 0:2, c:c + CH],
                                            bank(4 + step)[:, (4 + 2 * d) * CH:(6 + 2 * d) * CH]
                                            .rearrange("p (a b) -> p a b", b=CH), ALU.add)
                            v.drain()

            wc = sm[:, 48:56]

            def inv_count(jj, lv_, what, d):
                per = 2 + 5 * 4
                base = jj * per
                if lv_ == 0:
                    return base + d + 1
                return base + 2 + (lv_ - 1) * 4 + (0 if what == "T" else 2) + d + 1

            def inve_count(jj, lv_, what, d):
                per = 4 + 5 * 4
                base = jj * per
                if lv_ == 0:
                    return base + (0 if what == "T" else 2) + d + 1
                return base + 4 + (lv_ - 1) * 4 + (0 if what == "T" else 2) + d + 1

            def units(d):
                for hp in range(2):
                    for e_ in range(2):
                        for pi in range(2):
                            yield hp, e_, pi, 4 * d + 2 * hp + e_, slice(64 * e_, 64 * e_ + 64), slice(64 * pi, 64 * pi + 64)

            def pe_batch(e, j):
                jj = base_j + j
                T = [order[d][j] for d in range(2)]
                for d in range(2):
                    e.wait_ge(q["AR"], 2 * jj + d + 1)
                for i, (bk, sg) in enumerate(((0, "Lb"), (2, "Lk"))):
                    for half in range(2):
                        for d in range(2):
                            for hp, e_, pi, dh, re, rp in units(d):
                                if e_ == half:
                                    a = (2 * d + hp) * 2 * CH
                                    ins = e.matmul(bank(bk + e_)[rp, a:a + 2 * CH], BK[re, d, hp, i, rp],
                                                   AR[re, d, hp, :, rp], start=True, stop=True)
                        ins.then_inc(q[sg], 1)
                for d in range(2):
                    e.wait_ge(q["BK"], 2 * jj + d + 1)
                for i, sg in enumerate(("tA", "tB", "tK")):
                    for d in range(2):
                        for hp in range(2):
                            src = AR[:, d, hp, 0, :] if i == 0 else BK[:, d, hp, 1 + i, :]
                            a = (2 * d + hp) * P
                            ins = e.transpose(bank(4 + i)[:, a:a + P], src, ident)
                    ins.then_inc(q[sg], 1)
                e.wait_ge(q["mk"], 2 * jj + 2)
                for d in range(2):
                    for hp, e_, pi, dh, re, rp in units(d):
                        ins = e.matmul(bank(7)[rp, dh * CH:(dh + 1) * CH], MK[rp, dh, 0, :],
                                       vtok[rp, T[d], (2 * hp + e_) * CH:(2 * hp + e_ + 1) * CH], start=True, stop=True)
                ins.then_inc(q["w1"], 1)
                e.wait_ge(q["mb"], 2 * jj + 2)
                e.wait_ge(q["bh"], jj + 1)
                for d in range(2):
                    for hp, e_, pi, dh, re, rp in units(d):
                        a = (dh % 4) * CH
                        ins = e.matmul(bank(d)[rp, a:a + CH], MB[rp, dh, 0, :], ident2[rp, :], start=True, stop=True)
                    ins.then_inc(q["inv"], 1)
                for lv_ in range(1, 6):
                    for d in range(2):
                        e.wait_ge(q["inve"], inve_count(jj, lv_ - 1, "X", d))
                        for hp, e_, pi, dh, re, rp in units(d):
                            a = (dh % 4) * CH
                            ins = e.matmul(bank(d)[rp, a:a + CH], MB[rp, dh, 0, :], X[rp, dh, :], start=True, stop=True)
                        ins.then_inc(q["inv"], 1)
                    for d in range(2):
                        e.wait_ge(q["inve"], inve_count(jj, lv_, "T", d))
                        for hp, e_, pi, dh, re, rp in units(d):
                            a = (dh % 4) * CH
                            if lv_ < 5:
                                e.matmul(bank(2 + d)[rp, a:a + CH], XT[rp, dh, :], Tt[rp, dh, :], start=True, stop=True)
                            ins = e.matmul(bank(4 + d)[rp, a:a + CH], Tt[rp, dh, :], XT[rp, dh, :],
                                           start=True, stop=True)
                        ins.then_inc(q["inv"], 1)
                e.wait_ge(q["inve"], inve_count(jj, 5, "X", 1))
                e.wait_ge(q["w1e"], jj + 1)
                e.wait_ge(q["kh"], jj + 1)
                for d in range(2):
                    for hp, e_, pi, dh, re, rp in units(d):
                        a = (dh % 4) * 2 * CH
                        ins = e.matmul(bank(6 + d)[rp, a:a + 2 * CH], XT[rp, dh, :], AW[rp, dh, :, :],
                                       start=True, stop=True)
                    ins.then_inc(q["xa"], 1)
                e.wait_ge(q["xae"], 2 * jj + 2)
                for half in range(2):
                    for d in range(2):
                        for hp, e_, pi, dh, re, rp in units(d):
                            if pi == half:
                                a = (2 * d + hp) * 2 * CH
                                ins = e.matmul(bank(pi)[re, a:a + 2 * CH], AW[rp, dh, 1, :], MB[rp, dh, 2:0:-1, :],
                                               start=True, stop=True)
                    ins.then_inc(q["gq"], 1)
                for half in range(2):
                    for d in range(2):
                        for hp, e_, pi, dh, re, rp in units(d):
                            if pi == half:
                                a = (2 * d + hp) * CH
                                vv = vtok[rp, T[d], (2 * hp + e_) * CH:(2 * hp + e_ + 1) * CH]
                                acc = bank(2 + pi)[re, a:a + CH]
                                e.matmul(acc, MB[rp, dh, 2, :], AW[rp, dh, 0, :], start=True, stop=False)
                                ins = e.matmul(acc, KhT[rp, dh, :], vv, start=False, stop=True)
                                if has_y(j):
                                    acc = bank(2 + pi)[re, 4 * CH + a:5 * CH + a]
                                    e.matmul(acc, AW[rp, dh, 0, :], MB[rp, dh, 1, :], start=True, stop=False)
                                    ins = e.matmul(acc, vv, MK[rp, dh, 1, :], start=False, stop=True)
                    ins.then_inc(q["hy"], 1)
                e.wait_ge(q["gqe"], jj + 1)
                for step in range(2):
                    if step or jj:
                        e.wait_ge(q["che"], 2 * jj + step)
                    for d in range(2):
                        pi = step if d == 0 else 1 - step
                        for hp in range(2):
                            for e_ in range(2):
                                re = slice(64 * e_, 64 * e_ + 64)
                                a, g = (2 * d + hp) * CH, 4 * d + 2 * hp + pi
                                ins = e.matmul(bank(4 + step)[re, a:a + CH], G[re, g, :], ST[re, 2 * d + hp, :],
                                               start=True, stop=True)
                                if has_y(j):
                                    ins = e.matmul(bank(4 + step)[re, 4 * CH + a:5 * CH + a], ST[re, 2 * d + hp, :],
                                                   QT[re, g, :], start=True, stop=True)
                    ins.then_inc(q["chS"], 1)

            def dve_scan(v):
                v.memset(ST[:], 0.0)
                v.drain()
                for j in range(NBATCH):
                    dve_batch(v, j)
            phase(pe=lambda e: [pe_batch(e, j) for j in range(NBATCH)],
                  act=lambda a: [act_batch(a, j) for j in range(NBATCH)], dve=dve_scan)

            y = mix[:, 0:2, :]
            yc = arena2(f"yc{l}", [P, 2, TOK])
            ysq = arena2(f"ysq{l}", [P, 2, TOK], off=6 * K1)
            bon = arena2(f"bon{l}", [P, 2, TOK], off=12 * K1)
            rs = arena2(f"rs{l}", [P, 2, TOK], off=18 * K1)
            ro = Signal("readout_sums", 3)
            rd = Signal("readout_terms", 2)
            ra = Signal("readout_root", 2)
            segs = SEGS[n]

            def pe_read(e):
                for hp in range(2):
                    for s0, s1 in segs:
                        ins = e.matmul(PW[hp][:, s0:s1], headones, y[:, hp, s0:s1], start=True, stop=True)
                ins.then_inc(ro.sem, 1)
                e.wait_ge(rd.sem, rd.at(1))
                for hp in range(2):
                    for s0, s1 in segs:
                        ins = e.matmul(PW[2 + hp][:, s0:s1], headones, bon[:, hp, s0:s1], start=True, stop=True)
                ins.then_inc(ro.sem, 1)
                e.wait_ge(rd.sem, rd.at(2))
                for hp in range(2):
                    for s0, s1 in segs:
                        ins = e.matmul(PW[hp][:, s0:s1], headones, ysq[:, hp, s0:s1], start=True, stop=True)
                ins.then_inc(ro.sem, 1)

            def act_read(a):
                a.wait_ge(ro.sem, ro.at(3))
                for hp in range(2):
                    a.activation(rs[:, hp, 0:n], PW[hp][:, 0:n], ACT.Sqrt, scale=1.0 / CH, bias=epsc[:, 1:2]) \
                     .then_inc(ra.sem, 1)

            def dve_read(v):
                for hp in range(2):
                    v.tensor_tensor(bon[:, hp, 0:n], icl[:, 0, hp, 0:n], icl[:, 1, hp, 0:n], ALU.add)
                v.drain()
                for hp in range(2):
                    v.tensor_scalar(bon[:, hp, 0:n], bon[:, hp, 0:n], col("k_a", hp), scl_ka[:, 2 + hp:3 + hp],
                                    ALU.mult, ALU.add)
                v.drain()
                v.tensor_tensor(bon[:, :, 0:n], bon[:, :, 0:n], k[:, :, 0:n], ALU.mult)
                v.drain()
                for hp in range(2):
                    ins = v.scalar_tensor_tensor(out=bon[:, hp, 0:n], in0=r[:, hp, 0:n], scalar=col("r_k", hp),
                                                 in1=bon[:, hp, 0:n], op0=ALU.mult, op1=ALU.mult)
                ins.then_inc(rd.sem, 1)
                v.wait_ge(ro.sem, ro.at(1))
                for hp in range(2):
                    v.scalar_tensor_tensor(out=yc[:, hp, 0:n], in0=PW[hp][:, 0:n], scalar=-1.0 / CH,
                                           in1=y[:, hp, 0:n], op0=ALU.mult, op1=ALU.add)
                v.drain()
                v.tensor_tensor(ysq[:, :, 0:n], yc[:, :, 0:n], yc[:, :, 0:n], ALU.mult).then_inc(rd.sem, 1)
                v.wait_ge(ra.sem, ra.at(2))
                v.reciprocal(rs[:, :, 0:n], rs[:, :, 0:n])
                for hp in range(2):
                    v.tensor_tensor(bon[:, hp, 0:n], PW[2 + hp][:, 0:n], v_[:, hp, 0:n], ALU.mult)
                v.drain()
                for hp in range(2):
                    v.scalar_tensor_tensor(out=yc[:, hp, 0:n], in0=yc[:, hp, 0:n], scalar=col("ln_g", hp),
                                           in1=rs[:, hp, 0:n], op0=ALU.mult, op1=ALU.mult)
                v.drain()
                for hp in range(2):
                    v.scalar_tensor_tensor(out=yc[:, hp, 0:n], in0=yc[:, hp, 0:n], scalar=col("ln_b", hp),
                                           in1=bon[:, hp, 0:n], op0=ALU.add, op1=ALU.add)
                v.drain()
                v.tensor_tensor(y[:, :, 0:n], yc[:, :, 0:n], z[:, :, 0:n], ALU.mult)
            phase(pe=pe_read, act=act_read, dve=dve_read)

        phase_of = {}
        for l in range(DEPTH):
            full = l < DEPTH - 1
            n = TOK if full else SEQ
            v = lambda kind, l=l: (lambda b, s: scl[:, 3 * l + kind, 2 * b + s:2 * b + s + 1])
            pre_norm(f"pre{l}", TOK, v(0), v(1))
            conv_mixer(l, full)
            attention(l, full)
            rwkv(l, full)
            split_mix(f"b1_{l}", n)
            m = arena(f"m{l}", [P, NB, TOK])
            stream_phase(plain(f"wout{l}", t["w_out"][l], 0, 8, n, (hhi, hlo), to(m)))
            post_norm(f"post{l}", m, n, v(2))

        zero_shift = scl_zero = sm[:, 60:61]

        def dve_zero(v):
            v.memset(sm[:, 60:61], 0.0)
        phase(dve=dve_zero)
        b2 = lambda name, base=0: (lambda b, s: VC[:, 2, B2ROW[name] + base + b:B2ROW[name] + base + b + 1])
        noshift = lambda b, s: zero_shift
        LR = SEQ + 127
        revd = nc.dram_tensor("rel_bias_reversed", (8, P, LR), F32, kind="Internal").ap()

        def attn2(part):
            w = t["attn_w_in_2"][0]
            nm = "AB"[part]
            q = arena(f"q2{nm}", [P, 4, SEQ])
            k = arena(f"k2{nm}", [P, 4, SEQ], off=8 * K1)
            vch = arena(f"vc2{nm}", [P, 4, SEQ], off=16 * K1)
            AT = arena(f"AT2{nm}", [P, 4, SEQ], off=16 * K1)
            vtok = arena(f"vt2{nm}", [P, 4, SEQ], off=24 * K1)
            W = arena(f"wk2{nm}", [P, 4, SEQ], off=32 * K1)
            bias = arena(f"bias2{nm}", [P, 8, SEQ], off=40 * K1)
            rb = arena(f"rb2{nm}", [8, 513], off=56 * K1)
            rev = arena(f"rev2{nm}", [8, LR + 1], off=59 * K1)
            c0 = 1536 * part
            qs = plain(f"q2{nm}", w, c0, 4, SEQ, (hhi, hlo), to(q))
            ks = plain(f"k2{nm}", w, c0 + 512, 4, SEQ, (hhi, hlo), to(k))
            vs = plain(f"v2{nm}", w, c0 + 1024, 4, SEQ, (hhi, hlo), to(vch))

            vtu, vts = Signal("v2_turned", 4), Signal("v2_tokens", 4)

            def pe_v(e):
                e.wait_ge(S("evac_done0"), (vs["o0"] + 4) // 2)
                e.wait_ge(S("evac_done1"), (vs["o0"] + 4) // 2)
                for T in range(4):
                    if T >= 2:
                        e.wait_ge(vts.sem, vts.at(T - 1))
                    for h in range(4):
                        ins = e.transpose(bank(4 + T % 2)[:, h * P:(h + 1) * P], vch[:, h, T * P:(T + 1) * P], ident)
                    ins.then_inc(vtu.sem, 1)

            def act_v(a):
                for T in range(4):
                    a.wait_ge(vtu.sem, vtu.at(T + 1))
                    a.activation(vtok[:, T, :], bank(4 + T % 2), ACT.Copy).then_inc(vts.sem, 1)

            if part == 0:
                def pool_bias(pool):
                    pool.wait_ge(S("phase_end"), 3 * phase_of["bias"])
                    pool.dma_start(rb[:, :], t["attn_rel_bias_2"][0]).then_inc(S("rel_bias"), 16)
                    pool.wait_ge(S("rev_ready"), 1)
                    pool.dma_start(revd, rev[:, 0:LR].unsqueeze(1).to_broadcast([8, P, LR])).then_inc(S("rev_stored"), 16)
                    pool.wait_ge(S("rev_stored"), 16)
                    src = bass.AP(revd.tensor, revd.offset + P - 1, [[LR - 1, P], [P * LR, 8], [1, SEQ]])
                    pool.dma_start(bias[:, :, :], src).then_inc(S("bias_tile"), 16)

                def dve_bias(v):
                    v.wait_ge(S("rel_bias"), 16)
                    v.tensor_copy(rev[:, 255:LR], rb[:, 512:512 - (LR - 255):-1])
                    v.tensor_copy(rev[:, 0:255], rb[:, 512:513].to_broadcast([8, 255])).then_inc(S("rev_ready"), 1)
                    v.drain().then_inc(S("rev_ready2"), 1)
                    v.wait_ge(S("bias_tile"), 16)
                    v.memset(bias[0:64, :, 448:512], -1e30)
                phase_of["bias"] = len(phases)
                phase(pool=pool_bias, dve=dve_bias)

            stream_phase(qs, ks, vs, pe=pe_v, act=act_v)

            steps = [(h, qt) for h in range(8) for qt in range(4)]
            sg = {n_: S(f"a2{n_}{nm}") for n_ in ("score", "read", "soft", "exps", "prob", "turn", "AT", "pv", "out", "l")}
            scale = 64 ** -0.5
            st = sm[:, 16:32]

            def rows(h):
                return slice(64 * (h % 2), 64 * (h % 2) + 64)

            def pe_score(e, i):
                h, qt = steps[i]
                if i >= 2:
                    e.wait_ge(sg["read"], i - 1)
                e.matmul(bank(i % 2)[:, 0:(qt + 1) * P], q[rows(h), h // 2, qt * P:(qt + 1) * P],
                         k[rows(h), h // 2, 0:(qt + 1) * P], start=True, stop=True).then_inc(sg["score"], 1)

            def pe_main(e):
                pe_score(e, 0)
                for i, (h, qt) in enumerate(steps):
                    if i + 1 < len(steps):
                        pe_score(e, i + 1)
                    e.wait_ge(sg["prob"], i + 1)
                    if i >= 2:
                        e.wait_ge(sg["AT"], i - 1)
                    for kt in range(qt + 1):
                        ins = e.transpose(bank(2 + i % 2)[:, kt * P:(kt + 1) * P],
                                          W[:, i % 2, kt * P:(kt + 1) * P], ident)
                    ins.then_inc(sg["turn"], 1)
                    if qt == 3:
                        e.wait_ge(sg["AT"], i + 1)
                        if h >= 4 and h % 2 == 0:
                            e.wait_ge(sg["out"], h // 2 - 1)
                        o = bank(4 + (h // 2) % 2)
                        for kt in range(4):
                            ins = e.matmul(o[rows(h), kt * P:SEQ], vtok[:, kt, 64 * h:64 * h + 64],
                                           AT[:, kt, kt * P:SEQ], start=kt == 0, stop=kt == 3)
                        ins.then_inc(sg["pv"], 1)

            def act_at(a, i):
                h, qt = steps[i]
                a.wait_ge(sg["turn"], i + 1)
                if qt == 0 and h:
                    a.wait_ge(sg["pv"], h)
                a.activation(AT[:, 0:qt + 1, qt * P:(qt + 1) * P],
                             bank(2 + i % 2)[:, 0:(qt + 1) * P].rearrange("p (a b) -> p a b", b=P), ACT.Copy) \
                 .then_inc(sg["AT"], 1)
                if qt == 3 and h % 2 == 1:
                    a.wait_ge(sg["pv"], h + 1)
                    a.activation(mix[:, 4 * part + h // 2, 0:SEQ], bank(4 + (h // 2) % 2), ACT.Copy) \
                     .then_inc(sg["out"], 1)

            if part == 0:
                def act_main(a):
                    for i, (h, qt) in enumerate(steps):
                        N = (qt + 1) * P
                        a.wait_ge(sg["soft"], i + 1)
                        a.activation(W[:, i % 2, 0:N], W[:, i % 2, 0:N], ACT.Exp, bias=st[:, 2 + i % 2:3 + i % 2],
                                     accum_out=st[:, 4 + i % 2:5 + i % 2]).then_inc(sg["exps"], 1)
                        if i:
                            act_at(a, i - 1)
                    act_at(a, len(steps) - 1)

                def dve_main(v):
                    def logits(i):
                        h, qt = steps[i]
                        N = (qt + 1) * P
                        v.wait_ge(sg["score"], i + 1)
                        if i >= 2:
                            v.wait_ge(sg["turn"], i - 1)
                        v.scalar_tensor_tensor(out=W[:, i % 2, 0:N], in0=bank(i % 2)[:, 0:N], scalar=scale,
                                               in1=bias[:, h, SEQ - N:SEQ], op0=ALU.mult, op1=ALU.add) \
                         .then_inc(sg["read"], 1)
                        v.drain()
                        v.reduce_max(st[:, i % 2:i % 2 + 1], W[:, i % 2, 0:N], AXX)
                        v.drain()
                        v.tensor_scalar(st[:, 2 + i % 2:3 + i % 2], st[:, i % 2:i % 2 + 1], -1.0, None, ALU.mult) \
                         .then_inc(sg["soft"], 1)
                    logits(0)
                    for i, (h, qt) in enumerate(steps):
                        N = (qt + 1) * P
                        if i + 1 < len(steps):
                            logits(i + 1)
                        v.wait_ge(sg["exps"], i + 1)
                        v.reciprocal(st[:, 6 + i % 2:7 + i % 2], st[:, 4 + i % 2:5 + i % 2])
                        v.drain()
                        v.tensor_scalar(W[:, i % 2, 0:N], W[:, i % 2, 0:N], st[:, 6 + i % 2:7 + i % 2], None, ALU.mult) \
                         .then_inc(sg["prob"], 1)
            else:
                L = arena(f"l2{nm}", [P, 2, SEQ], off=40 * K1)
                NEG = arena(f"n2{nm}", [P, 2, SEQ], off=44 * K1)
                CS = arena(f"c2{nm}", [P, 2, SEQ], off=48 * K1)
                Zs = arena(f"z2{nm}", [P, 2, SEQ], off=52 * K1)

                def act_main(a):
                    def soft(i):
                        h, qt = steps[i]
                        N = (qt + 1) * P
                        a.wait_ge(sg["read"], i + 1)
                        if i >= 2:
                            a.wait_ge(sg["soft"], i - 1)
                        a.activation(L[:, i % 2, 0:N], Zs[:, i % 2, 0:N], ACT.Abs)
                        a.drain()
                        a.activation(L[:, i % 2, 0:N], L[:, i % 2, 0:N], ACT.Exp, scale=-1.0)
                        a.drain()
                        a.activation(L[:, i % 2, 0:N], L[:, i % 2, 0:N], ACT.Ln, bias=1.0).then_inc(sg["l"], 1)
                    soft(0)
                    for i, (h, qt) in enumerate(steps):
                        N = (qt + 1) * P
                        if i:
                            act_at(a, i - 1)
                        if i + 1 < len(steps):
                            soft(i + 1)
                        a.wait_ge(sg["soft"], i + 1)
                        if i >= 2:
                            a.wait_ge(sg["turn"], i - 1)
                        a.activation(W[:, i % 2, 0:N], CS[:, i % 2, 0:N], ACT.Exp).then_inc(sg["exps"], 1)
                    act_at(a, len(steps) - 1)

                def dve_main(v):
                    def zs(i):
                        h, qt = steps[i]
                        N = (qt + 1) * P
                        v.wait_ge(sg["score"], i + 1)
                        if i >= 2:
                            v.wait_ge(sg["l"], i - 1)
                        v.tensor_scalar(Zs[:, i % 2, 0:N], bank(i % 2)[:, 0:N], scale, None, ALU.mult) \
                         .then_inc(sg["read"], 1)
                        v.drain()
                        v.tensor_scalar(NEG[:, i % 2, 0:N], Zs[:, i % 2, 0:N], -1.0, 0.0, ALU.mult, ALU.min)
                        v.drain()
                        v.tensor_tensor(NEG[:, i % 2, N - P:N], NEG[:, i % 2, N - P:N], cc("strict"), ALU.mult)
                    zs(0)
                    for i, (h, qt) in enumerate(steps):
                        N = (qt + 1) * P
                        if i + 1 < len(steps):
                            zs(i + 1)
                        v.wait_ge(sg["l"], i + 1)
                        v.tensor_tensor(L[:, i % 2, N - P:N], L[:, i % 2, N - P:N], cc("strict"), ALU.mult)
                        v.drain()
                        v.tensor_tensor_scan(CS[:, i % 2, N - 1::-1] if N == SEQ or True else None,
                                             NEG[:, i % 2, N - 1::-1], L[:, i % 2, N - 1::-1], 0.0,
                                             ALU.add, ALU.subtract)
                        v.drain()
                        v.tensor_tensor(CS[:, i % 2, 0:N], CS[:, i % 2, 0:N], Zs[:, i % 2, 0:N], ALU.add) \
                         .then_inc(sg["soft"], 1)
                        v.wait_ge(sg["exps"], i + 1)
                        v.tensor_tensor(W[:, i % 2, N - P:N], W[:, i % 2, N - P:N], cc("strict"), ALU.mult) \
                         .then_inc(sg["prob"], 1)
            phase(pe=pe_main, act=act_main, dve=dve_main)

        def ffn(l):
            fhi = place(f"fhi{l}", [P, FB, SEQ], F32R, at=at_mix)
            flo = place(f"flo{l}", [P, FB, SEQ], F32R, at=at_mix + FB * SEQ * 4)
            assert at_mix + 2 * FB * SEQ * 4 <= nc.sbuf_usable_end
            gate = xT[:, 0:4, SEQ:TOK]
            pre_norm(f"ffn{l}", SEQ, b2("ffn_pre", 8 * l), noshift)
            gb = place(f"gb{l}", [P, 2, SEQ], at=at_mix + 2 * FB * SEQ * 4)
            wg, wu, wd = (kview(t[n_][l]) for n_ in ("ffn_w_gate_2", "ffn_w_up_2", "ffn_w_down_2"))

            def ev_gate(eng, i, o, acc):
                eng.wait_ge(S("evac_done1"), i + evac_base(st_gu))
                return eng.activation(gb[:, 0, :], acc, ACT.Silu)

            def evac_base(st):
                return st["o0"] // 2

            def ev_up(eng, i, o, acc):
                eng.wait_ge(S("evac_done0"), i + (evac_base(st_gu) + 1))
                eng.tensor_tensor(gb[:, 1, :], gb[:, 0, :], acc, ALU.mult)
                eng.drain()
                hi = fhi[:, bass.ds(i, 1), :].rearrange("p a n -> p (a n)")
                eng.tensor_copy(hi, gb[:, 1, :])
                eng.drain()
                lo = flo[:, bass.ds(i, 1), :].rearrange("p a n -> p (a n)")
                return eng.tensor_tensor(lo, gb[:, 1, :], hi.bitcast(F32), ALU.subtract)
            body = [(wg, 0, 8, 0, P, 0, True, True), (wu, 0, 8, 0, P, 1, True, True)]
            st_gu = add_stage(f"gateup{l}", body, FB, SEQ, (hhi, hlo), [("act", ev_gate), ("dve", ev_up)])
            stream_phase(st_gu)
            m = arena2(f"mf{l}", [P, NB, SEQ])
            body = []
            for o in range(2):
                for k0, kb in ((0, 8), (8, 8), (16, 6)):
                    body.append((wd, k0, kb, o * P, 2 * P, o, k0 == 0, k0 == 16))
            stream_phase(add_stage(f"down{l}", body, NB // 2, SEQ, (fhi, flo), [("act", to(m))] * 2))
            post_norm(f"ffnpost{l}", m, SEQ, b2("ffn_post", 8 * l))

        def recurrent():
            w = t["rg_w_in_2"][0]
            gate = arena("rggate", [P, NB, SEQ])
            xr = arena("rgx", [P, NB, SEQ], off=16 * K1)
            xc = arena("rgxc", [P, NB, SEQ], off=32 * K1)
            gs = plain("rggate", w, 0, 8, SEQ, (hhi, hlo), to(gate, ACT.Gelu_apprx_tanh))
            xs = plain("rgxr", w, 1024, 8, SEQ, (hhi, hlo), to(xr))
            stream_phase(gs, xs)
            wa = arena2("rgwa", [P, 8, 256])
            wi = arena2("rgwi", [P, 8, 256], off=8 * K1)
            WK = arena2("rgwork", [P, 2, 6, SEQ], off=16 * K1)
            col = lambda name, i: VC[:, 2, B2ROW[name] + i:B2ROW[name] + i + 1]

            def pool_w(pool):
                pool.wait_ge(S("phase_end"), 3 * phase_of["rg"])
                pool.dma_start(wa[:], t["rg_w_a_2"][0].rearrange("n (k p) j -> p (n k) j", p=P)).then_inc(S("rg_w"), 16)
                pool.dma_start(wi[:], t["rg_w_i_2"][0].rearrange("n (k p) j -> p (n k) j", p=P)).then_inc(S("rg_w"), 16)
            xcr, gm, ga, rd, rs = S("rg_xc"), S("rg_mm"), S("rg_act"), S("rg_dve"), S("rg_sqrt")

            def dve_conv(v):
                for b in range(NB):
                    v.tensor_scalar(xc[:, b, :], xr[:, b, :], col("rg_conv_w", 24 + b), col("rg_conv_b", b),
                                    ALU.mult, ALU.add)
                v.drain()
                for j in range(3):
                    sh = 3 - j
                    for b in range(NB):
                        v.scalar_tensor_tensor(out=xc[:, b, sh:SEQ], in0=xr[:, b, 0:SEQ - sh],
                                               scalar=col("rg_conv_w", 8 * j + b), in1=xc[:, b, sh:SEQ],
                                               op0=ALU.mult, op1=ALU.add)
                    v.drain()
                v.drain().then_inc(xcr, 1)
                for b in range(NB):
                    wk = WK[:, b % 2]
                    A, TH, U, MU, I = (wk[:, i, :] for i in range(5))
                    v.wait_ge(ga, b + 1)
                    v.tensor_scalar(MU, TH, 1.0, None, ALU.add)
                    v.drain()
                    v.reciprocal(MU, MU)
                    v.drain()
                    v.scalar_tensor_tensor(out=MU, in0=TH, scalar=2.0, in1=MU, op0=ALU.mult, op1=ALU.mult) \
                     .then_inc(rd, 1)
                    v.tensor_tensor(U, I, xc[:, b, :], ALU.mult)
                    v.drain()
                    v.wait_ge(rs, b + 1)
                    v.tensor_tensor(U, U, MU, ALU.mult)
                    v.drain()
                    v.tensor_tensor_scan(TH, A, U, 0.0, ALU.mult, ALU.add)
                    v.drain()
                    v.tensor_tensor(mix[:, b, 0:SEQ], TH, gate[:, b, :], ALU.mult).then_inc(rd, 1)

            def pe_g(e):
                e.wait_ge(S("rg_w"), 32)
                e.wait_ge(xcr, 1)
                for b in range(NB):
                    n_, ob = b // 2, b % 2
                    if b >= 2:
                        e.wait_ge(ga, b - 1)
                    for i, W_ in enumerate((wa, wi)):
                        for k_ in range(2):
                            ins = e.matmul(bank(2 * (b % 2) + i), W_[:, 2 * n_ + k_, ob * P:(ob + 1) * P],
                                           xc[:, 2 * n_ + k_, :], start=k_ == 0, stop=k_ == 1)
                    ins.then_inc(gm, 1)

            def act_g(a):
                def root(b):
                    wk = WK[:, b % 2]
                    a.wait_ge(rd, 2 * b + 1)
                    a.activation(wk[:, 3, :], wk[:, 3, :], ACT.Sqrt).then_inc(rs, 1)
                for b in range(NB):
                    wk = WK[:, b % 2]
                    A, TH, U, MU, I, Rr = (wk[:, i, :] for i in range(6))
                    a.wait_ge(gm, b + 1)
                    if b >= 2:
                        a.wait_ge(rd, 2 * (b - 1))
                    a.activation(Rr, bank(2 * (b % 2)), ACT.Sigmoid, bias=col("b_a", b))
                    a.activation(I, bank(2 * (b % 2) + 1), ACT.Sigmoid, bias=col("b_i", b))
                    a.drain()
                    a.activation(A, Rr, ACT.Exp, scale=scl[:, 6, 8 + b:9 + b])
                    a.activation(TH, Rr, ACT.Tanh, scale=scl[:, 6, b:b + 1]).then_inc(ga, 1)
                    if b:
                        root(b - 1)
                root(NB - 1)
            phase_of["rg"] = len(phases)
            phase(pool=pool_w, pe=pe_g, act=act_g, dve=dve_conv)

        pre_norm("mix0", SEQ, b2("mix_pre"), noshift)
        attn2(0)
        attn2(1)
        split_mix("b2_0", SEQ)
        m0 = arena("mo0", [P, NB, SEQ])
        stream_phase(plain("wout2", t["attn_w_out_2"][0], 0, 8, SEQ, (hhi, hlo), to(m0)))
        post_norm("mixpost0", m0, SEQ, b2("mix_post"))
        ffn(0)
        pre_norm("mix1", SEQ, b2("mix_pre", 8), noshift)
        recurrent()
        split_mix("b2_1", SEQ)
        m1 = arena("mo1", [P, NB, SEQ])
        stream_phase(plain("wout3", t["rg_w_out_2"][0], 0, 8, SEQ, (hhi, hlo), to(m1)))
        post_norm("mixpost1", m1, SEQ, b2("mix_post", 8))
        ffn(1)

        otok = arena("otok", [P, 4, D])

        def pe_out(e):
            for T in range(4):
                if T >= 2:
                    e.wait_ge(S("out_rows"), T - 1)
                for b in range(NB):
                    ins = e.transpose(PW[T % 2][:, b * P:(b + 1) * P], xT[:, b, T * P:(T + 1) * P], ident)
                ins.then_inc(S("out_turned"), 1)

        def dve_out(v):
            for T in range(4):
                v.wait_ge(S("out_turned"), T + 1)
                v.tensor_copy(otok[:, T, :], PW[T % 2][:, :]).then_inc(S("out_rows"), 1)

        def sp_out(sp):
            for T in range(4):
                sp.wait_ge(S("out_rows"), T + 1)
                sp.dma_start(out[0, T * P:(T + 1) * P, :], otok[:, T, :]).then_inc(S("out_stored"), 16)
            sp.wait_ge(S("out_stored"), 64)
        phase(sp=sp_out, pe=pe_out, dve=dve_out)

        def run(eng, which):
            for i, ph in enumerate(phases):
                if which in ph:
                    ph[which](eng)
                eng.drain().then_inc(S("phase_end"), 1)
                eng.wait_ge(S("phase_end"), 3 * (i + 1))

        block = ctx.enter_context(nc.Block())

        @block.sync
        def _(sp):
            for ph in phases:
                if "sp" in ph:
                    ph["sp"](sp)

        @block.gpsimd
        def _(pool):
            for ph in phases:
                if "pool" in ph:
                    ph["pool"](pool)

        @block.tensor
        def _(pe):
            run(pe, "pe")

        @block.scalar
        def _(act):
            hi_part(act, 0, stages[0], 0, stages[0]["body"][0])
            run(act, "act")

        @block.vector
        def _(dve):
            lo_part(dve, 0, stages[0], 0, stages[0]["body"][0])
            run(dve, "dve")


_INS = ["x", "c", "ctx", "c_ctx", "mod_w", "mod_b", "norm_pre_g", "norm_post_g", "w_in", "w_out", "rwkv_w0",
        "rwkv_w_up", "rwkv_a0", "rwkv_a_up", "rwkv_k_k", "rwkv_k_a", "rwkv_r_k", "rwkv_ln_g", "rwkv_ln_b", "conv_w",
        "diff_lambda", "diff_subln_g", "attn_w_in_2", "attn_rel_bias_2", "attn_w_out_2", "rg_w_in_2", "rg_conv_w_2",
        "rg_conv_b_2", "rg_w_a_2", "rg_b_a_2", "rg_w_i_2", "rg_b_i_2", "rg_lambda_2", "rg_w_out_2", "norm_mix_pre_2",
        "norm_mix_post_2", "norm_ffn_pre_2", "norm_ffn_post_2", "ffn_w_gate_2", "ffn_w_up_2", "ffn_w_down_2"]


def kernel(**inputs):
    from concourse import bacc as _bacc
    from concourse.bass_utils import run_bass_kernel_spmd as _run

    nc = _bacc.Bacc("TRN2", target_bir_lowering=False, num_devices=1)
    arrays, t = {}, {}
    for name in _INS:
        a = np.ascontiguousarray(inputs[name])
        arrays[f"in_{name}"] = a
        t[name] = nc.dram_tensor(f"in_{name}", a.shape, mybir.dt.from_np(a.dtype), kind="ExternalInput").ap()
    _, table = constant_columns()
    arrays["shape_constants"] = table
    t["const"] = nc.dram_tensor("shape_constants", table.shape, F32, kind="ExternalInput").ap()
    out = nc.dram_tensor("out_0", (1, SEQ, D), F32, kind="ExternalOutput").ap()
    build_program(nc, t, out)
    r = _run(nc, [arrays], core_ids=[0])
    return r.results[0]["out_0"]
```

```python
import math
from contextlib import ExitStack

import numpy as np

import concourse.bass as bass
from concourse import mybir

ALU = mybir.AluOpType
ACT = mybir.ActivationFunctionType
AXX = mybir.AxisListType.X
F32 = mybir.dt.float32
F32R = mybir.dt.float32r

P = 128
D = 1024
NB = D // P
SEQ, CTX = 512, 256
TOK = SEQ + CTX
NT = TOK // P
DEPTH = 2
CH = 64
DFF = 2816
FB = DFF // P
GRID_W = 64
EPS = 1e-6
GN_EPS = 64e-5
C_R, C_K, C_V, C_LORA, C_Z = 0, 256, 512, 768, 1024
C_CONV = 1280
C_AQ, C_AK, C_AV, C_AZ = 2304, 2816, 3328, 3840

LAYER_VECS = [("mod_b", 24), ("pre_g", 8), ("post_g", 8), ("w0", 4), ("a0", 4), ("k_k", 2), ("k_a", 2),
              ("r_k", 2), ("ln_g", 2), ("ln_b", 2), ("conv_w", 6), ("subln", 1)]
BLOCK2_VECS = [("rg_conv_w", 32), ("rg_conv_b", 8), ("b_a", 8), ("b_i", 8), ("lam", 8),
               ("mix_pre", 16), ("mix_post", 16), ("ffn_pre", 16), ("ffn_post", 16)]


def row_table(vecs, start=0):
    at, out = start, {}
    for name, n in vecs:
        out[name] = at
        at += n
    return out, at


LROW, LROWS = row_table(LAYER_VECS)
B2ROW, B2ROWS = row_table(BLOCK2_VECS)
CROW = LROWS


def constant_columns():
    cols, parts = {}, []

    def put(name, a):
        cols[name] = (sum(p.shape[1] for p in parts), a.shape[1])
        parts.append(a.astype(np.float32))

    p = np.arange(P)
    put("ident", np.eye(P))
    put("headones", (p[:, None] // CH == p[None, :] // CH))
    put("ones", np.ones((P, P)))
    t = p % CH
    s = np.arange(CH)
    put("ident2", t[:, None] == s[None, :])
    for d in range(2):
        before = t[:, None] < s[None, :] if d == 0 else t[:, None] > s[None, :]
        put(f"seen{d}", np.concatenate([before, before | (t[:, None] == s[None, :])], 1))
    lev = []
    for j in range(6):
        for d in range(2):
            r, c = t[:, None] >> j, s[None, :] >> j
            same = (r >> 1) == (c >> 1)
            lev.append(same & ((r & 1) == 1) & ((c & 1) == 0) if d == 0 else same & ((r & 1) == 0) & ((c & 1) == 1))
    put("level", np.concatenate(lev, 1))
    put("reset", np.tile((np.arange(TOK) % CH != 0), (P, 1)))
    inv = 10000.0 ** (-np.arange(0, 32, 2, dtype=np.float32) / np.float32(32))
    tok = np.arange(SEQ)
    ch = p % 64
    pos = np.where(ch[:, None] < 32, tok[None, :] // GRID_W, tok[None, :] % GRID_W).astype(np.float32)
    ang = pos * inv[ch % 16].astype(np.float32)[:, None]
    put("cos", np.cos(ang))
    put("sin", np.where((ch % 32)[:, None] < 16, -1.0, 1.0) * np.sin(ang))
    put("strict", p[None, :] < p[:, None])
    return cols, np.concatenate(parts, 1)


CONST_AT, _CONST = constant_columns()
NCONST = _CONST.shape[1]


def build_program(nc, t, out):
    with ExitStack() as ctx:
        base = (nc.sbuf_base + 63) // 64 * 64
        here = [base]

        def place(name, shape, dt=F32, at=None):
            size = int(np.prod(shape[1:])) * 4
            off = here[0] if at is None else at
            if at is None:
                here[0] += (size + 63) // 64 * 64
            return nc.alloc_sbuf_tensor_at(name, [int(x) for x in shape], dt, offset=off)

        xT = place("xT", [P, NB, TOK])
        at_h = here[0]
        hhi = place("hhi", [P, NB, TOK], F32R)
        hlo = place("hlo", [P, NB, TOK], F32R)
        wraw = place("wraw", [P, 2, 8, P])
        at_whi1 = here[0] + 8 * P * 4
        whi = place("whi", [P, 2, 8, P], F32R)
        at_wlo1 = here[0] + 8 * P * 4
        wlo = place("wlo", [P, 2, 8, P], F32R)
        const = place("const", [P, NCONST])
        VC = place("VC", [P, 3, P])
        modT = place("modT", [P, 2, 24, 2])
        cs = place("cs", [P, NB, 2])
        scl = place("scl", [P, 8, 16])
        sm = place("sm", [P, 64])
        epsc = place("epsc", [P, 3])
        ltmp = place("ltmp", [P, 8, 8])
        at_mix = here[0]
        mix = place("mix", [P, NB, TOK])
        at_a = here[0]
        arena_size = nc.sbuf_usable_end - at_a

        def arena(name, shape, dt=F32, off=0):
            size = int(np.prod(shape[1:])) * 4
            assert off + size <= arena_size, (name, off + size, arena_size)
            return place(name, shape, dt, at=at_a + off)

        def arena2(name, shape, dt=F32, off=0):
            size = int(np.prod(shape[1:])) * 4
            assert off + size <= 2 * NB * TOK * 4, (name, off + size)
            return place(name, shape, dt, at=at_h + off)

        K1 = 1024

        def kview(w):
            return w.rearrange("(k p) n -> p k n", p=P)

        def cc(name):
            a, n = CONST_AT[name]
            return const[:, a:a + n]

        ident, headones, ones, ident2 = cc("ident"), cc("headones"), cc("ones"), cc("ident2")
        PW = [ctx.enter_context(nc.psum_tensor(f"PW{i}", [P, 1024], F32)) for i in range(4)]

        def bank(i):
            return PW[i // 2][:, (i % 2) * 512:(i % 2) * 512 + 512]

        sems = {}

        def S(name):
            if name not in sems:
                sems[name] = ctx.enter_context(nc.semaphore(name))
            return sems[name]

        totals = {}

        class Signal:
            def __init__(self, name, total):
                self.sem, self.base = S(name), totals.get(name, 0)
                totals[name] = self.base + total

            def at(self, n):
                return self.base + n

        SEGS = {TOK: [(0, 512), (512, TOK)], SEQ: [(0, 512)]}
        stages = []

        def add_stage(name, body, iters, ntok, rhs, outs):
            st = dict(name=name, body=body, iters=iters, ntok=ntok, rhs=rhs, outs=outs, U=len(body), no=len(outs))
            if stages:
                l = stages[-1]
                st["g0"], st["o0"] = l["g0"] + l["U"] * l["iters"], l["o0"] + l["no"] * l["iters"]
                l["next"] = body[0]
            else:
                st["g0"], st["o0"] = 0, 0
            st["next"] = None
            assert st["U"] % 2 == 0 and st["no"] % 2 == 0
            stages.append(st)
            return st

        def plain(name, w, col, nblk, ntok, rhs, evac):
            v = kview(w)
            body = [(v, 0, 8, col + P * j, 2 * P, j, True, True) for j in range(2)]
            return add_stage(name, body, nblk // 2, ntok, rhs, [("act", evac)] * 2)

        def turns(st):
            n, lo = st["iters"], 1 if st["g0"] == 0 or "ready" in st else 0
            return lo, n - 1

        def run_turns(eng, st, do):
            lo, hi = turns(st)
            if lo == 1 and st["iters"] > 1:
                do(0, False)
            if hi - lo >= 2:
                with eng.Fori(lo, hi) as i:
                    do(i, False)
            else:
                for i in range(lo, hi):
                    do(i, False)
            do(st["iters"] - 1, True)

        def wait_pos(eng, sem, value):
            if not isinstance(value, int) or value > 0:
                eng.wait_ge(sem, value)

        def sp_stage(sp, st):
            def do(i, last):
                for u, (v, k0, kb, c0, cstep, o, first, fin) in enumerate(st["body"]):
                    g = i * st["U"] + (st["g0"] + u)
                    wait_pos(sp, S("w_split"), g - 1)
                    sp.dma_start(wraw[:, u % 2, 0:kb, :], v[:, k0:k0 + kb, bass.ds(i * cstep + c0, P)]) \
                        .then_inc(S(f"w_landed{u % 2}"), 16)
            run_turns(sp, st, do)

        def hi_part(act, i, st, u, desc):
            g = i * st["U"] + (st["g0"] + u)
            slot = u % 2
            act.wait_ge(S(f"w_landed{slot}"), (i * (st["U"] // 2) + (st["g0"] // 2 + u // 2)) * 16 + 16)
            wait_pos(act, S("w_used"), g - 1)
            kb = desc[2]
            act.activation(whi[:, slot, 0:kb, :], wraw[:, slot, 0:kb, :], ACT.Copy).then_inc(S("w_hi"), 1)

        def lo_part(dve, i, st, u, desc):
            g = i * st["U"] + (st["g0"] + u)
            slot = u % 2
            dve.wait_ge(S("w_hi"), g + 1)
            kb = desc[2]
            dve.tensor_tensor(wlo[:, slot, 0:kb, :], wraw[:, slot, 0:kb, :], whi[:, slot, 0:kb, :].bitcast(F32),
                              ALU.subtract).then_inc(S("w_split"), 1)

        def split_and_evac(eng, which, part, st):
            def do(i, last):
                for u, desc in enumerate(st["body"]):
                    nxt = st["body"][(u + 1) % st["U"]]
                    if u == st["U"] - 1 and last:
                        nxt = st["next"]
                    if nxt is not None:
                        part(eng, i, st, u + 1, nxt)
                    if "beside" in st and which in st["beside"]:
                        st["beside"][which](eng, i * st["U"] + u)
                    o = desc[5]
                    if desc[7] and st["outs"][o][0] == which:
                        eng.wait_ge(S("w_used"), i * st["U"] + (st["g0"] + u + 1))
                        st["outs"][o][1](eng, i, o, PW[o % 2][:, 0:st["ntok"]]) \
                            .then_inc(S(f"evac_done{o % 2}"), 1)
            run_turns(eng, st, do)

        def pe_stage(pe, st):
            def do(i, last):
                for u, (v, k0, kb, c0, cstep, o, first, fin) in enumerate(st["body"]):
                    g = i * st["U"] + (st["g0"] + u)
                    pe.wait_ge(S("w_split"), g + 1)
                    if first:
                        wait_pos(pe, S(f"evac_done{o % 2}"), i * (st["no"] // 2) + (st["o0"] // 2 + o // 2))
                    rhi, rlo = st["rhs"]
                    for s0, s1 in SEGS[st["ntok"]]:
                        acc = PW[o % 2][:, s0:s1]
                        for k in range(kb):
                            if "ready" in st and isinstance(i, int) and i == 0 and u == 0 and s0 == 0:
                                pe.wait_ge(*st["ready"](k))
                            a, b = first and k == 0, fin and k == kb - 1
                            pe.matmul(acc, whi[:, u % 2, k, :], rhi[:, k0 + k, s0:s1], start=a, stop=False)
                            pe.matmul(acc, wlo[:, u % 2, k, :], rhi[:, k0 + k, s0:s1], start=False, stop=False)
                            last_mm = pe.matmul(acc, whi[:, u % 2, k, :], rlo[:, k0 + k, s0:s1], start=False, stop=b)
                    last_mm.then_inc(S("w_used"), 1)
            run_turns(pe, st, do)

        phases = []

        def phase(name, **engines):
            phases.append(engines)

        def to(dest, func=ACT.Copy, ntok=None):
            def ev(eng, i, o, acc):
                n = acc.shape[1]
                d = dest[:, bass.ds(i * 2 + o, 1), 0:n].rearrange("p a n -> p (a n)")
                return eng.activation(d, acc, func)
            return ev

        xtok = arena("xtok", [P, NT, D])
        VR = arena("VR", [P, 3, P], off=24 * K1)
        lamb = arena("lamb", [P, 2, 256], off=26 * K1)
        lamp = arena("lamp", [P, 2, 2, 64], off=28 * K1)
        n_in = [0]

        def sp_inputs(sp):
            def load(dst, src):
                sp.dma_start(dst, src).then_inc(S("inputs"), 16)
                n_in[0] += 16
            load(const[:, :], t["const"])
            load(xtok[:, 0:4, :], t["x"][0].rearrange("(a p) n -> p a n", p=P))
            load(xtok[:, 4:6, :], t["ctx"][0].rearrange("(a p) n -> p a n", p=P))

            def rows(i, at, ap, n):
                load(VR[at:at + n, i, :], ap)
            for l in range(DEPTH):
                r = LROW
                one = lambda name, a: rows(l, r[name], a.rearrange("(k p) -> k p", p=P), a.shape[0] // P)
                one("mod_b", t["mod_b"][l])
                one("pre_g", t["norm_pre_g"][l])
                one("post_g", t["norm_post_g"][l])
                one("w0", t["rwkv_w0"][l].rearrange("d n -> (d n)"))
                one("a0", t["rwkv_a0"][l].rearrange("d n -> (d n)"))
                one("k_k", t["rwkv_k_k"][l])
                one("k_a", t["rwkv_k_a"][l])
                one("r_k", t["rwkv_r_k"][l].rearrange("d n -> (d n)"))
                one("ln_g", t["rwkv_ln_g"][l])
                one("ln_b", t["rwkv_ln_b"][l])
                one("conv_w", t["conv_w"][l].rearrange("d n -> (d n)"))
                one("subln", t["diff_subln_g"][l])
            rows(0, CROW, t["c"][0].rearrange("(k p) -> k p", p=P), 8)
            rows(0, CROW + 8, t["c_ctx"].rearrange("(k p) -> k p", p=P), 8)
            b = B2ROW
            rows(2, b["rg_conv_w"], t["rg_conv_w_2"][0, :, 0].rearrange("j (k p) -> (j k) p", p=P), 32)
            rows(2, b["rg_conv_b"], t["rg_conv_b_2"][0].rearrange("(k p) -> k p", p=P), 8)
            rows(2, b["b_a"], t["rg_b_a_2"][0].rearrange("j (k p) -> (j k) p", p=P), 8)
            rows(2, b["b_i"], t["rg_b_i_2"][0].rearrange("j (k p) -> (j k) p", p=P), 8)
            rows(2, b["lam"], t["rg_lambda_2"][0].rearrange("(k p) -> k p", p=P), 8)
            for n, key in (("mix_pre", "norm_mix_pre_2"), ("mix_post", "norm_mix_post_2"),
                           ("ffn_pre", "norm_ffn_pre_2"), ("ffn_post", "norm_ffn_post_2")):
                rows(2, b[n], t[key].rearrange("l (k p) -> (l k) p", p=P), 16)
            for l in range(DEPTH):
                load(lamb[:, l, :], t["diff_lambda"][l].rearrange("a b -> (a b)").unsqueeze(0).to_broadcast([P, 256]))

            for g in range(MSLOTS, MGROUPS):
                sp.wait_ge(S("mod_used"), g - MSLOTS + 1)
                load_mod(sp, g)

        mslots = [arena("mod_w0", [P, 8, 512], off=32 * K1), arena("mod_w1", [P, 8, 512], off=48 * K1)] + \
                 [arena2(f"mod_w{2 + i}", [P, 8, 512], off=16 * i * K1) for i in range(3)]
        MSLOTS, MGROUPS = len(mslots), 6 * DEPTH

        def load_mod(eng, g):
            src = kview(t["mod_w"][g // 6])[:, :, (g % 6) * 512:(g % 6) * 512 + 512]
            eng.dma_start(mslots[g % MSLOTS][:, :, :], src).then_inc(S(f"mod_landed{g % MSLOTS}"), 16)

        N_INPUTS = 3 + 12 * DEPTH + 2 + 9 + DEPTH

        def pe_inputs(pe):
            pe.wait_ge(S("inputs"), 16 * N_INPUTS)
            for i, n in ((0, CROW + 16), (1, LROWS), (2, B2ROWS)):
                ins = pe.transpose(bank(6)[:, i * P:i * P + n], VR[0:n, i, :], ident[0:n, 0:n])
            ins.then_inc(S("vec_cols"), 1)
            for T in range(NT):
                if T >= 2:
                    pe.wait_ge(S("xT_ready"), T - 1)
                for b in range(NB):
                    ins = pe.transpose(PW[T % 2][:, b * P:(b + 1) * P], xtok[:, T, b * P:(b + 1) * P], ident)
                ins.then_inc(S("xT_turned"), 1)
            pe.wait_ge(S("silu_c"), 1)
            for g in range(MGROUPS):
                pe.wait_ge(S(f"mod_landed{g % MSLOTS}"), 16 * (g // MSLOTS + 1))
                for b in range(4):
                    for k in range(8):
                        ins = pe.matmul(bank(7)[:, 8 * g + 2 * b:8 * g + 2 * b + 2],
                                        mslots[g % MSLOTS][:, k, b * P:(b + 1) * P], cs[:, k, :],
                                        start=k == 0, stop=k == 7)
                ins.then_inc(S("mod_used"), 1)

        def dve_inputs(dve):
            dve.memset(epsc[:, 0:1], EPS)
            dve.memset(epsc[:, 2:3], 0.0)
            dve.memset(epsc[:, 1:2], GN_EPS)
            dve.wait_ge(S("inputs"), 16 * N_INPUTS)
            dve.wait_ge(S("vec_cols"), 1)
            for i, n in ((0, CROW + 16), (1, LROWS), (2, B2ROWS)):
                ins = dve.tensor_copy(VC[:, i, 0:n], bank(6)[:, i * P:i * P + n])
            ins.then_inc(S("VC_ready"), 1)
            for T in range(NT):
                dve.wait_ge(S("xT_turned"), T + 1)
                dve.tensor_copy(xT[:, :, T * P:(T + 1) * P], PW[T % 2][:, :].rearrange("p (b n) -> p b n", b=NB)) \
                   .then_inc(S("xT_ready"), 1)
            lv = lamb[:].rearrange("p l (a c b) -> p l a c b", a=2, c=2)
            dve.tensor_tensor(lamp[:], lv[:, :, :, 0, :], lv[:, :, :, 1, :], ALU.mult)
            dve.drain()
            dve.tensor_reduce(sm[:, 0:4], lamp[:].rearrange("p l a b -> p (l a) b"), AXX, ALU.add) \
               .then_inc(S("lam_sums"), 1)
            dve.wait_ge(S("lam_exps"), 1)
            for l in range(DEPTH):
                init = 0.8 - 0.6 * math.exp(-0.3 * l)
                dve.tensor_tensor(sm[:, 8 + l:9 + l], sm[:, 4 + 2 * l + 1:4 + 2 * l + 2],
                                  sm[:, 4 + 2 * l:4 + 2 * l + 1], ALU.subtract)
                dve.drain()
                dve.tensor_scalar(sm[:, 8 + l:9 + l], sm[:, 8 + l:9 + l], init, None, ALU.subtract)
                dve.tensor_scalar(scl[:, 7, l:l + 1], VC[:, l, LROW["subln"]:LROW["subln"] + 1], 1.0 - init, None,
                                  ALU.mult)
            lcol = VC[:, 2, B2ROW["lam"]:B2ROW["lam"] + 8]
            E, A, Q, R, Z = (ltmp[:, i, :] for i in range(5))
            dve.wait_ge(S("lam_exps"), 2)
            dve.tensor_scalar(A, E, 2.0, None, ALU.add)
            dve.drain()
            dve.reciprocal(Q, A)
            dve.drain()
            dve.tensor_tensor(A, E, Q, ALU.mult)
            dve.drain()
            dve.tensor_tensor(Q, A, A, ALU.mult)
            dve.memset(R, 2.0 / 19)
            dve.drain()
            for n in range(17, 0, -2):
                dve.tensor_tensor(R, R, Q, ALU.mult)
                dve.drain()
                dve.tensor_scalar(R, R, 2.0 / n, None, ALU.add)
                dve.drain()
            dve.tensor_tensor(R, R, A, ALU.mult)
            dve.tensor_scalar(Z, lcol, -1.0, 0.0, ALU.mult, ALU.max)
            dve.drain()
            dve.tensor_tensor(R, R, Z, ALU.add)
            dve.drain()
            dve.tensor_scalar(scl[:, 6, 0:8], R, 8.0, None, ALU.mult)
            dve.tensor_scalar(scl[:, 6, 8:16], R, -8.0, None, ALU.mult)
            dve.wait_ge(S("mod_used"), MGROUPS)
            dve_scales(dve)
            lo_part(dve, 0, stages[0], 0, stages[0]["body"][0])

        def act_inputs(act):
            for g in range(MSLOTS):
                load_mod(act, g)
            act.wait_ge(S("VC_ready"), 1)
            act.activation(cs[:, :, 0], VC[:, 0, CROW:CROW + 8], ACT.Silu)
            act.activation(cs[:, :, 1], VC[:, 0, CROW + 8:CROW + 16], ACT.Silu).then_inc(S("silu_c"), 1)
            act.wait_ge(S("lam_sums"), 1)
            act.activation(sm[:, 4:8], sm[:, 0:4], ACT.Exp).then_inc(S("lam_exps"), 1)
            act.activation(ltmp[:, 1, :], VC[:, 2, B2ROW["lam"]:B2ROW["lam"] + 8], ACT.Abs)
            act.drain()
            act.activation(ltmp[:, 0, :], ltmp[:, 1, :], ACT.Exp, scale=-1.0).then_inc(S("lam_exps"), 1)
            hi_part(act, 0, stages[0], 0, stages[0]["body"][0])

        phase("inputs", sp=sp_inputs, pe=pe_inputs, dve=dve_inputs, act=act_inputs)

        def stream_phase(*sts, before=(), pe=None, dve=None, act=None):
            if before and "ready" in before[-1]:
                sts[0]["ready"] = before[-1]["ready"]

            def engine(which, stage, after):
                def run(e):
                    for part in before:
                        if which in part:
                            part[which](e)
                    for st in sts:
                        stage(e, st)
                    if after:
                        after(e)
                return run
            phase(sts[0]["name"], sp=lambda sp: [sp_stage(sp, st) for st in sts], pe=engine("pe", pe_stage, pe),
                  act=engine("act", lambda e, st: split_and_evac(e, "act", hi_part, st), act),
                  dve=engine("dve", lambda e, st: split_and_evac(e, "dve", lo_part, st), dve))

        def dve_scales(dve):
            for l in range(DEPTH):
                for s in range(2):
                    m = bank(7)[:, 48 * l:48 * l + 48].rearrange("p (b s) -> p b s", s=2)
                    dve.tensor_tensor(modT[:, l, :, s], m[:, :, s], VC[:, l, 0:24], ALU.add)
            dve.drain()
            for l in range(DEPTH):
                for s in range(2):
                    g, pg = (VC[:, l, LROW[n]:LROW[n] + 8] for n in ("pre_g", "post_g"))
                    v = scl[:, 3 * l:3 * l + 3, :].rearrange("p a (b s) -> p a b s", s=2)
                    dve.scalar_tensor_tensor(out=v[:, 0, :, s], in0=modT[:, l, 8:16, s], scalar=1.0, in1=g,
                                             op0=ALU.add, op1=ALU.mult)
                    dve.tensor_copy(v[:, 1, :, s], modT[:, l, 0:8, s])
                    dve.tensor_tensor(v[:, 2, :, s], modT[:, l, 16:24, s], pg, ALU.mult)

        def inverse_root(a, dst, work, sums, count, eps):
            a.activation(work, sums, ACT.Ln, scale=1.0 / count, bias=eps)
            a.drain()
            return a.activation(dst, work, ACT.Exp, scale=-0.5)

        def norm_buffers(name):
            o = 48 * K1
            return (arena(f"sq_{name}", [P, 2, TOK], off=o), arena(f"root_{name}", [P, TOK], off=o + 6 * K1),
                    arena(f"rstd_{name}", [P, TOK], off=o + 9 * K1), arena(f"tmp_{name}", [P, 2, TOK], off=o + 12 * K1))

        def post_norm(name, m, ntok, gcol, own_buffers=None):
            segs = SEGS[ntok]
            sq, root, rstd, tmp = own_buffers or norm_buffers("post" + name)
            made, summed, rooted, xnew = (Signal(f"post_{n_}", c) for n_, c in
                                          (("squares", NB), ("summed", NB), ("rooted", 1), ("x", NB)))

            def act(a):
                a.preload_act_table_set("natural_log_exp_and_others")
                for b in range(NB):
                    if b >= 2:
                        a.wait_ge(summed.sem, summed.at(b - 1))
                    a.activation(sq[:, b % 2, 0:ntok], m[:, b, 0:ntok], ACT.Square).then_inc(made.sem, 1)
                a.wait_ge(summed.sem, summed.at(NB))
                inverse_root(a, rstd[:, 0:ntok], root[:, 0:ntok], PW[2][:, 0:ntok], D, epsc[:, 0:1]) \
                    .then_inc(rooted.sem, 1)

            def pe(e):
                for b in range(NB):
                    e.wait_ge(made.sem, made.at(b + 1))
                    for s0, s1 in segs:
                        ins = e.matmul(PW[2][:, s0:s1], ones, sq[:, b % 2, s0:s1], start=b == 0, stop=b == NB - 1)
                    ins.then_inc(summed.sem, 1)

            def dve(v):
                v.wait_ge(rooted.sem, rooted.at(1))
                for b in range(NB):
                    for s, (s0, s1) in enumerate(segs):
                        v.scalar_tensor_tensor(out=tmp[:, b % 2, s0:s1], in0=m[:, b, s0:s1], scalar=gcol(b, s),
                                               in1=rstd[:, s0:s1], op0=ALU.mult, op1=ALU.mult)
                    if b:
                        v.tensor_tensor(xT[:, b - 1, 0:ntok], xT[:, b - 1, 0:ntok], tmp[:, (b - 1) % 2, 0:ntok], ALU.add) \
                         .then_inc(xnew.sem, 1)
                    v.drain()
                v.tensor_tensor(xT[:, NB - 1, 0:ntok], xT[:, NB - 1, 0:ntok], tmp[:, (NB - 1) % 2, 0:ntok], ALU.add) \
                 .then_inc(xnew.sem, 1)
                v.drain()
            return dict(pe=pe, act=act, dve=dve, xnew=xnew)

        def pre_norm(name, ntok, gcol, shift, xnew=None):
            segs = SEGS[ntok]
            ns = len(segs)
            sq, root, rstd, tmp = norm_buffers("pre" + name)
            made, summed, rooted, scaled, rounded, low_done = (
                Signal(f"pre_{n_}", c) for n_, c in (("squares", NB), ("summed", NB), ("rooted", 1),
                                                     ("scaled", NB), ("rounded", NB), ("low", NB)))

            def act(a):
                a.preload_act_table_set("natural_log_exp_and_others")
                for b in range(NB):
                    if xnew:
                        a.wait_ge(xnew.sem, xnew.at(b + 1))
                    if b >= 2:
                        a.wait_ge(summed.sem, summed.at(b - 1))
                    a.activation(sq[:, b % 2, 0:ntok], xT[:, b, 0:ntok], ACT.Square).then_inc(made.sem, 1)
                a.wait_ge(summed.sem, summed.at(NB))
                inverse_root(a, rstd[:, 0:ntok], root[:, 0:ntok], PW[3][:, 0:ntok], D, epsc[:, 0:1]) \
                    .then_inc(rooted.sem, 1)
                for b in range(NB):
                    a.wait_ge(scaled.sem, scaled.at(b + 1))
                    for s, (s0, s1) in enumerate(segs):
                        ins = a.activation(hhi[:, b, s0:s1], tmp[:, b % 2, s0:s1], ACT.Identity, bias=shift(b, s))
                    ins.then_inc(rounded.sem, 1)

            def pe(e):
                for b in range(NB):
                    e.wait_ge(made.sem, made.at(b + 1))
                    for s0, s1 in segs:
                        ins = e.matmul(PW[3][:, s0:s1], ones, sq[:, b % 2, s0:s1], start=b == 0, stop=b == NB - 1)
                    ins.then_inc(summed.sem, 1)

            def dve(v):
                def low(b):
                    v.wait_ge(rounded.sem, rounded.at(b + 1))
                    for s, (s0, s1) in enumerate(segs):
                        ins = v.scalar_tensor_tensor(out=hlo[:, b, s0:s1], in0=tmp[:, b % 2, s0:s1], scalar=shift(b, s),
                                                     in1=hhi[:, b, s0:s1].bitcast(F32), op0=ALU.add, op1=ALU.subtract)
                    ins.then_inc(low_done.sem, 1)
                v.wait_ge(rooted.sem, rooted.at(1))
                for b in range(NB):
                    if b >= 2:
                        v.drain()
                    for s, (s0, s1) in enumerate(segs):
                        ins = v.scalar_tensor_tensor(out=tmp[:, b % 2, s0:s1], in0=xT[:, b, s0:s1], scalar=gcol(b, s),
                                                     in1=rstd[:, s0:s1], op0=ALU.mult, op1=ALU.mult)
                    ins.then_inc(scaled.sem, 1)
                    if b:
                        low(b - 1)
                low(NB - 1)
            return dict(pe=pe, act=act, dve=dve, ready=lambda k: (low_done.sem, low_done.at(k + 1)))

        def split_mix(ntok):
            hr, low_done = Signal("mix_rounded", NB), Signal("mix_low", NB)

            def act(a):
                for b in range(NB):
                    a.activation(hhi[:, b, 0:ntok], mix[:, b, 0:ntok], ACT.Copy).then_inc(hr.sem, 1)

            def dve(v):
                for b in range(NB):
                    v.wait_ge(hr.sem, hr.at(b + 1))
                    v.tensor_tensor(hlo[:, b, 0:ntok], mix[:, b, 0:ntok], hhi[:, b, 0:ntok].bitcast(F32),
                                    ALU.subtract).then_inc(low_done.sem, 1)
            return dict(act=act, dve=dve, ready=lambda k: (low_done.sem, low_done.at(k + 1)))

        HALF = {TOK: 2, SEQ: 1}

        def conv_mixer(l, full, before):
            n = TOK if full else SEQ
            cb = arena(f"cb{l}", [P, 8, TOK])
            u = arena(f"cu{l}", [P, TOK], off=24 * K1)
            y = arena(f"cy{l}", [P, TOK], off=27 * K1)
            w = lambda j, hp: VC[:, l, LROW["conv_w"] + 2 * j + hp:LROW["conv_w"] + 2 * j + hp + 1]

            def dve(v):
                v.wait_ge(S("evac_done1"), conv_last[l])
                v.wait_ge(S("evac_done0"), conv_last[l])
                for hp in range(2):
                    v.tensor_tensor(u[:, 0:n], cb[:, 2 + hp, 0:n], cb[:, 4 + hp, 0:n], ALU.mult)
                    v.drain()
                    v.tensor_scalar(y[:, 0:n], u[:, 0:n], w(1, hp), None, ALU.mult)
                    v.drain()
                    for s0, s1 in SEGS[n]:
                        v.scalar_tensor_tensor(out=y[:, s0 + 1:s1], in0=u[:, s0:s1 - 1], scalar=w(0, hp),
                                               in1=y[:, s0 + 1:s1], op0=ALU.mult, op1=ALU.add)
                    v.drain()
                    for s0, s1 in SEGS[n]:
                        v.scalar_tensor_tensor(out=y[:, s0:s1 - 1], in0=u[:, s0 + 1:s1], scalar=w(2, hp),
                                               in1=y[:, s0:s1 - 1], op0=ALU.mult, op1=ALU.add)
                    v.drain()
                    v.tensor_tensor(y[:, 0:n], y[:, 0:n], cb[:, hp, 0:n], ALU.mult)
                    v.drain()
                    v.tensor_tensor(mix[:, 2 + hp, 0:n], y[:, 0:n], cb[:, 6 + hp, 0:n], ALU.mult)
                    v.drain()
            w_in = t["w_in"][l]
            a = plain(f"conv{l}", w_in, C_CONV, 6, n, (hhi, hlo), to(cb))
            b = plain(f"convz{l}", w_in, C_CONV + 768, 2, n, (hhi, hlo), to(cb[:, 6:8, :], ACT.Silu))
            conv_last[l] = (b["o0"] + 2) // 2
            stream_phase(a, b, before=before, dve=dve)

        conv_last = {}

        def attention(l, full):
            n = TOK if full else SEQ
            w_in = t["w_in"][l]
            q = arena(f"aq{l}", [P, 4, TOK])
            k = arena(f"ak{l}", [P, 4, TOK], off=12 * K1)
            z = arena(f"az{l}", [P, 4, TOK], off=24 * K1)
            vtok = arena(f"avt{l}", [P, NT, 512], off=36 * K1)
            vch = arena(f"avc{l}", [P, 4, TOK], off=48 * K1)
            AT = arena(f"aAT{l}", [P, NT, 512], off=48 * K1)
            prob = arena(f"apr{l}", [P, 2, TOK], off=60 * K1)
            rot = arena(f"arot{l}", [P, 2, SEQ], off=60 * K1)
            st = sm[:, 16:32]

            vtu, vts = Signal("v_turned", NT), Signal("v_tokens", NT)

            def pe_v(e):
                e.wait_ge(S("evac_done0"), (vs["o0"] + 4) // 2)
                e.wait_ge(S("evac_done1"), (vs["o0"] + 4) // 2)
                for T in range(NT):
                    if T >= 2:
                        e.wait_ge(vts.sem, vts.at(T - 1))
                    for h in range(4):
                        ins = e.transpose(bank(4 + T % 2)[:, h * P:(h + 1) * P], vch[:, h, T * P:(T + 1) * P], ident)
                    ins.then_inc(vtu.sem, 1)

            def act_v(a):
                for T in range(NT):
                    a.wait_ge(vtu.sem, vtu.at(T + 1))
                    a.activation(vtok[:, T, :], bank(4 + T % 2), ACT.Copy).then_inc(vts.sem, 1)
            vs = plain(f"av{l}", w_in, C_AV, 4, TOK, (hhi, hlo), to(vch))
            stream_phase(vs, pe=pe_v, act=act_v)

            def dve_rope(v):
                for i, sts in ((0, qs), (1, ks)):
                    v.wait_ge(S("evac_done0"), (sts["o0"] + 4) // 2)
                    v.wait_ge(S("evac_done1"), (sts["o0"] + 4) // 2)
                    x = (q, k)[i]
                    for h in range(4):
                        v.stream_shuffle(rot[:, 0, :], x[:, h, 0:SEQ], [j ^ 16 for j in range(32)])
                        v.tensor_tensor(rot[:, 1, :], x[:, h, 0:SEQ], cc("cos"), ALU.mult)
                        v.drain()
                        v.tensor_tensor(rot[:, 0, :], rot[:, 0, :], cc("sin"), ALU.mult)
                        v.drain()
                        v.tensor_tensor(x[:, h, 0:SEQ], rot[:, 0, :], rot[:, 1, :], ALU.add)
                        v.drain()
            qs = plain(f"aq{l}", w_in, C_AQ, 4, n, (hhi, hlo), to(q))
            ks = plain(f"ak{l}", w_in, C_AK, 4, TOK, (hhi, hlo), to(k))
            zs = plain(f"az{l}", w_in, C_AZ, 4, n, (hhi, hlo), to(z, ACT.Silu))
            stream_phase(qs, ks, zs, dve=dve_rope)

            steps = []
            for h in range(4):
                steps += [(h, qt, 0, 0, NT) for qt in range(4)]
                if full:
                    steps += [(h, qt, SEQ, 4, 2) for qt in (4, 5)]
            finals = []
            for i, (h, qt, c0, kt0, nk) in enumerate(steps):
                if qt in (3, 5):
                    finals.append((i, h, qt == 5))
            fin_at = {i: (f, h, c) for f, (i, h, c) in enumerate(finals)}
            ns, nf = len(steps), len(finals)
            sc_, mx, ex, cb_, tr, at, pv, osq, osum, ort, omix = (
                Signal(f"attn_{nm}", c) for nm, c in (
                    ("scores", 2 * ns), ("max", ns), ("exps", 2 * ns), ("combined", ns), ("turned", ns), ("AT", ns),
                    ("out", nf), ("out_read", 2 * nf), ("sums", nf), ("root", nf), ("mixed", nf)))
            scale = 64 ** -0.5
            osb = place(f"aosb{l}", [P, 3, 512], at=at_mix)

            def pe_scores(e, i):
                h, qt, c0, kt0, nk = steps[i]
                for j in range(2):
                    if i:
                        e.wait_ge(ex.sem, ex.at(2 * (i - 1) + j + 1))
                    width = nk * P
                    for s0 in range(0, width, 512):
                        s1 = min(width, s0 + 512)
                        ins = e.matmul(PW[j][:, s0:s1], q[64 * j:64 * j + 64, h, qt * P:(qt + 1) * P],
                                       k[64 * j:64 * j + 64, h, c0 + s0:c0 + s1], start=True, stop=True)
                    ins.then_inc(sc_.sem, 1)

            def pe_attn(e):
                pe_scores(e, 0)
                for i, (h, qt, c0, kt0, nk) in enumerate(steps):
                    if i + 1 < len(steps):
                        pe_scores(e, i + 1)
                    e.wait_ge(cb_.sem, cb_.at(i + 1))
                    if i:
                        e.wait_ge(at.sem, at.at(i))
                    for kt in range(nk):
                        ins = e.transpose(PW[2][:, kt * P:(kt + 1) * P], prob[:, 0, kt * P:(kt + 1) * P], ident)
                    ins.then_inc(tr.sem, 1)
                    if i in fin_at:
                        f, _, is_ctx = fin_at[i]
                        w = 256 if is_ctx else 512
                        e.wait_ge(at.sem, at.at(i + 1))
                        if f:
                            e.wait_ge(osq.sem, osq.at(2 * f))
                        for kt in range(nk):
                            ins = e.matmul(bank(6)[:, 0:w], vtok[:, kt0 + kt, h * P:(h + 1) * P],
                                           AT[:, kt, 0:w], start=kt == 0, stop=kt == nk - 1)
                        ins.then_inc(pv.sem, 1)
                        e.wait_ge(osq.sem, osq.at(2 * f + 2))
                        if f:
                            e.wait_ge(ort.sem, ort.at(f))
                        e.matmul(bank(7)[:, 0:w], ones, osb[:, 1, 0:w], start=True, stop=True).then_inc(osum.sem, 1)

            def act_attn(a):
                for i, (h, qt, c0, kt0, nk) in enumerate(steps):
                    a.wait_ge(mx.sem, mx.at(i + 1))
                    if i:
                        a.wait_ge(tr.sem, tr.at(i))
                    for j in range(2):
                        a.activation(prob[:, j, 0:nk * P], PW[j][:, 0:nk * P], ACT.Exp, scale=scale,
                                     bias=st[:, 2 + j:3 + j], accum_out=st[:, 4 + j:5 + j]).then_inc(ex.sem, 1)
                    a.wait_ge(tr.sem, tr.at(i + 1))
                    is_ctx = qt >= 4
                    if qt in (0, 4) and i:
                        a.wait_ge(pv.sem, pv.at(sum(1 for x in finals if x[0] < i)))
                    qq = (qt - 4 if is_ctx else qt) * P
                    a.activation(AT[:, 0:nk, qq:qq + P], PW[2][:, 0:nk * P].rearrange("p (a b) -> p a b", b=P),
                                 ACT.Copy).then_inc(at.sem, 1)
                    if i in fin_at:
                        f, _, is_ctx = fin_at[i]
                        w = 256 if is_ctx else 512
                        a.wait_ge(pv.sem, pv.at(f + 1))
                        if f:
                            a.wait_ge(omix.sem, omix.at(f))
                        a.activation(osb[:, 0, 0:w], bank(6)[:, 0:w], ACT.Copy).then_inc(osq.sem, 1)
                        a.activation(osb[:, 1, 0:w], bank(6)[:, 0:w], ACT.Square).then_inc(osq.sem, 1)
                        a.wait_ge(osum.sem, osum.at(f + 1))
                        a.activation(osb[:, 2, 0:w], bank(7)[:, 0:w], ACT.Sqrt, scale=1.0 / P, bias=epsc[:, 0:1]) \
                         .then_inc(ort.sem, 1)

            def dve_attn(v):
                def finish(f, h, is_ctx):
                    w, c = (256, SEQ) if is_ctx else (512, 0)
                    v.wait_ge(ort.sem, ort.at(f + 1))
                    v.reciprocal(osb[:, 2, 0:w], osb[:, 2, 0:w])
                    v.drain()
                    v.scalar_tensor_tensor(out=osb[:, 0, 0:w], in0=osb[:, 0, 0:w], scalar=scl[:, 7, l:l + 1],
                                           in1=osb[:, 2, 0:w], op0=ALU.mult, op1=ALU.mult)
                    v.drain()
                    v.tensor_tensor(mix[:, 4 + h, c:c + w], osb[:, 0, 0:w], z[:, h, c:c + w], ALU.mult) \
                     .then_inc(omix.sem, 1)
                for i, (h, qt, c0, kt0, nk) in enumerate(steps):
                    for j in range(2):
                        v.wait_ge(sc_.sem, sc_.at(2 * i + j + 1))
                        v.reduce_max(st[:, j:j + 1], PW[j][:, 0:nk * P], AXX)
                    v.drain()
                    v.tensor_scalar(st[:, 2:4], st[:, 0:2], -scale, None, ALU.mult).then_inc(mx.sem, 1)
                    v.wait_ge(ex.sem, ex.at(2 * i + 2))
                    v.reciprocal(st[:, 6:8], st[:, 4:6])
                    v.drain()
                    v.tensor_tensor(st[:, 8:9], st[:, 7:8], sm[:, 8 + l:9 + l], ALU.mult)
                    v.drain()
                    v.tensor_scalar(prob[:, 1, 0:nk * P], prob[:, 1, 0:nk * P], st[:, 8:9], None, ALU.mult)
                    v.drain()
                    v.scalar_tensor_tensor(out=prob[:, 0, 0:nk * P], in0=prob[:, 0, 0:nk * P], scalar=st[:, 6:7],
                                           in1=prob[:, 1, 0:nk * P], op0=ALU.mult, op1=ALU.add).then_inc(cb_.sem, 1)
                    if i in fin_at:
                        finish(*fin_at[i])
            phase("attention", pe=pe_attn, act=act_attn, dve=dve_attn)

        def rwkv(l, full):
            n = TOK if full else SEQ
            w_in = t["w_in"][l]
            col = lambda name, i: VC[:, l, LROW[name] + i:LROW[name] + i + 1]
            r = arena(f"r{l}", [P, 2, TOK])
            k = arena(f"k{l}", [P, 2, TOK], off=6 * K1)
            v_ = arena(f"v{l}", [P, 2, TOK], off=12 * K1)
            z = arena(f"z{l}", [P, 2, TOK], off=18 * K1)
            lora = arena(f"lora{l}", [P, 2, TOK], off=24 * K1)
            kk = arena(f"kk{l}", [P, 2, TOK], off=30 * K1)
            nkk = kk
            icl = arena(f"icl{l}", [P, 2, 2, TOK], off=36 * K1)
            vtok = arena(f"rvt{l}", [P, NT, 256], off=48 * K1)
            wup = arena(f"wup{l}", [P, 2, 256], off=54 * K1)
            cm = arena2(f"cm{l}", [P, 2, 2, TOK])
            cum = arena2(f"cum{l}", [P, 2, 2, TOK], off=12 * K1)
            AR = arena2(f"AR{l}", [P, 2, 2, 3, P], off=24 * K1)
            BK = arena2(f"BK{l}", [P, 2, 2, 4, P], off=30 * K1)
            MB = arena2(f"MB{l}", [P, 8, 3, CH], off=38 * K1)
            MK = arena2(f"MK{l}", [P, 8, 2, CH], off=44 * K1)
            AW = arena(f"AW{l}", [P, 8, 2, CH], off=54 * K1)
            Tt = arena(f"Tt{l}", [P, 8, CH], off=58 * K1)
            X = arena(f"X{l}", [P, 8, CH], off=60 * K1)
            XT = arena(f"XT{l}", [P, 8, CH], off=62 * K1)
            G = arena(f"G{l}", [P, 8, CH], off=64 * K1)
            QT = arena(f"QT{l}", [P, 8, CH], off=66 * K1)
            ST = arena(f"ST{l}", [P, 4, CH], off=24 * K1)
            LTbd = arena(f"LTbd{l}", [P, 8, P], off=26 * K1)
            Tbd = place(f"Tbd{l}", [P, 8, P], at=at_whi1)
            XTbd = place(f"XTbd{l}", [P, 8, P], at=at_wlo1)
            SH = arena(f"SH{l}", [P, 4, CH], off=25 * K1)
            t1 = arena2(f"t1{l}", [P, 2, TOK], off=24 * K1)
            t2 = arena2(f"t2{l}", [P, 2, TOK], off=30 * K1)

            r_st = plain(f"pr{l}", w_in, C_R, 2, n, (hhi, hlo), to(r))
            k_st = plain(f"pk{l}", w_in, C_K, 2, TOK, (hhi, hlo), to(k))
            v_st = plain(f"pv{l}", w_in, C_V, 2, TOK, (hhi, hlo), to(v_))

            def ev_lora(eng, i, o, acc):
                return eng.activation(lora[:, o, 0:TOK], acc, ACT.Tanh if o == 0 else ACT.Copy)
            l_st = plain(f"pl{l}", w_in, C_LORA, 2, TOK, (hhi, hlo), ev_lora)
            z_st = plain(f"pz{l}", w_in, C_Z, 2, n, (hhi, hlo), to(z, ACT.Silu))
            stream_phase(r_st, k_st, v_st, l_st, z_st)

            lnorm, s_wup, s_vtok, s_vturn = (Signal("kk_squares", 2), Signal("lora_weights", 32), Signal("rwkv_v_tokens", NT),
                                             Signal("rwkv_v_turned", NT))
            s_kksum, s_kkroot = Signal("kk_summed", 2), Signal("kk_root", 2)

            def pool_prep(pool):
                pool.wait_ge(S("phase_end"), 3 * phase_of[f"rprep{l}"])
                pool.dma_start(wup[:, 0, :], t["rwkv_w_up"][l].rearrange("d a n -> (d a) n")).then_inc(s_wup.sem, 16)
                pool.dma_start(wup[:, 1, :], t["rwkv_a_up"][l].rearrange("d a n -> (d a) n")).then_inc(s_wup.sem, 16)

            up, upe = Signal("lora_up", 8), Signal("lora_up_read", 8)

            def pe_prep(e):
                for T in range(NT):
                    if T >= 2:
                        e.wait_ge(s_vtok.sem, s_vtok.at(T - 1))
                    for hp in range(2):
                        ins = e.transpose(bank(6 + T % 2)[:, hp * P:(hp + 1) * P], v_[:, hp, T * P:(T + 1) * P], ident)
                    ins.then_inc(s_vturn.sem, 1)
                e.wait_ge(s_wup.sem, s_wup.at(32))
                i = 0
                for kind in range(2):
                    for d in range(2):
                        for hp in range(2):
                            if i >= 2:
                                e.wait_ge(upe.sem, upe.at(i - 1))
                            for s0, s1 in SEGS[TOK]:
                                ins = e.matmul(PW[i % 2][:, s0:s1], wup[64 * d:64 * d + 64, kind, hp * P:(hp + 1) * P],
                                               lora[64 * d:64 * d + 64, kind, s0:s1], start=True, stop=True)
                            ins.then_inc(up.sem, 1)
                            i += 1
                for hp in range(2):
                    e.wait_ge(lnorm.sem, lnorm.at(hp + 1))
                    if hp == 0:
                        e.wait_ge(upe.sem, upe.at(8))
                    for s0, s1 in SEGS[TOK]:
                        ins = e.matmul(PW[hp][:, s0:s1], headones, t1[:, hp, s0:s1], start=True, stop=True)
                    ins.then_inc(s_kksum.sem, 1)

            def act_prep(a):
                i = 0
                for kind in range(2):
                    for d in range(2):
                        for hp in range(2):
                            a.wait_ge(up.sem, up.at(i + 1))
                            dst = (cm, icl)[kind][:, d, hp, :]
                            a.activation(dst, PW[i % 2][:, 0:TOK], ACT.Sigmoid,
                                         bias=col(("w0", "a0")[kind], 2 * d + hp)).then_inc(upe.sem, 1)
                            i += 1
                for hp in range(2):
                    a.wait_ge(s_kksum.sem, s_kksum.at(hp + 1))
                    a.activation(t2[:, hp, :], PW[hp][:, 0:TOK], ACT.Sqrt).then_inc(s_kkroot.sem, 1)

            def dve_prep(v):
                for hp in range(2):
                    v.tensor_scalar(kk[:, hp, :], k[:, hp, :], col("k_k", hp), None, ALU.mult)
                v.drain()
                for hp in range(2):
                    v.tensor_tensor(t1[:, hp, :], kk[:, hp, :], kk[:, hp, :], ALU.mult).then_inc(lnorm.sem, 1)
                v.memset(mix[:, 0:2, 0:n], 0.0)
                for T in range(NT):
                    v.wait_ge(s_vturn.sem, s_vturn.at(T + 1))
                    v.tensor_copy(vtok[:, T, :], bank(6 + T % 2)[:, 0:256]).then_inc(s_vtok.sem, 1)
                v.wait_ge(upe.sem, upe.at(4))
                v.tensor_scalar(cm[:], cm[:], -math.exp(-0.5), None, ALU.mult)
                v.drain()
                for hp in range(2):
                    v.tensor_tensor_scan(cum[:, 0, hp, :], cc("reset"), cm[:, 0, hp, :], 0.0, ALU.mult, ALU.add)
                    v.tensor_tensor_scan(cum[:, 1, hp, ::-1], cc("reset"), cm[:, 1, hp, ::-1], 0.0, ALU.mult, ALU.add)
                v.drain()
                v.tensor_tensor(cm[:], cum[:], cm[:], ALU.subtract)
                v.wait_ge(s_kkroot.sem, s_kkroot.at(2))
                v.tensor_scalar(t2[:], t2[:], 1e-12, None, ALU.max)
                v.drain()
                v.reciprocal(t2[:], t2[:])
                v.drain()
                v.scalar_tensor_tensor(out=kk[:].rearrange("p a b -> p (a b)"), in0=kk[:].rearrange("p a b -> p (a b)"),
                                       scalar=-1.0, in1=t2[:].rearrange("p a b -> p (a b)"),
                                       op0=ALU.mult, op1=ALU.mult)
                v.tensor_scalar(scl_ka[:, 0:2], VC[:, l, LROW["k_a"]:LROW["k_a"] + 2], -1.0, 1.0, ALU.mult, ALU.add)
                v.tensor_scalar(scl_ka[:, 2:4], VC[:, l, LROW["k_a"]:LROW["k_a"] + 2], -2.0, 2.0, ALU.mult, ALU.add)
            scl_ka = sm[:, 40:44]
            phase_of[f"rprep{l}"] = len(phases)
            phase("rwkv prep", pool=pool_prep, pe=pe_prep, act=act_prep, dve=dve_prep)

            order = [[4, 5, 0, 1, 2, 3], [5, 4, 3, 2, 1, 0]]
            NBATCH = NT

            def has_y(j):
                return full or j >= 2

            per = dict(exps=2, AR=2, BK=2, Lb=2, Lk=2, tA=1, tB=1, tK=1, mb=2, mk=2, aw=1, bh=1, kh=1, w1=1, w1e=1,
                       ltbd=1, T=12, Te=12, Tbd=10, X=8, Xe=10, XT=10, XTe=12, XTbd=12, xa=2, xae=2, gq=2, gqe=1,
                       hy=2, chS=2, che=2)
            sem = {nm: S(f"rw_{nm}") for nm in per}

            def value(nm, j, n):
                return (l * NBATCH + j) * per[nm] + n

            def tiles(j):
                return [slice(order[d][j] * P, order[d][j] * P + P) for d in range(2)]

            def group(d):
                return slice(4 * d, 4 * d + 4)

            a0, a1 = CONST_AT["seen0"][0], CONST_AT["seen1"][0]
            assert a1 == a0 + 2 * CH
            seen_both = const[:, a0:a0 + 4 * CH]
            levels = cc("level").rearrange("p (j d b) -> p j d b", j=6, d=2)
            I4 = ident2.unsqueeze(1).to_broadcast([P, 4, CH])

            def wcol(j, d, pi, hp):
                c = 48 + 8 * (j % 2) + 4 * d + 2 * pi + hp
                return sm[:, c:c + 1]

            def block_diagonal(a, dst, src, sl):
                a.activation(dst[0:64, sl, 0:CH], src[0:64], ACT.Copy)
                return a.activation(dst[64:P, sl, CH:P], src[64:P], ACT.Copy)

            def act_exps(a, j):
                if j:
                    a.wait_ge(sem["tK"], value("tK", j - 1, 1))
                for d in range(2):
                    s = tiles(j)[d]
                    a.activation(AR[:, d, :, 0, :], cm[:, d, :, s], ACT.Exp)
                    a.activation(AR[:, d, :, 1 + j % 2, :], cum[:, d, :, s], ACT.Exp)
                    a.activation(BK[:, d, :, 0, :], cum[:, d, :, s], ACT.Exp, scale=-1.0).then_inc(sem["exps"], 1)

            def act_batch(a, j):
                v4 = lambda i: bank(i).rearrange("p (a b) -> p a b", b=CH)
                if j:
                    a.wait_ge(sem["chS"], value("chS", j - 1, 2))
                a.wait_ge(sem["tA"], value("tA", j, 1))
                a.activation(AW[:, :, 0, :], v4(4), ACT.Copy).then_inc(sem["aw"], 1)
                a.wait_ge(sem["tB"], value("tB", j, 1))
                a.activation(MB[:, :, 2, :], v4(5), ACT.Copy).then_inc(sem["bh"], 1)
                a.wait_ge(sem["mb"], value("mb", j, 2))
                block_diagonal(a, LTbd, MB[:, :, 0, :], slice(0, 8)).then_inc(sem["ltbd"], 1)
                for d in range(2):
                    a.wait_ge(sem["XTe"], value("XTe", j, d + 1))
                    block_diagonal(a, XTbd, XT[:, group(d), :], group(d)).then_inc(sem["XTbd"], 1)
                a.wait_ge(sem["w1"], value("w1", j, 1))
                a.activation(AW[:, :, 1, :], v4(7), ACT.Copy).then_inc(sem["w1e"], 1)
                a.wait_ge(sem["tK"], value("tK", j, 1))
                a.activation(MK[:, :, 0, :], v4(6), ACT.Copy).then_inc(sem["kh"], 1)
                for lv in range(1, 6):
                    for d in range(2):
                        a.wait_ge(sem["Te"], value("Te", j, 2 * lv + d + 1))
                        block_diagonal(a, Tbd, Tt[:, group(d), :], group(d)).then_inc(sem["Tbd"], 1)
                    for d in range(2):
                        a.wait_ge(sem["XTe"], value("XTe", j, 2 * lv + d + 1))
                        block_diagonal(a, XTbd, XT[:, group(d), :], group(d)).then_inc(sem["XTbd"], 1)
                    if lv == 1 and j + 1 < NBATCH:
                        act_exps(a, j + 1)
                for d in range(2):
                    a.wait_ge(sem["xa"], value("xa", j, d + 1))
                    src = bank(6 + d).rearrange("p (a c b) -> p a c b", c=2, b=CH)
                    a.activation(AW[:, group(d), 1::-1, :], src, ACT.Copy).then_inc(sem["xae"], 1)

            def pool_batch(g, j):
                for d in range(2):
                    s = tiles(j)[d]
                    A, R = AR[:, d, :, 0, :], AR[:, d, :, 1 + j % 2, :]
                    B, K, Bh = (BK[:, d, :, i, :] for i in range(3))
                    if j:
                        g.wait_ge(sem["tK"], value("tK", j - 1, 1))
                    for hp in range(2):
                        g.tensor_scalar(K[:, hp, :], icl[:, d, hp, s], col("k_a", hp), scl_ka[:, hp:hp + 1],
                                        ALU.mult, ALU.add)
                    g.tensor_tensor(Bh, nkk[:, :, s], icl[:, d, :, s], ALU.mult)
                    g.drain()
                    g.wait_ge(sem["exps"], value("exps", j, d + 1))
                    g.tensor_tensor(A, nkk[:, :, s], A, ALU.mult)
                    g.tensor_tensor(K, K, k[:, :, s], ALU.mult)
                    g.tensor_scalar(Bh, Bh, -1.0, None, ALU.mult)
                    end = CH - 1 if d == 0 else 0
                    c = 48 + 8 * (j % 2) + 4 * d
                    g.tensor_copy(sm[:, c:c + 4].rearrange("p (i h) -> p h i", i=2), R[:, :, end::CH])
                    g.drain()
                    g.tensor_tensor(K, K, B, ALU.mult)
                    if has_y(j):
                        g.tensor_tensor(R, R, r[:, :, s], ALU.mult)
                    g.drain()
                    g.tensor_tensor(B, Bh, B, ALU.mult).then_inc(sem["AR"], 1)
                    g.drain()
                    for hp in range(2):
                        for pi in range(2):
                            g.tensor_scalar(BK[:, d, hp, 2:4, pi * CH:(pi + 1) * CH],
                                            BK[:, d, hp, 0:2, pi * CH:(pi + 1) * CH], wcol(j, d, pi, hp), None,
                                            ALU.mult)
                    g.drain().then_inc(sem["BK"], 1)

            def dve_batch(v, j):
                for bk, M, made, masked in ((0, MB, "Lb", "mb"), (2, MK, "Lk", "mk")):
                    seen = seen_both.rearrange("p (d n) -> p d n", d=2).unsqueeze(2).to_broadcast([P, 2, 2, 2 * CH])
                    for e_ in range(2):
                        v.wait_ge(sem[made], value(made, j, e_ + 1))
                        dst = M[:, :, 0:2, :].rearrange("p (d h e) c b -> p e d h (c b)", d=2, e=2)[:, e_]
                        v.tensor_tensor(dst, bank(bk + e_).rearrange("p (d h n) -> p d h n", d=2, h=2), seen,
                                        ALU.mult).then_inc(sem[masked], 1)
                    if M is MB:
                        v.drain()
                        v.tensor_tensor(XT[:].rearrange("p (d h) b -> p d h b", d=2),
                                        MB[:, :, 0, :].rearrange("p (d h) b -> p d h b", d=2),
                                        levels[:, 0, ::-1, :].unsqueeze(2).to_broadcast([P, 2, 4, CH]), ALU.mult)
                        v.drain()
                        for d in range(2):
                            v.tensor_tensor(XT[:, group(d), :], XT[:, group(d), :], I4, ALU.add) \
                             .then_inc(sem["XTe"], 1)
                for lv in range(6):
                    for d in range(2):
                        v.wait_ge(sem["T"], value("T", j, 2 * lv + d + 1))
                        v.tensor_tensor(Tt[:, group(d), :], bank(d)[:, 0:256].rearrange("p (a b) -> p a b", b=CH),
                                        levels[:, lv, d, :].unsqueeze(1).to_broadcast([P, 4, CH]), ALU.mult) \
                         .then_inc(sem["Te"], 1)
                    if lv == 0:
                        v.drain()
                        for d in range(2):
                            v.tensor_tensor(X[:, group(d), :], Tt[:, group(d), :], I4, ALU.add) \
                             .then_inc(sem["Xe"], 1)
                        continue
                    for d in range(2):
                        if lv < 5:
                            v.wait_ge(sem["X"], value("X", j, 2 * lv + d - 1))
                            v.tensor_tensor(X[:, group(d), :], X[:, group(d), :],
                                            bank(2 + d)[:, 0:256].rearrange("p (a b) -> p a b", b=CH), ALU.add) \
                             .then_inc(sem["Xe"], 1)
                    for d in range(2):
                        v.wait_ge(sem["XT"], value("XT", j, 2 * lv + d - 1))
                        v.tensor_tensor(XT[:, group(d), :], XT[:, group(d), :],
                                        bank(4 + d)[:, 0:256].rearrange("p (a b) -> p a b", b=CH), ALU.add) \
                         .then_inc(sem["XTe"], 1)
                for pi in range(2):
                    v.wait_ge(sem["gq"], value("gq", j, pi + 1))
                    src = bank(pi).rearrange("p (g c b) -> p g c b", g=4, b=CH)
                    v.tensor_copy(G[:].rearrange("p (g c) b -> p c g b", c=2)[:, pi], src[:, :, 0, :])
                    if has_y(j):
                        v.tensor_tensor(QT[:].rearrange("p (g c) b -> p c g b", c=2)[:, pi], src[:, :, 1, :],
                                        AR[:, :, :, 1 + j % 2, pi * CH:(pi + 1) * CH].rearrange("p d h b -> p (d h) b"),
                                        ALU.add)
                v.drain().then_inc(sem["gqe"], 1)

                def add_y(src, pis):
                    for d in range(2):
                        c = tiles(j)[d].start + pis[d] * CH
                        y = mix[:, 0:2, c:c + CH]
                        v.tensor_tensor(y, y, src(d)[:, (4 + 2 * d) * CH:(6 + 2 * d) * CH]
                                        .rearrange("p (a b) -> p a b", b=CH), ALU.add)

                def decayed(step):
                    c = 48 + 8 * (j % 2)
                    w = sm[:, c + 2 * step:c + 8 - 2 * step]
                    n = 8 - 4 * step
                    wv = sm[:, c:c + 8].rearrange("p (d i h) -> p d i h", d=2, i=2)
                    for d in range(2):
                        v.tensor_tensor(SH[:, 2 * d:2 * d + 2, :], ST[:, 2 * d:2 * d + 2, :],
                                        wv[:, d, (step, 1 - step)[d], :].unsqueeze(2).to_broadcast([P, 2, CH]), ALU.mult)
                    v.drain()
                    for d in range(2):
                        pi = (step, 1 - step)[d]
                        v.tensor_tensor(SH[:, 2 * d:2 * d + 2, :], SH[:, 2 * d:2 * d + 2, :],
                                        bank(2 + pi)[:, 2 * d * CH:(2 * d + 2) * CH].rearrange("p (a b) -> p a b", b=CH),
                                        ALU.add)
                    v.drain()
                v.wait_ge(sem["hy"], value("hy", j, 2))
                for step in range(2):
                    decayed(step)
                    v.wait_ge(sem["chS"], value("chS", j, step + 1))
                    v.tensor_tensor(ST[:], SH[:], bank(4 + step)[:, 0:4 * CH].rearrange("p (a b) -> p a b", b=CH),
                                    ALU.add)
                    v.drain().then_inc(sem["che"], 1)
                if has_y(j):
                    for step in range(2):
                        add_y(lambda d: bank(2 + (step, 1 - step)[d]), (step, 1 - step))
                    v.drain()
                    for step in range(2):
                        add_y(lambda d: bank(4 + step), (step, 1 - step))
                v.drain().then_inc(S("rw_y_added"), 1)

            def units(d):
                for hp in range(2):
                    for e_ in range(2):
                        for pi in range(2):
                            yield hp, e_, pi, 4 * d + 2 * hp + e_, slice(64 * e_, 64 * e_ + 64), slice(64 * pi, 64 * pi + 64)

            def pe_batch(e, j):
                T = [order[d][j] for d in range(2)]
                Rk = 1 + j % 2
                for d in range(2):
                    e.wait_ge(sem["AR"], value("AR", j, d + 1))
                if l or j:
                    e.wait_ge(S("rw_y_added"), l * NBATCH + j)
                for i, (bk, made) in enumerate(((0, "Lb"), (2, "Lk"))):
                    for half in range(2):
                        for d in range(2):
                            for hp, e_, pi, dh, re, rp in units(d):
                                if e_ == half:
                                    a = (2 * d + hp) * 2 * CH
                                    ins = e.matmul(bank(bk + e_)[rp, a:a + 2 * CH], BK[re, d, hp, i, rp],
                                                   AR[re, d, hp, 0:Rk + 1:Rk, rp], start=True, stop=True)
                        ins.then_inc(sem[made], 1)
                for d in range(2):
                    e.wait_ge(sem["BK"], value("BK", j, d + 1))
                for i, made in enumerate(("tA", "tB", "tK")):
                    for d in range(2):
                        for hp in range(2):
                            src = AR[:, d, hp, 0, :] if i == 0 else BK[:, d, hp, 1 + i, :]
                            a = (2 * d + hp) * P
                            ins = e.transpose(bank(4 + i)[:, a:a + P], src, ident)
                    ins.then_inc(sem[made], 1)
                e.wait_ge(sem["ltbd"], value("ltbd", j, 1))
                e.wait_ge(sem["mb"], value("mb", j, 2))
                for d in range(2):
                    for h in range(4):
                        ins = e.matmul(bank(d)[:, h * CH:(h + 1) * CH], LTbd[:, 4 * d + h, :], ident2,
                                       start=True, stop=True)
                    ins.then_inc(sem["T"], 1)
                e.wait_ge(sem["mk"], value("mk", j, 2))
                for d in range(2):
                    for hp, e_, pi, dh, re, rp in units(d):
                        ins = e.matmul(bank(7)[rp, dh * CH:(dh + 1) * CH], MK[rp, dh, 0, :],
                                       vtok[rp, T[d], (2 * hp + e_) * CH:(2 * hp + e_ + 1) * CH], start=True, stop=True)
                ins.then_inc(sem["w1"], 1)
                e.wait_ge(sem["bh"], value("bh", j, 1))
                for lv in range(1, 6):
                    for d in range(2):
                        e.wait_ge(sem["Xe"], value("Xe", j, 2 * lv - 2 + d + 1))
                        for h in range(4):
                            ins = e.matmul(bank(d)[:, h * CH:(h + 1) * CH], LTbd[:, 4 * d + h, :], X[:, 4 * d + h, :],
                                           start=True, stop=True)
                        ins.then_inc(sem["T"], 1)
                    if lv < 5:
                        for d in range(2):
                            e.wait_ge(sem["Te"], value("Te", j, 2 * lv + d + 1))
                            e.wait_ge(sem["XTbd"], value("XTbd", j, 2 * lv - 2 + d + 1))
                            for h in range(4):
                                ins = e.matmul(bank(2 + d)[:, h * CH:(h + 1) * CH], XTbd[:, 4 * d + h, :],
                                               Tt[:, 4 * d + h, :], start=True, stop=True)
                            ins.then_inc(sem["X"], 1)
                    for d in range(2):
                        e.wait_ge(sem["Tbd"], value("Tbd", j, 2 * lv - 2 + d + 1))
                        e.wait_ge(sem["XTe"], value("XTe", j, 2 * lv - 2 + d + 1))
                        for h in range(4):
                            ins = e.matmul(bank(4 + d)[:, h * CH:(h + 1) * CH], Tbd[:, 4 * d + h, :],
                                           XT[:, 4 * d + h, :], start=True, stop=True)
                        ins.then_inc(sem["XT"], 1)
                e.wait_ge(sem["w1e"], value("w1e", j, 1))
                e.wait_ge(sem["kh"], value("kh", j, 1))
                for d in range(2):
                    e.wait_ge(sem["XTbd"], value("XTbd", j, 10 + d + 1))
                    for h in range(4):
                        ins = e.matmul(bank(6 + d)[:, 2 * h * CH:2 * (h + 1) * CH], XTbd[:, 4 * d + h, :],
                                       AW[:, 4 * d + h, :, :], start=True, stop=True)
                    ins.then_inc(sem["xa"], 1)
                e.wait_ge(sem["xae"], value("xae", j, 2))
                for half in range(2):
                    for d in range(2):
                        for hp, e_, pi, dh, re, rp in units(d):
                            if pi == half:
                                a = (2 * d + hp) * 2 * CH
                                ins = e.matmul(bank(pi)[re, a:a + 2 * CH], AW[rp, dh, 1, :], MB[rp, dh, 2:0:-1, :],
                                               start=True, stop=True)
                    ins.then_inc(sem["gq"], 1)
                for half in range(2):
                    for d in range(2):
                        for hp, e_, pi, dh, re, rp in units(d):
                            if pi == half:
                                a = (2 * d + hp) * CH
                                vv = vtok[rp, T[d], (2 * hp + e_) * CH:(2 * hp + e_ + 1) * CH]
                                acc = bank(2 + pi)[re, a:a + CH]
                                e.matmul(acc, MB[rp, dh, 2, :], AW[rp, dh, 0, :], start=True, stop=False)
                                ins = e.matmul(acc, MK[rp, dh, 0, :], vv, start=False, stop=True)
                                if has_y(j):
                                    acc = bank(2 + pi)[re, 4 * CH + a:5 * CH + a]
                                    e.matmul(acc, AW[rp, dh, 0, :], MB[rp, dh, 1, :], start=True, stop=False)
                                    ins = e.matmul(acc, vv, MK[rp, dh, 1, :], start=False, stop=True)
                    ins.then_inc(sem["hy"], 1)
                e.wait_ge(sem["gqe"], value("gqe", j, 1))
                for step in range(2):
                    if step or j or l:
                        e.wait_ge(sem["che"], value("che", j, step))
                    for d in range(2):
                        pi = step if d == 0 else 1 - step
                        for hp in range(2):
                            for e_ in range(2):
                                re = slice(64 * e_, 64 * e_ + 64)
                                a, g = (2 * d + hp) * CH, 4 * d + 2 * hp + pi
                                ins = e.matmul(bank(4 + step)[re, a:a + CH], G[re, g, :], ST[re, 2 * d + hp, :],
                                               start=True, stop=True)
                                if has_y(j):
                                    ins = e.matmul(bank(4 + step)[re, 4 * CH + a:5 * CH + a], ST[re, 2 * d + hp, :],
                                                   QT[re, g, :], start=True, stop=True)
                    ins.then_inc(sem["chS"], 1)

            def dve_scan(v):
                v.memset(ST[:], 0.0)
                v.drain()
                for j in range(NBATCH):
                    dve_batch(v, j)

            def act_scan(a):
                act_exps(a, 0)
                a.wait_ge(S("rw_zeroed"), l + 1)
                for j in range(NBATCH):
                    act_batch(a, j)

            def pool_scan(g):
                g.wait_ge(S("phase_end"), 3 * phase_of[f"rscan{l}"])
                for M in (LTbd, Tbd, XTbd):
                    g.memset(M[:], 0.0)
                g.drain().then_inc(S("rw_zeroed"), 1)
                for j in range(NBATCH):
                    pool_batch(g, j)
            phase_of[f"rscan{l}"] = len(phases)
            phase("rwkv chunks", pe=lambda e: [pe_batch(e, j) for j in range(NBATCH)], act=act_scan, dve=dve_scan,
                  pool=pool_scan)

            y = mix[:, 0:2, :]
            yc = arena2(f"yc{l}", [P, 2, TOK])
            ysq = arena2(f"ysq{l}", [P, 2, TOK], off=6 * K1)
            bon = arena2(f"bon{l}", [P, 2, TOK], off=12 * K1)
            rs = arena2(f"rs{l}", [P, 2, TOK], off=18 * K1)
            ro = Signal("readout_sums", 3)
            rd = Signal("readout_terms", 2)
            ra = Signal("readout_root", 2)
            segs = SEGS[n]

            def pe_read(e):
                for hp in range(2):
                    for s0, s1 in segs:
                        ins = e.matmul(PW[hp][:, s0:s1], headones, y[:, hp, s0:s1], start=True, stop=True)
                ins.then_inc(ro.sem, 1)
                e.wait_ge(rd.sem, rd.at(1))
                for hp in range(2):
                    for s0, s1 in segs:
                        ins = e.matmul(PW[2 + hp][:, s0:s1], headones, bon[:, hp, s0:s1], start=True, stop=True)
                ins.then_inc(ro.sem, 1)
                e.wait_ge(rd.sem, rd.at(2))
                for hp in range(2):
                    for s0, s1 in segs:
                        ins = e.matmul(PW[hp][:, s0:s1], headones, ysq[:, hp, s0:s1], start=True, stop=True)
                ins.then_inc(ro.sem, 1)

            def act_read(a):
                a.wait_ge(ro.sem, ro.at(3))
                for hp in range(2):
                    a.activation(rs[:, hp, 0:n], PW[hp][:, 0:n], ACT.Sqrt, scale=1.0 / CH, bias=epsc[:, 1:2]) \
                     .then_inc(ra.sem, 1)

            def dve_read(v):
                for hp in range(2):
                    v.tensor_tensor(bon[:, hp, 0:n], icl[:, 0, hp, 0:n], icl[:, 1, hp, 0:n], ALU.add)
                v.drain()
                for hp in range(2):
                    v.tensor_scalar(bon[:, hp, 0:n], bon[:, hp, 0:n], col("k_a", hp), scl_ka[:, 2 + hp:3 + hp],
                                    ALU.mult, ALU.add)
                v.drain()
                v.tensor_tensor(bon[:, :, 0:n], bon[:, :, 0:n], k[:, :, 0:n], ALU.mult)
                v.drain()
                for hp in range(2):
                    ins = v.scalar_tensor_tensor(out=bon[:, hp, 0:n], in0=r[:, hp, 0:n], scalar=col("r_k", hp),
                                                 in1=bon[:, hp, 0:n], op0=ALU.mult, op1=ALU.mult)
                ins.then_inc(rd.sem, 1)
                v.wait_ge(ro.sem, ro.at(1))
                for hp in range(2):
                    v.scalar_tensor_tensor(out=yc[:, hp, 0:n], in0=PW[hp][:, 0:n], scalar=-1.0 / CH,
                                           in1=y[:, hp, 0:n], op0=ALU.mult, op1=ALU.add)
                v.drain()
                v.tensor_tensor(ysq[:, :, 0:n], yc[:, :, 0:n], yc[:, :, 0:n], ALU.mult).then_inc(rd.sem, 1)
                v.wait_ge(ra.sem, ra.at(2))
                v.reciprocal(rs[:, :, 0:n], rs[:, :, 0:n])
                for hp in range(2):
                    v.tensor_tensor(bon[:, hp, 0:n], PW[2 + hp][:, 0:n], v_[:, hp, 0:n], ALU.mult)
                v.drain()
                for hp in range(2):
                    v.scalar_tensor_tensor(out=yc[:, hp, 0:n], in0=yc[:, hp, 0:n], scalar=col("ln_g", hp),
                                           in1=rs[:, hp, 0:n], op0=ALU.mult, op1=ALU.mult)
                v.drain()
                for hp in range(2):
                    v.scalar_tensor_tensor(out=yc[:, hp, 0:n], in0=yc[:, hp, 0:n], scalar=col("ln_b", hp),
                                           in1=bon[:, hp, 0:n], op0=ALU.add, op1=ALU.add)
                v.drain()
                v.tensor_tensor(y[:, :, 0:n], yc[:, :, 0:n], z[:, :, 0:n], ALU.mult)
            phase("rwkv readout", pe=pe_read, act=act_read, dve=dve_read)

        phase_of = {}
        before = []
        for l in range(DEPTH):
            full = l < DEPTH - 1
            n = TOK if full else SEQ
            v = lambda kind, l=l: (lambda b, s: scl[:, 3 * l + kind, 2 * b + s:2 * b + s + 1])
            conv_mixer(l, full, before + [pre_norm(f"{l}", TOK, v(0), v(1), before[0]["xnew"] if before else None)])
            attention(l, full)
            rwkv(l, full)
            m = arena(f"m{l}", [P, NB, TOK], off=24 * K1)
            stream_phase(plain(f"wout{l}", t["w_out"][l], 0, 8, n, (hhi, hlo), to(m)), before=[split_mix(n)])
            before = [post_norm(f"{l}", m, n, v(2))]

        zero_shift = epsc[:, 2:3]
        b2 = lambda name, base=0: (lambda b, s: VC[:, 2, B2ROW[name] + base + b:B2ROW[name] + base + b + 1])
        noshift = lambda b, s: zero_shift
        LR = SEQ + 127
        revd = nc.dram_tensor("rel_bias_reversed", (8, P, LR), F32, kind="Internal").ap()

        def attn2(part, before=()):
            w = t["attn_w_in_2"][0]
            nm = "AB"[part]
            q = arena(f"q2{nm}", [P, 4, SEQ])
            k = arena(f"k2{nm}", [P, 4, SEQ], off=8 * K1)
            vch = arena(f"vc2{nm}", [P, 4, SEQ], off=16 * K1)
            AT = arena(f"AT2{nm}", [P, 4, SEQ], off=16 * K1)
            vtok = arena(f"vt2{nm}", [P, 4, SEQ], off=24 * K1)
            W = arena(f"wk2{nm}", [P, 4, SEQ], off=32 * K1)
            bias = arena(f"bias2{nm}", [P, 8, SEQ], off=40 * K1)
            rb = arena(f"rb2{nm}", [8, 513], off=56 * K1)
            rev = arena(f"rev2{nm}", [8, LR + 1], off=59 * K1)
            c0 = 1536 * part
            qs = plain(f"q2{nm}", w, c0, 4, SEQ, (hhi, hlo), to(q))
            ks = plain(f"k2{nm}", w, c0 + 512, 4, SEQ, (hhi, hlo), to(k))
            vs = plain(f"v2{nm}", w, c0 + 1024, 4, SEQ, (hhi, hlo), to(vch))

            vtu, vts = Signal("v2_turned", 4), Signal("v2_tokens", 4)

            def pe_v(e):
                e.wait_ge(S("evac_done0"), (vs["o0"] + 4) // 2)
                e.wait_ge(S("evac_done1"), (vs["o0"] + 4) // 2)
                for T in range(4):
                    if T >= 2:
                        e.wait_ge(vts.sem, vts.at(T - 1))
                    for h in range(4):
                        ins = e.transpose(bank(4 + T % 2)[:, h * P:(h + 1) * P], vch[:, h, T * P:(T + 1) * P], ident)
                    ins.then_inc(vtu.sem, 1)

            def act_v(a):
                for T in range(4):
                    a.wait_ge(vtu.sem, vtu.at(T + 1))
                    a.activation(vtok[:, T, :], bank(4 + T % 2), ACT.Copy).then_inc(vts.sem, 1)

            if part == 0:
                def pool_bias(pool):
                    pool.wait_ge(S("phase_end"), 3 * phase_of["bias"])
                    pool.wait_ge(*before[-1]["ready"](NB - 1))
                    pool.dma_start(rb[:, :], t["attn_rel_bias_2"][0]).then_inc(S("rel_bias"), 16)
                    pool.wait_ge(S("rel_bias"), 16)
                    pool.tensor_copy(rev[:, 255:LR], rb[:, 512:512 - (LR - 255):-1])
                    pool.tensor_copy(rev[:, 0:255], rb[:, 512:513].to_broadcast([8, 255]))
                    pool.drain()
                    pool.dma_start(revd, rev[:, 0:LR].unsqueeze(1).to_broadcast([8, P, LR])).then_inc(S("rev_stored"), 16)
                    pool.wait_ge(S("rev_stored"), 16)
                    src = bass.AP(revd.tensor, revd.offset + P - 1, [[LR - 1, P], [P * LR, 8], [1, SEQ]])
                    pool.dma_start(bias[:, :, :], src).then_inc(S("bias_tile"), 16)
                    pool.wait_ge(S("bias_tile"), 16)
                    pool.memset(bias[0:64, :, 448:512], -1e30).then_inc(S("bias_ready"), 1)

                phase_of["bias"] = len(phases)
            stream_phase(qs, ks, vs, before=before, pe=pe_v, act=act_v)
            if part == 0:
                phases[-1]["pool"] = pool_bias

            steps = [(h, qt) for h in range(8) for qt in range(4)]
            sg = {n_: S(f"a2{n_}{nm}") for n_ in ("score", "read", "soft", "exps", "prob", "turn", "AT", "pv", "out", "l")}
            scale = 64 ** -0.5
            st = sm[:, 16:32]

            def rows(h):
                return slice(64 * (h % 2), 64 * (h % 2) + 64)

            def pe_score(e, i):
                h, qt = steps[i]
                if i >= 2:
                    e.wait_ge(sg["read"], i - 1)
                e.matmul(bank(i % 2)[:, 0:(qt + 1) * P], q[rows(h), h // 2, qt * P:(qt + 1) * P],
                         k[rows(h), h // 2, 0:(qt + 1) * P], start=True, stop=True).then_inc(sg["score"], 1)

            def pe_main(e):
                pe_score(e, 0)
                for i, (h, qt) in enumerate(steps):
                    if i + 1 < len(steps):
                        pe_score(e, i + 1)
                    e.wait_ge(sg["prob"], i + 1)
                    if i >= 2:
                        e.wait_ge(sg["AT"], i - 1)
                    for kt in range(qt + 1):
                        ins = e.transpose(bank(2 + i % 2)[:, kt * P:(kt + 1) * P],
                                          W[:, i % 2, kt * P:(kt + 1) * P], ident)
                    ins.then_inc(sg["turn"], 1)
                    if qt == 3:
                        e.wait_ge(sg["AT"], i + 1)
                        if h >= 4 and h % 2 == 0:
                            e.wait_ge(sg["out"], h // 2 - 1)
                        o = bank(4 + (h // 2) % 2)
                        for kt in range(4):
                            ins = e.matmul(o[rows(h), kt * P:SEQ], vtok[:, kt, 64 * h:64 * h + 64],
                                           AT[:, kt, kt * P:SEQ], start=kt == 0, stop=kt == 3)
                        ins.then_inc(sg["pv"], 1)

            def act_at(a, i):
                h, qt = steps[i]
                a.wait_ge(sg["turn"], i + 1)
                if qt == 0 and h:
                    a.wait_ge(sg["pv"], h)
                a.activation(AT[:, 0:qt + 1, qt * P:(qt + 1) * P],
                             bank(2 + i % 2)[:, 0:(qt + 1) * P].rearrange("p (a b) -> p a b", b=P), ACT.Copy) \
                 .then_inc(sg["AT"], 1)
                if qt == 3 and h % 2 == 1:
                    a.wait_ge(sg["pv"], h + 1)
                    a.activation(mix[:, 4 * part + h // 2, 0:SEQ], bank(4 + (h // 2) % 2), ACT.Copy) \
                     .then_inc(sg["out"], 1)

            if part == 0:
                def act_main(a):
                    for i, (h, qt) in enumerate(steps):
                        N = (qt + 1) * P
                        a.wait_ge(sg["soft"], i + 1)
                        a.activation(W[:, i % 2, 0:N], W[:, i % 2, 0:N], ACT.Exp, bias=st[:, 2 + i % 2:3 + i % 2],
                                     accum_out=st[:, 4 + i % 2:5 + i % 2]).then_inc(sg["exps"], 1)
                        if i:
                            act_at(a, i - 1)
                    act_at(a, len(steps) - 1)

                def dve_main(v):
                    def logits(i):
                        h, qt = steps[i]
                        N = (qt + 1) * P
                        v.wait_ge(sg["score"], i + 1)
                        if i >= 2:
                            v.wait_ge(sg["turn"], i - 1)
                        v.scalar_tensor_tensor(out=W[:, i % 2, 0:N], in0=bank(i % 2)[:, 0:N], scalar=scale,
                                               in1=bias[:, h, SEQ - N:SEQ], op0=ALU.mult, op1=ALU.add) \
                         .then_inc(sg["read"], 1)
                        v.drain()
                        v.reduce_max(st[:, i % 2:i % 2 + 1], W[:, i % 2, 0:N], AXX)
                        v.drain()
                        v.tensor_scalar(st[:, 2 + i % 2:3 + i % 2], st[:, i % 2:i % 2 + 1], -1.0, None, ALU.mult) \
                         .then_inc(sg["soft"], 1)
                    v.wait_ge(S("bias_ready"), 1)
                    logits(0)
                    for i, (h, qt) in enumerate(steps):
                        N = (qt + 1) * P
                        if i + 1 < len(steps):
                            logits(i + 1)
                        v.wait_ge(sg["exps"], i + 1)
                        v.reciprocal(st[:, 6 + i % 2:7 + i % 2], st[:, 4 + i % 2:5 + i % 2])
                        v.drain()
                        v.tensor_scalar(W[:, i % 2, 0:N], W[:, i % 2, 0:N], st[:, 6 + i % 2:7 + i % 2], None, ALU.mult) \
                         .then_inc(sg["prob"], 1)
            else:
                L = arena(f"l2{nm}", [P, 2, SEQ], off=40 * K1)
                NEG = arena(f"n2{nm}", [P, 2, SEQ], off=44 * K1)
                CS = arena(f"c2{nm}", [P, 2, SEQ], off=48 * K1)
                Zs = arena(f"z2{nm}", [P, 2, SEQ], off=52 * K1)

                def act_main(a):
                    a.preload_act_table_set("natural_log_exp_and_others")

                    def soft(i):
                        h, qt = steps[i]
                        N = (qt + 1) * P
                        a.wait_ge(sg["read"], i + 1)
                        if i >= 2:
                            a.wait_ge(sg["soft"], i - 1)
                        a.activation(L[:, i % 2, 0:N], Zs[:, i % 2, 0:N], ACT.Abs)
                        a.drain()
                        a.activation(L[:, i % 2, 0:N], L[:, i % 2, 0:N], ACT.Exp, scale=-1.0)
                        a.drain()
                        a.activation(L[:, i % 2, 0:N], L[:, i % 2, 0:N], ACT.Ln, bias=1.0).then_inc(sg["l"], 1)
                    soft(0)
                    for i, (h, qt) in enumerate(steps):
                        N = (qt + 1) * P
                        if i:
                            act_at(a, i - 1)
                        if i + 1 < len(steps):
                            soft(i + 1)
                        a.wait_ge(sg["soft"], i + 1)
                        if i >= 2:
                            a.wait_ge(sg["turn"], i - 1)
                        a.activation(W[:, i % 2, 0:N], CS[:, i % 2, 0:N], ACT.Exp).then_inc(sg["exps"], 1)
                    act_at(a, len(steps) - 1)

                def dve_main(v):
                    def zs(i):
                        h, qt = steps[i]
                        N = (qt + 1) * P
                        v.wait_ge(sg["score"], i + 1)
                        if i >= 2:
                            v.wait_ge(sg["l"], i - 1)
                        v.tensor_scalar(Zs[:, i % 2, 0:N], bank(i % 2)[:, 0:N], scale, None, ALU.mult) \
                         .then_inc(sg["read"], 1)
                        v.drain()
                        v.tensor_scalar(NEG[:, i % 2, 0:N], Zs[:, i % 2, 0:N], -1.0, 0.0, ALU.mult, ALU.min)
                        v.drain()
                        v.tensor_tensor(NEG[:, i % 2, N - P:N], NEG[:, i % 2, N - P:N], cc("strict"), ALU.mult)
                    zs(0)
                    for i, (h, qt) in enumerate(steps):
                        N = (qt + 1) * P
                        if i + 1 < len(steps):
                            zs(i + 1)
                        v.wait_ge(sg["l"], i + 1)
                        v.tensor_tensor(L[:, i % 2, N - P:N], L[:, i % 2, N - P:N], cc("strict"), ALU.mult)
                        v.drain()
                        v.tensor_tensor_scan(CS[:, i % 2, N - 1::-1] if N == SEQ or True else None,
                                             NEG[:, i % 2, N - 1::-1], L[:, i % 2, N - 1::-1], 0.0,
                                             ALU.add, ALU.subtract)
                        v.drain()
                        v.tensor_tensor(CS[:, i % 2, 0:N], CS[:, i % 2, 0:N], Zs[:, i % 2, 0:N], ALU.add) \
                         .then_inc(sg["soft"], 1)
                        v.wait_ge(sg["exps"], i + 1)
                        v.tensor_tensor(W[:, i % 2, N - P:N], W[:, i % 2, N - P:N], cc("strict"), ALU.mult) \
                         .then_inc(sg["prob"], 1)
            phase("attention 2" + nm, pe=pe_main, act=act_main, dve=dve_main)

        def ffn(l, post):
            fhi = place(f"fhi{l}", [P, FB, SEQ], F32R, at=at_mix)
            flo = place(f"flo{l}", [P, FB, SEQ], F32R, at=at_mix + FB * SEQ * 4)
            assert at_mix + 2 * FB * SEQ * 4 <= nc.sbuf_usable_end
            gb = place(f"gb{l}", [P, 2, SEQ], at=at_mix + 2 * FB * SEQ * 4)
            wg, wu, wd = (kview(t[n_][l]) for n_ in ("ffn_w_gate_2", "ffn_w_up_2", "ffn_w_down_2"))

            def ev_gate(eng, i, o, acc):
                eng.wait_ge(S("evac_done1"), i + evac_base(st_gu))
                return eng.activation(gb[:, 0, :], acc, ACT.Silu)

            def evac_base(st):
                return st["o0"] // 2

            def ev_up(eng, i, o, acc):
                eng.wait_ge(S("evac_done0"), i + (evac_base(st_gu) + 1))
                eng.tensor_tensor(gb[:, 1, :], gb[:, 0, :], acc, ALU.mult)
                eng.drain()
                hi = fhi[:, bass.ds(i, 1), :].rearrange("p a n -> p (a n)")
                eng.tensor_copy(hi, gb[:, 1, :])
                eng.drain()
                lo = flo[:, bass.ds(i, 1), :].rearrange("p a n -> p (a n)")
                return eng.tensor_tensor(lo, gb[:, 1, :], hi.bitcast(F32), ALU.subtract)
            body = [(wg, 0, 8, 0, P, 0, True, True), (wu, 0, 8, 0, P, 1, True, True)]
            st_gu = add_stage(f"gateup{l}", body, FB, SEQ, (hhi, hlo), [("act", ev_gate), ("dve", ev_up)])
            stream_phase(st_gu, before=[post, pre_norm(f"ffn{l}", SEQ, b2("ffn_pre", 8 * l), noshift, post["xnew"])])
            m = arena2(f"mf{l}", [P, NB, SEQ])
            body = []
            for o in range(2):
                for k0, kb in ((0, 8), (8, 8), (16, 6)):
                    body.append((wd, k0, kb, o * P, 2 * P, o, k0 == 0, k0 == 16))
            stream_phase(add_stage(f"down{l}", body, NB // 2, SEQ, (fhi, flo), [("act", to(m))] * 2))
            return post_norm(f"ffn{l}", m, SEQ, b2("ffn_post", 8 * l))

        def recurrent(before):
            w = t["rg_w_in_2"][0]
            gate = arena("rggate", [P, NB, SEQ])
            xr = arena("rgx", [P, NB, SEQ], off=16 * K1)
            xc = arena("rgxc", [P, NB, SEQ], off=32 * K1)
            gs = plain("rggate", w, 0, 8, SEQ, (hhi, hlo), to(gate, ACT.Gelu_apprx_tanh))
            xs = plain("rgxr", w, 1024, 8, SEQ, (hhi, hlo), to(xr))
            stream_phase(gs, xs, before=before)
            wa = arena2("rgwa", [P, 8, 256])
            wi = arena2("rgwi", [P, 8, 256], off=8 * K1)
            WK = arena2("rgwork", [P, 2, 6, SEQ], off=16 * K1)
            col = lambda name, i: VC[:, 2, B2ROW[name] + i:B2ROW[name] + i + 1]

            def pool_w(pool):
                pool.wait_ge(S("phase_end"), 3 * phase_of["rg"])
                pool.dma_start(wa[:], t["rg_w_a_2"][0].rearrange("n (k p) j -> p (n k) j", p=P)).then_inc(S("rg_w"), 16)
                pool.dma_start(wi[:], t["rg_w_i_2"][0].rearrange("n (k p) j -> p (n k) j", p=P)).then_inc(S("rg_w"), 16)
            xcr, gm, ga, rd, rs = S("rg_xc"), S("rg_mm"), S("rg_act"), S("rg_dve"), S("rg_sqrt")

            def dve_conv(v):
                for b in range(NB):
                    v.tensor_scalar(xc[:, b, :], xr[:, b, :], col("rg_conv_w", 24 + b), col("rg_conv_b", b),
                                    ALU.mult, ALU.add)
                v.drain()
                for j in range(3):
                    sh = 3 - j
                    for b in range(NB):
                        v.scalar_tensor_tensor(out=xc[:, b, sh:SEQ], in0=xr[:, b, 0:SEQ - sh],
                                               scalar=col("rg_conv_w", 8 * j + b), in1=xc[:, b, sh:SEQ],
                                               op0=ALU.mult, op1=ALU.add)
                    v.drain()
                v.drain().then_inc(xcr, 1)
                for b in range(NB):
                    wk = WK[:, b % 2]
                    A, TH, U, MU, I = (wk[:, i, :] for i in range(5))
                    v.wait_ge(ga, b + 1)
                    v.tensor_scalar(MU, TH, 1.0, None, ALU.add)
                    v.drain()
                    v.reciprocal(MU, MU)
                    v.drain()
                    v.scalar_tensor_tensor(out=MU, in0=TH, scalar=2.0, in1=MU, op0=ALU.mult, op1=ALU.mult) \
                     .then_inc(rd, 1)
                    v.tensor_tensor(U, I, xc[:, b, :], ALU.mult)
                    v.drain()
                    v.wait_ge(rs, b + 1)
                    v.tensor_tensor(U, U, MU, ALU.mult)
                    v.drain()
                    v.tensor_tensor_scan(TH, A, U, 0.0, ALU.mult, ALU.add)
                    v.drain()
                    v.tensor_tensor(mix[:, b, 0:SEQ], TH, gate[:, b, :], ALU.mult).then_inc(rd, 1)

            def pe_g(e):
                e.wait_ge(S("rg_w"), 32)
                e.wait_ge(xcr, 1)
                for b in range(NB):
                    n_, ob = b // 2, b % 2
                    if b >= 2:
                        e.wait_ge(ga, b - 1)
                    for i, W_ in enumerate((wa, wi)):
                        for k_ in range(2):
                            ins = e.matmul(bank(2 * (b % 2) + i), W_[:, 2 * n_ + k_, ob * P:(ob + 1) * P],
                                           xc[:, 2 * n_ + k_, :], start=k_ == 0, stop=k_ == 1)
                    ins.then_inc(gm, 1)

            def act_g(a):
                def root(b):
                    wk = WK[:, b % 2]
                    a.wait_ge(rd, 2 * b + 1)
                    a.activation(wk[:, 3, :], wk[:, 3, :], ACT.Sqrt).then_inc(rs, 1)
                for b in range(NB):
                    wk = WK[:, b % 2]
                    A, TH, U, MU, I, Rr = (wk[:, i, :] for i in range(6))
                    a.wait_ge(gm, b + 1)
                    if b >= 2:
                        a.wait_ge(rd, 2 * (b - 1))
                    a.activation(Rr, bank(2 * (b % 2)), ACT.Sigmoid, bias=col("b_a", b))
                    a.activation(I, bank(2 * (b % 2) + 1), ACT.Sigmoid, bias=col("b_i", b))
                    a.drain()
                    a.activation(A, Rr, ACT.Exp, scale=scl[:, 6, 8 + b:9 + b])
                    a.activation(TH, Rr, ACT.Tanh, scale=scl[:, 6, b:b + 1]).then_inc(ga, 1)
                    if b:
                        root(b - 1)
                root(NB - 1)
            phase_of["rg"] = len(phases)
            phase("rg gates", pool=pool_w, pe=pe_g, act=act_g, dve=dve_conv)

        attn2(0, before + [pre_norm("mix0", SEQ, b2("mix_pre"), noshift, before[0]["xnew"])])
        attn2(1)
        m0 = arena("mo0", [P, NB, SEQ])
        stream_phase(plain("wout2", t["attn_w_out_2"][0], 0, 8, SEQ, (hhi, hlo), to(m0)), before=[split_mix(SEQ)])
        last = ffn(0, post_norm("mix0", m0, SEQ, b2("mix_post")))
        recurrent([last, pre_norm("mix1", SEQ, b2("mix_pre", 8), noshift, last["xnew"])])
        m1 = arena("mo1", [P, NB, SEQ])
        stream_phase(plain("wout3", t["rg_w_out_2"][0], 0, 8, SEQ, (hhi, hlo), to(m1)), before=[split_mix(SEQ)])
        last = ffn(1, post_norm("mix1", m1, SEQ, b2("mix_post", 8)))
        phase("last norm", **{e: last[e] for e in ("pe", "act", "dve")})

        otok = arena("otok", [P, 4, D])

        def pe_out(e):
            for T in range(4):
                if T >= 2:
                    e.wait_ge(S("out_rows"), T - 1)
                for b in range(NB):
                    ins = e.transpose(PW[T % 2][:, b * P:(b + 1) * P], xT[:, b, T * P:(T + 1) * P], ident)
                ins.then_inc(S("out_turned"), 1)

        def dve_out(v):
            for T in range(4):
                v.wait_ge(S("out_turned"), T + 1)
                v.tensor_copy(otok[:, T, :], PW[T % 2][:, :]).then_inc(S("out_rows"), 1)

        def sp_out(sp):
            for T in range(4):
                sp.wait_ge(S("out_rows"), T + 1)
                sp.dma_start(out[0, T * P:(T + 1) * P, :], otok[:, T, :]).then_inc(S("out_stored"), 16)
            sp.wait_ge(S("out_stored"), 64)
        phase("output", sp=sp_out, pe=pe_out, dve=dve_out)

        def run(eng, which):
            for i, ph in enumerate(phases):
                if which in ph:
                    ph[which](eng)
                eng.drain().then_inc(S("phase_end"), 1)
                eng.wait_ge(S("phase_end"), 3 * (i + 1))

        block = ctx.enter_context(nc.Block())

        @block.sync
        def _(sp):
            for ph in phases:
                if "sp" in ph:
                    ph["sp"](sp)

        @block.gpsimd
        def _(pool):
            for ph in phases:
                if "pool" in ph:
                    ph["pool"](pool)

        @block.tensor
        def _(pe):
            run(pe, "pe")

        @block.scalar
        def _(act):
            run(act, "act")

        @block.vector
        def _(dve):
            run(dve, "dve")


_INS = ["x", "c", "ctx", "c_ctx", "mod_w", "mod_b", "norm_pre_g", "norm_post_g", "w_in", "w_out", "rwkv_w0",
        "rwkv_w_up", "rwkv_a0", "rwkv_a_up", "rwkv_k_k", "rwkv_k_a", "rwkv_r_k", "rwkv_ln_g", "rwkv_ln_b", "conv_w",
        "diff_lambda", "diff_subln_g", "attn_w_in_2", "attn_rel_bias_2", "attn_w_out_2", "rg_w_in_2", "rg_conv_w_2",
        "rg_conv_b_2", "rg_w_a_2", "rg_b_a_2", "rg_w_i_2", "rg_b_i_2", "rg_lambda_2", "rg_w_out_2", "norm_mix_pre_2",
        "norm_mix_post_2", "norm_ffn_pre_2", "norm_ffn_post_2", "ffn_w_gate_2", "ffn_w_up_2", "ffn_w_down_2"]


def kernel(**inputs):
    from concourse import bacc as _bacc
    from concourse.bass_utils import run_bass_kernel_spmd as _run

    nc = _bacc.Bacc("TRN2", target_bir_lowering=False, num_devices=1)
    arrays, t = {}, {}
    for name in _INS:
        a = np.ascontiguousarray(inputs[name])
        arrays[f"in_{name}"] = a
        t[name] = nc.dram_tensor(f"in_{name}", a.shape, mybir.dt.from_np(a.dtype), kind="ExternalInput").ap()
    _, table = constant_columns()
    arrays["shape_constants"] = table
    t["const"] = nc.dram_tensor("shape_constants", table.shape, F32, kind="ExternalInput").ap()
    out = nc.dram_tensor("out_0", (1, SEQ, D), F32, kind="ExternalOutput").ap()
    build_program(nc, t, out)
    r = _run(nc, [arrays], core_ids=[0])
    return r.results[0]["out_0"]
```

```python
import math
from contextlib import ExitStack

import numpy as np

import concourse.bass as bass
from concourse import mybir

ALU = mybir.AluOpType
ACT = mybir.ActivationFunctionType
AXX = mybir.AxisListType.X
F32 = mybir.dt.float32
F32R = mybir.dt.float32r

P = 128
D = 1024
NB = D // P
SEQ, CTX = 512, 256
TOK = SEQ + CTX
NT = TOK // P
DEPTH = 2
CH = 64
DFF = 2816
FB = DFF // P
GRID_W = 64
EPS = 1e-6
GN_EPS = 64e-5
C_R, C_K, C_V, C_LORA, C_Z = 0, 256, 512, 768, 1024
C_CONV = 1280
C_AQ, C_AK, C_AV, C_AZ = 2304, 2816, 3328, 3840

LAYER_VECS = [("mod_b", 24), ("pre_g", 8), ("post_g", 8), ("w0", 4), ("a0", 4), ("k_k", 2), ("k_a", 2),
              ("r_k", 2), ("ln_g", 2), ("ln_b", 2), ("conv_w", 6), ("subln", 1)]
BLOCK2_VECS = [("rg_conv_w", 32), ("rg_conv_b", 8), ("b_a", 8), ("b_i", 8), ("lam", 8),
               ("mix_pre", 16), ("mix_post", 16), ("ffn_pre", 16), ("ffn_post", 16)]


def row_table(vecs, start=0):
    at, out = start, {}
    for name, n in vecs:
        out[name] = at
        at += n
    return out, at


LROW, LROWS = row_table(LAYER_VECS)
B2ROW, B2ROWS = row_table(BLOCK2_VECS)


def constant_columns():
    cols, parts = {}, []

    def put(name, a):
        cols[name] = (sum(p.shape[1] for p in parts), a.shape[1])
        parts.append(a.astype(np.float32))

    p = np.arange(P)
    put("ident", np.eye(P))
    put("headones", (p[:, None] // CH == p[None, :] // CH))
    put("ones", np.ones((P, P)))
    t = p % CH
    s = np.arange(CH)
    put("ident2", t[:, None] == s[None, :])
    for d in range(2):
        before = t[:, None] < s[None, :] if d == 0 else t[:, None] > s[None, :]
        put(f"seen{d}", np.concatenate([before, before | (t[:, None] == s[None, :])], 1))
    lev = []
    for j in range(6):
        for d in range(2):
            r, c = t[:, None] >> j, s[None, :] >> j
            same = (r >> 1) == (c >> 1)
            lev.append(same & ((r & 1) == 1) & ((c & 1) == 0) if d == 0 else same & ((r & 1) == 0) & ((c & 1) == 1))
    put("level", np.concatenate(lev, 1))
    put("reset", np.tile((np.arange(TOK) % CH != 0), (P, 1)))
    inv = 10000.0 ** (-np.arange(0, 32, 2, dtype=np.float32) / np.float32(32))
    tok = np.arange(SEQ)
    ch = p % 64
    pos = np.where(ch[:, None] < 32, tok[None, :] // GRID_W, tok[None, :] % GRID_W).astype(np.float32)
    ang = pos * inv[ch % 16].astype(np.float32)[:, None]
    put("cos", np.cos(ang))
    put("sin", np.where((ch % 32)[:, None] < 16, -1.0, 1.0) * np.sin(ang))
    put("strict", p[None, :] < p[:, None])
    return cols, np.concatenate(parts, 1)


CONST_AT, _CONST = constant_columns()
NCONST = _CONST.shape[1]


def build_program(nc, t, out):
    with ExitStack() as ctx:
        base = (nc.sbuf_base + 63) // 64 * 64
        here = [base]

        def place(name, shape, dt=F32, at=None):
            size = int(np.prod(shape[1:])) * 4
            off = here[0] if at is None else at
            if at is None:
                here[0] += (size + 63) // 64 * 64
            return nc.alloc_sbuf_tensor_at(name, [int(x) for x in shape], dt, offset=off)

        xT = place("xT", [P, NB, TOK])
        at_h = here[0]
        hhi = place("hhi", [P, NB, TOK], F32R)
        hlo = place("hlo", [P, NB, TOK], F32R)
        wraw = place("wraw", [P, 2, 8, P])
        at_whi1 = here[0] + 8 * P * 4
        whi = place("whi", [P, 2, 8, P], F32R)
        at_wlo1 = here[0] + 8 * P * 4
        wlo = place("wlo", [P, 2, 8, P], F32R)
        const = place("const", [P, NCONST])
        VC = place("VC", [P, 3, P])
        modT = place("modT", [P, 2, 24, 2])
        cs = place("cs", [P, NB, 2])
        scl = place("scl", [P, 8, 16])
        sm = place("sm", [P, 64])
        epsc = place("epsc", [P, 3])
        ltmp = place("ltmp", [P, 8, 8])
        at_mix = here[0]
        mix = place("mix", [P, NB, TOK])
        at_a = here[0]
        arena_size = nc.sbuf_usable_end - at_a

        def arena(name, shape, dt=F32, off=0):
            size = int(np.prod(shape[1:])) * 4
            assert off + size <= arena_size, (name, off + size, arena_size)
            return place(name, shape, dt, at=at_a + off)

        def arena2(name, shape, dt=F32, off=0):
            size = int(np.prod(shape[1:])) * 4
            assert off + size <= 2 * NB * TOK * 4, (name, off + size)
            return place(name, shape, dt, at=at_h + off)

        K1 = 1024

        def kview(w):
            return w.rearrange("(k p) n -> p k n", p=P)

        def cc(name):
            a, n = CONST_AT[name]
            return const[:, a:a + n]

        ident, headones, ones, ident2 = cc("ident"), cc("headones"), cc("ones"), cc("ident2")
        PW = [ctx.enter_context(nc.psum_tensor(f"PW{i}", [P, 1024], F32)) for i in range(4)]

        def bank(i):
            return PW[i // 2][:, (i % 2) * 512:(i % 2) * 512 + 512]

        sems = {}

        def S(name):
            if name not in sems:
                sems[name] = ctx.enter_context(nc.semaphore(name))
            return sems[name]

        totals = {}

        class Signal:
            def __init__(self, name, total):
                self.sem, self.base = S(name), totals.get(name, 0)
                totals[name] = self.base + total

            def at(self, n):
                return self.base + n

        SEGS = {TOK: [(0, 512), (512, TOK)], SEQ: [(0, 512)]}
        stages = []

        def add_stage(name, body, iters, ntok, rhs, outs):
            st = dict(name=name, body=body, iters=iters, ntok=ntok, rhs=rhs, outs=outs, U=len(body), no=len(outs))
            if stages:
                l = stages[-1]
                st["g0"], st["o0"] = l["g0"] + l["U"] * l["iters"], l["o0"] + l["no"] * l["iters"]
                l["next"] = body[0]
            else:
                st["g0"], st["o0"] = 0, 0
            st["next"] = None
            assert st["U"] % 2 == 0 and st["no"] % 2 == 0
            stages.append(st)
            return st

        def plain(name, w, col, nblk, ntok, rhs, evac):
            v = kview(w)
            body = [(v, 0, 8, col + P * j, 2 * P, j, True, True) for j in range(2)]
            return add_stage(name, body, nblk // 2, ntok, rhs, [("act", evac)] * 2)

        def turns(st):
            n, lo = st["iters"], 1 if st["g0"] == 0 or "ready" in st else 0
            return lo, n - 1

        def run_turns(eng, st, do):
            lo, hi = turns(st)
            if lo == 1 and st["iters"] > 1:
                do(0, False)
            if hi - lo >= 2:
                with eng.Fori(lo, hi) as i:
                    do(i, False)
            else:
                for i in range(lo, hi):
                    do(i, False)
            do(st["iters"] - 1, True)

        def wait_pos(eng, sem, value):
            if not isinstance(value, int) or value > 0:
                eng.wait_ge(sem, value)

        def sp_stage(sp, st):
            def do(i, last):
                for u, (v, k0, kb, c0, cstep, o, first, fin) in enumerate(st["body"]):
                    g = i * st["U"] + (st["g0"] + u)
                    wait_pos(sp, S("w_split"), g - 1)
                    sp.dma_start(wraw[:, u % 2, 0:kb, :], v[:, k0:k0 + kb, bass.ds(i * cstep + c0, P)]) \
                        .then_inc(S(f"w_landed{u % 2}"), 16)
            run_turns(sp, st, do)

        def hi_part(act, i, st, u, desc):
            g = i * st["U"] + (st["g0"] + u)
            slot = u % 2
            act.wait_ge(S(f"w_landed{slot}"), (i * (st["U"] // 2) + (st["g0"] // 2 + u // 2)) * 16 + 16)
            wait_pos(act, S("w_used"), g - 1)
            kb = desc[2]
            act.activation(whi[:, slot, 0:kb, :], wraw[:, slot, 0:kb, :], ACT.Copy).then_inc(S("w_hi"), 1)

        def lo_part(dve, i, st, u, desc):
            g = i * st["U"] + (st["g0"] + u)
            slot = u % 2
            dve.wait_ge(S("w_hi"), g + 1)
            kb = desc[2]
            dve.tensor_tensor(wlo[:, slot, 0:kb, :], wraw[:, slot, 0:kb, :], whi[:, slot, 0:kb, :].bitcast(F32),
                              ALU.subtract).then_inc(S("w_split"), 1)

        def split_and_evac(eng, which, part, st):
            def do(i, last):
                for u, desc in enumerate(st["body"]):
                    nxt = st["body"][(u + 1) % st["U"]]
                    if u == st["U"] - 1 and last:
                        nxt = st["next"]
                    if nxt is not None:
                        part(eng, i, st, u + 1, nxt)
                    if "beside" in st and which in st["beside"]:
                        st["beside"][which](eng, i * st["U"] + u)
                    o = desc[5]
                    if desc[7] and st["outs"][o][0] == which:
                        eng.wait_ge(S("w_used"), i * st["U"] + (st["g0"] + u + 1))
                        st["outs"][o][1](eng, i, o, PW[o % 2][:, 0:st["ntok"]]) \
                            .then_inc(S(f"evac_done{o % 2}"), 1)
                    if desc[7] and which == "dve" and "after" in st:
                        st["after"](eng, i, o)
            run_turns(eng, st, do)

        def pe_stage(pe, st):
            def do(i, last):
                for u, (v, k0, kb, c0, cstep, o, first, fin) in enumerate(st["body"]):
                    g = i * st["U"] + (st["g0"] + u)
                    pe.wait_ge(S("w_split"), g + 1)
                    if first:
                        wait_pos(pe, S(f"evac_done{o % 2}"), i * (st["no"] // 2) + (st["o0"] // 2 + o // 2))
                    rhi, rlo = st["rhs"]
                    for s0, s1 in SEGS[st["ntok"]]:
                        acc = PW[o % 2][:, s0:s1]
                        for k in range(kb):
                            if "ready" in st and isinstance(i, int) and i == 0 and u == 0 and s0 == 0:
                                pe.wait_ge(*st["ready"](k))
                            a, b = first and k == 0, fin and k == kb - 1
                            pe.matmul(acc, whi[:, u % 2, k, :], rhi[:, k0 + k, s0:s1], start=a, stop=False)
                            pe.matmul(acc, wlo[:, u % 2, k, :], rhi[:, k0 + k, s0:s1], start=False, stop=False)
                            last_mm = pe.matmul(acc, whi[:, u % 2, k, :], rlo[:, k0 + k, s0:s1], start=False, stop=b)
                    last_mm.then_inc(S("w_used"), 1)
            run_turns(pe, st, do)

        phases = []

        def phase(name, **engines):
            phases.append(engines)

        def to(dest, func=ACT.Copy, ntok=None):
            def ev(eng, i, o, acc):
                n = acc.shape[1]
                d = dest[:, bass.ds(i * 2 + o, 1), 0:n].rearrange("p a n -> p (a n)")
                return eng.activation(d, acc, func)
            return ev

        xtok = arena("xtok", [P, NT, D])
        VR = arena("VR", [P, 3, P], off=24 * K1)
        crow = arena("crow", [16, P], off=30 * K1)
        lamb = arena("lamb", [P, 2, 256], off=26 * K1)
        lamp = arena("lamp", [P, 2, 2, 64], off=28 * K1)
        n_in = [0]

        def sp_inputs(sp):
            def load(dst, src):
                sp.dma_start(dst, src).then_inc(S("inputs"), 16)
                n_in[0] += 16
            for dst, src in ((const[:, :], t["const"]), (crow[0:8, :], t["c"][0].rearrange("(k p) -> k p", p=P)),
                             (crow[8:16, :], t["c_ctx"].rearrange("(k p) -> k p", p=P))):
                sp.dma_start(dst, src).then_inc(S("first_inputs"), 16)
            load(xtok[:, 0:4, :], t["x"][0].rearrange("(a p) n -> p a n", p=P))
            load(xtok[:, 4:6, :], t["ctx"][0].rearrange("(a p) n -> p a n", p=P))

            def rows(i, at, ap, n):
                load(VR[at:at + n, i, :], ap)
            for l in range(DEPTH):
                r = LROW
                one = lambda name, a: rows(l, r[name], a.rearrange("(k p) -> k p", p=P), a.shape[0] // P)
                one("mod_b", t["mod_b"][l])
                one("pre_g", t["norm_pre_g"][l])
                one("post_g", t["norm_post_g"][l])
                one("w0", t["rwkv_w0"][l].rearrange("d n -> (d n)"))
                one("a0", t["rwkv_a0"][l].rearrange("d n -> (d n)"))
                one("k_k", t["rwkv_k_k"][l])
                one("k_a", t["rwkv_k_a"][l])
                one("r_k", t["rwkv_r_k"][l].rearrange("d n -> (d n)"))
                one("ln_g", t["rwkv_ln_g"][l])
                one("ln_b", t["rwkv_ln_b"][l])
                one("conv_w", t["conv_w"][l].rearrange("d n -> (d n)"))
                one("subln", t["diff_subln_g"][l])
            b = B2ROW
            rows(2, b["rg_conv_w"], t["rg_conv_w_2"][0, :, 0].rearrange("j (k p) -> (j k) p", p=P), 32)
            rows(2, b["rg_conv_b"], t["rg_conv_b_2"][0].rearrange("(k p) -> k p", p=P), 8)
            rows(2, b["b_a"], t["rg_b_a_2"][0].rearrange("j (k p) -> (j k) p", p=P), 8)
            rows(2, b["b_i"], t["rg_b_i_2"][0].rearrange("j (k p) -> (j k) p", p=P), 8)
            rows(2, b["lam"], t["rg_lambda_2"][0].rearrange("(k p) -> k p", p=P), 8)
            for n, key in (("mix_pre", "norm_mix_pre_2"), ("mix_post", "norm_mix_post_2"),
                           ("ffn_pre", "norm_ffn_pre_2"), ("ffn_post", "norm_ffn_post_2")):
                rows(2, b[n], t[key].rearrange("l (k p) -> (l k) p", p=P), 16)
            for l in range(DEPTH):
                load(lamb[:, l, :], t["diff_lambda"][l].rearrange("a b -> (a b)").unsqueeze(0).to_broadcast([P, 256]))

            for g in range(MSLOTS, MGROUPS):
                sp.wait_ge(S("mod_used"), g - MSLOTS + 1)
                load_mod(sp, g)

        mslots = [arena("mod_w0", [P, 8, 512], off=32 * K1), arena("mod_w1", [P, 8, 512], off=48 * K1)] + \
                 [arena2(f"mod_w{2 + i}", [P, 8, 512], off=16 * i * K1) for i in range(3)]
        MSLOTS, MGROUPS, MFIRST = len(mslots), 6 * DEPTH, 4
        mrow = place("mod_rows_sb", [2, MGROUPS * 512], at=at_mix)

        def load_mod(eng, g):
            src = kview(t["mod_w"][g // 6])[:, :, (g % 6) * 512:(g % 6) * 512 + 512]
            eng.dma_start(mslots[g % MSLOTS][:, :, :], src).then_inc(S(f"mod_landed{g % MSLOTS}"), 16)

        N_INPUTS = 2 + 12 * DEPTH + 9 + DEPTH

        def pe_inputs(pe):
            pe.wait_ge(S("first_inputs"), 48)
            pe.transpose(bank(6)[:, 496:512], crow[0:16, :], ident[0:16, 0:16]).then_inc(S("c_cols"), 1)
            pe.wait_ge(S("silu_c"), 1)

            def mod_group(g):
                pe.wait_ge(S(f"mod_landed{g % MSLOTS}"), 16 * (g // MSLOTS + 1))
                if g >= 2:
                    pe.wait_ge(S("mod_rows"), g - 1)
                for k in range(8):
                    ins = pe.matmul(bank(4 + g % 2)[0:2, :], cs[:, k, :], mslots[g % MSLOTS][:, k, :],
                                    start=k == 0, stop=k == 7)
                ins.then_inc(S("mod_used"), 1)
            for g in range(MFIRST):
                mod_group(g)
            pe.wait_ge(S("inputs"), 16 * N_INPUTS)
            for i, n in ((0, LROWS), (1, LROWS), (2, B2ROWS)):
                ins = pe.transpose(bank(6)[:, i * P:i * P + n], VR[0:n, i, :], ident[0:n, 0:n])
            ins.then_inc(S("vec_cols"), 1)
            for T in range(NT):
                if T >= 2:
                    pe.wait_ge(S("xT_ready"), T - 1)
                for b in range(NB):
                    ins = pe.transpose(PW[T % 2][:, b * P:(b + 1) * P], xtok[:, T, b * P:(b + 1) * P], ident)
                ins.then_inc(S("xT_turned"), 1)
            for g in range(MFIRST, MGROUPS):
                mod_group(g)
            pe.wait_ge(S("mod_rows"), MGROUPS)
            for b in range(4 * MGROUPS):
                ins = pe.transpose(bank(7)[:, 2 * b:2 * b + 2], mrow[0:2, b * P:(b + 1) * P], ident[0:2, 0:2])
            ins.then_inc(S("mod_turned"), 1)

        def dve_inputs(dve):
            dve.memset(epsc[:, 0:1], EPS)
            dve.memset(epsc[:, 2:3], 0.0)
            dve.memset(epsc[:, 1:2], GN_EPS)
            dve.wait_ge(S("inputs"), 16 * N_INPUTS)
            dve.wait_ge(S("vec_cols"), 1)
            for i, n in ((0, LROWS), (1, LROWS), (2, B2ROWS)):
                ins = dve.tensor_copy(VC[:, i, 0:n], bank(6)[:, i * P:i * P + n])
            ins.then_inc(S("VC_ready"), 1)
            for T in range(NT):
                dve.wait_ge(S("xT_turned"), T + 1)
                dve.tensor_copy(xT[:, :, T * P:(T + 1) * P], PW[T % 2][:, :].rearrange("p (b n) -> p b n", b=NB)) \
                   .then_inc(S("xT_ready"), 1)
            lv = lamb[:].rearrange("p l (a c b) -> p l a c b", a=2, c=2)
            dve.tensor_tensor(lamp[:], lv[:, :, :, 0, :], lv[:, :, :, 1, :], ALU.mult)
            dve.drain()
            dve.tensor_reduce(sm[:, 0:4], lamp[:].rearrange("p l a b -> p (l a) b"), AXX, ALU.add) \
               .then_inc(S("lam_sums"), 1)
            dve.wait_ge(S("lam_exps"), 1)
            for l in range(DEPTH):
                init = 0.8 - 0.6 * math.exp(-0.3 * l)
                dve.tensor_tensor(sm[:, 8 + l:9 + l], sm[:, 4 + 2 * l + 1:4 + 2 * l + 2],
                                  sm[:, 4 + 2 * l:4 + 2 * l + 1], ALU.subtract)
                dve.drain()
                dve.tensor_scalar(sm[:, 8 + l:9 + l], sm[:, 8 + l:9 + l], init, None, ALU.subtract)
                dve.tensor_scalar(scl[:, 7, l:l + 1], VC[:, l, LROW["subln"]:LROW["subln"] + 1], 1.0 - init, None,
                                  ALU.mult)
            lcol = VC[:, 2, B2ROW["lam"]:B2ROW["lam"] + 8]
            E, A, Q, R, Z = (ltmp[:, i, :] for i in range(5))
            dve.wait_ge(S("lam_exps"), 2)
            dve.tensor_scalar(A, E, 2.0, None, ALU.add)
            dve.drain()
            dve.reciprocal(Q, A)
            dve.drain()
            dve.tensor_tensor(A, E, Q, ALU.mult)
            dve.drain()
            dve.tensor_tensor(Q, A, A, ALU.mult)
            dve.memset(R, 2.0 / 19)
            dve.drain()
            for n in range(17, 0, -2):
                dve.tensor_tensor(R, R, Q, ALU.mult)
                dve.drain()
                dve.tensor_scalar(R, R, 2.0 / n, None, ALU.add)
                dve.drain()
            dve.tensor_tensor(R, R, A, ALU.mult)
            dve.tensor_scalar(Z, lcol, -1.0, 0.0, ALU.mult, ALU.max)
            dve.drain()
            dve.tensor_tensor(R, R, Z, ALU.add)
            dve.drain()
            dve.tensor_scalar(scl[:, 6, 0:8], R, 8.0, None, ALU.mult)
            dve.tensor_scalar(scl[:, 6, 8:16], R, -8.0, None, ALU.mult)
            dve.wait_ge(S("mod_turned"), 1)
            dve_scales(dve)
            lo_part(dve, 0, stages[0], 0, stages[0]["body"][0])

        def act_inputs(act):
            act.wait_ge(S("first_inputs"), 48)
            for g in range(MSLOTS):
                load_mod(act, g)
            act.wait_ge(S("c_cols"), 1)
            act.activation(cs[:, :, 0], bank(6)[:, 496:504], ACT.Silu)
            act.activation(cs[:, :, 1], bank(6)[:, 504:512], ACT.Silu).then_inc(S("silu_c"), 1)

            def mod_rows(g):
                act.wait_ge(S("mod_used"), g + 1)
                act.activation(mrow[0:2, g * 512:(g + 1) * 512], bank(4 + g % 2)[0:2, :], ACT.Copy) \
                   .then_inc(S("mod_rows"), 1)
            for g in range(MFIRST):
                mod_rows(g)
            act.wait_ge(S("VC_ready"), 1)
            act.wait_ge(S("lam_sums"), 1)
            act.activation(sm[:, 4:8], sm[:, 0:4], ACT.Exp).then_inc(S("lam_exps"), 1)
            act.activation(ltmp[:, 1, :], VC[:, 2, B2ROW["lam"]:B2ROW["lam"] + 8], ACT.Abs)
            act.drain()
            act.activation(ltmp[:, 0, :], ltmp[:, 1, :], ACT.Exp, scale=-1.0).then_inc(S("lam_exps"), 1)
            for g in range(MFIRST, MGROUPS):
                mod_rows(g)
            hi_part(act, 0, stages[0], 0, stages[0]["body"][0])

        phase("inputs", sp=sp_inputs, pe=pe_inputs, dve=dve_inputs, act=act_inputs)

        def stream_phase(*sts, before=(), pe=None, dve=None, act=None):
            if before and "ready" in before[-1]:
                sts[0]["ready"] = before[-1]["ready"]

            def engine(which, stage, after):
                def run(e):
                    for part in before:
                        if which in part:
                            part[which](e)
                    for st in sts:
                        stage(e, st)
                    if after:
                        after(e)
                return run
            phase(sts[0]["name"], sp=lambda sp: [sp_stage(sp, st) for st in sts], pe=engine("pe", pe_stage, pe),
                  act=engine("act", lambda e, st: split_and_evac(e, "act", hi_part, st), act),
                  dve=engine("dve", lambda e, st: split_and_evac(e, "dve", lo_part, st), dve))

        def dve_scales(dve):
            for l in range(DEPTH):
                for s in range(2):
                    m = bank(7)[:, 48 * l:48 * l + 48].rearrange("p (b s) -> p b s", s=2)
                    dve.tensor_tensor(modT[:, l, :, s], m[:, :, s], VC[:, l, 0:24], ALU.add)
            dve.drain()
            for l in range(DEPTH):
                for s in range(2):
                    g, pg = (VC[:, l, LROW[n]:LROW[n] + 8] for n in ("pre_g", "post_g"))
                    v = scl[:, 3 * l:3 * l + 3, :].rearrange("p a (b s) -> p a b s", s=2)
                    dve.scalar_tensor_tensor(out=v[:, 0, :, s], in0=modT[:, l, 8:16, s], scalar=1.0, in1=g,
                                             op0=ALU.add, op1=ALU.mult)
                    dve.tensor_copy(v[:, 1, :, s], modT[:, l, 0:8, s])
                    dve.tensor_tensor(v[:, 2, :, s], modT[:, l, 16:24, s], pg, ALU.mult)

        def inverse_root(a, dst, work, sums, count, eps):
            a.activation(work, sums, ACT.Ln, scale=1.0 / count, bias=eps)
            a.drain()
            return a.activation(dst, work, ACT.Exp, scale=-0.5)

        def squares_beside(name, m, place_at, make_stage):
            ring = place_at(f"msq_{name}", [P, 2, TOK], 0)
            total = place_at(f"msum_{name}", [P, TOK], 6 * K1)
            added = Signal("squares_added", NB)

            def ev(eng, i, o, acc):
                w = acc.shape[1]
                if not isinstance(i, int) or i > 0:
                    eng.wait_ge(added.sem, i * 2 + (added.base + o - 1))
                eng.activation(ring[:, o, 0:w], acc, ACT.Square)
                d = m[:, bass.ds(i * 2 + o, 1), 0:w].rearrange("p a n -> p (a n)")
                return eng.activation(d, acc, ACT.Copy)
            st = make_stage(ev)

            def add(eng, i, o):
                w = st["ntok"]
                eng.wait_ge(S(f"evac_done{o % 2}"), i + (st["o0"] // 2 + 1))
                eng.tensor_tensor(total[:, 0:w], total[:, 0:w], ring[:, o, 0:w], ALU.add)
                eng.drain().then_inc(added.sem, 1)
            st["after"] = add

            def zero(v):
                v.memset(total[:], 0.0)
                v.drain()
            return st, total, dict(dve=zero)

        def norm_buffers(name):
            o = 48 * K1
            return (arena(f"sq_{name}", [P, 2, TOK], off=o), arena(f"root_{name}", [P, TOK], off=o + 6 * K1),
                    arena(f"rstd_{name}", [P, TOK], off=o + 9 * K1), arena(f"tmp_{name}", [P, 2, TOK], off=o + 12 * K1))

        def post_norm(name, m, total, ntok, gcol):
            segs = SEGS[ntok]
            _, root, rstd, tmp = norm_buffers("post" + name)
            summed, rooted, xnew = (Signal(f"post_{n_}", c) for n_, c in (("summed", 1), ("rooted", 1), ("x", NB)))

            def act(a):
                a.preload_act_table_set("natural_log_exp_and_others")
                a.wait_ge(summed.sem, summed.at(1))
                inverse_root(a, rstd[:, 0:ntok], root[:, 0:ntok], PW[2][:, 0:ntok], D, epsc[:, 0:1]) \
                    .then_inc(rooted.sem, 1)

            def pe(e):
                for s0, s1 in segs:
                    ins = e.matmul(PW[2][:, s0:s1], ones, total[:, s0:s1], start=True, stop=True)
                ins.then_inc(summed.sem, 1)

            def dve(v):
                v.wait_ge(rooted.sem, rooted.at(1))
                for b in range(NB):
                    for s, (s0, s1) in enumerate(segs):
                        v.scalar_tensor_tensor(out=tmp[:, b % 2, s0:s1], in0=m[:, b, s0:s1], scalar=gcol(b, s),
                                               in1=rstd[:, s0:s1], op0=ALU.mult, op1=ALU.mult)
                    if b:
                        v.tensor_tensor(xT[:, b - 1, 0:ntok], xT[:, b - 1, 0:ntok], tmp[:, (b - 1) % 2, 0:ntok], ALU.add) \
                         .then_inc(xnew.sem, 1)
                    v.drain()
                v.tensor_tensor(xT[:, NB - 1, 0:ntok], xT[:, NB - 1, 0:ntok], tmp[:, (NB - 1) % 2, 0:ntok], ALU.add) \
                 .then_inc(xnew.sem, 1)
                v.drain()
            return dict(pe=pe, act=act, dve=dve, xnew=xnew)

        def pre_norm(name, ntok, gcol, shift, xnew=None):
            segs = SEGS[ntok]
            ns = len(segs)
            sq, root, rstd, tmp = norm_buffers("pre" + name)
            made, summed, rooted, scaled, rounded, low_done = (
                Signal(f"pre_{n_}", c) for n_, c in (("squares", NB), ("summed", NB), ("rooted", 1),
                                                     ("scaled", NB), ("rounded", NB), ("low", NB)))

            def act(a):
                a.preload_act_table_set("natural_log_exp_and_others")
                for b in range(NB):
                    if xnew:
                        a.wait_ge(xnew.sem, xnew.at(b + 1))
                    if b >= 2:
                        a.wait_ge(summed.sem, summed.at(b - 1))
                    a.activation(sq[:, b % 2, 0:ntok], xT[:, b, 0:ntok], ACT.Square).then_inc(made.sem, 1)
                a.wait_ge(summed.sem, summed.at(NB))
                inverse_root(a, rstd[:, 0:ntok], root[:, 0:ntok], PW[3][:, 0:ntok], D, epsc[:, 0:1]) \
                    .then_inc(rooted.sem, 1)
                for b in range(NB):
                    a.wait_ge(scaled.sem, scaled.at(b + 1))
                    for s, (s0, s1) in enumerate(segs):
                        ins = a.activation(hhi[:, b, s0:s1], tmp[:, b % 2, s0:s1], ACT.Identity, bias=shift(b, s))
                    ins.then_inc(rounded.sem, 1)

            def pe(e):
                for b in range(NB):
                    e.wait_ge(made.sem, made.at(b + 1))
                    for s0, s1 in segs:
                        ins = e.matmul(PW[3][:, s0:s1], ones, sq[:, b % 2, s0:s1], start=b == 0, stop=b == NB - 1)
                    ins.then_inc(summed.sem, 1)

            def dve(v):
                def low(b):
                    v.wait_ge(rounded.sem, rounded.at(b + 1))
                    for s, (s0, s1) in enumerate(segs):
                        ins = v.scalar_tensor_tensor(out=hlo[:, b, s0:s1], in0=tmp[:, b % 2, s0:s1], scalar=shift(b, s),
                                                     in1=hhi[:, b, s0:s1].bitcast(F32), op0=ALU.add, op1=ALU.subtract)
                    ins.then_inc(low_done.sem, 1)
                v.wait_ge(rooted.sem, rooted.at(1))
                for b in range(NB):
                    if b >= 2:
                        v.drain()
                    for s, (s0, s1) in enumerate(segs):
                        ins = v.scalar_tensor_tensor(out=tmp[:, b % 2, s0:s1], in0=xT[:, b, s0:s1], scalar=gcol(b, s),
                                                     in1=rstd[:, s0:s1], op0=ALU.mult, op1=ALU.mult)
                    ins.then_inc(scaled.sem, 1)
                    if b:
                        low(b - 1)
                low(NB - 1)
            return dict(pe=pe, act=act, dve=dve, ready=lambda k: (low_done.sem, low_done.at(k + 1)))

        def split_mix(ntok):
            hr, low_done = Signal("mix_rounded", NB), Signal("mix_low", NB)

            def act(a):
                for b in range(NB):
                    a.activation(hhi[:, b, 0:ntok], mix[:, b, 0:ntok], ACT.Copy).then_inc(hr.sem, 1)

            def dve(v):
                for b in range(NB):
                    v.wait_ge(hr.sem, hr.at(b + 1))
                    v.tensor_tensor(hlo[:, b, 0:ntok], mix[:, b, 0:ntok], hhi[:, b, 0:ntok].bitcast(F32),
                                    ALU.subtract).then_inc(low_done.sem, 1)
            return dict(act=act, dve=dve, ready=lambda k: (low_done.sem, low_done.at(k + 1)))

        def conv_mixer(l, full, before):
            n = TOK if full else SEQ
            cb = arena(f"cb{l}", [P, 8, TOK])
            u = arena(f"cu{l}", [P, TOK], off=24 * K1)
            y = arena(f"cy{l}", [P, TOK], off=27 * K1)
            w = lambda j, hp: VC[:, l, LROW["conv_w"] + 2 * j + hp:LROW["conv_w"] + 2 * j + hp + 1]

            def dve(v):
                v.wait_ge(S("evac_done1"), conv_last[l])
                v.wait_ge(S("evac_done0"), conv_last[l])
                for hp in range(2):
                    v.tensor_tensor(u[:, 0:n], cb[:, 2 + hp, 0:n], cb[:, 4 + hp, 0:n], ALU.mult)
                    v.drain()
                    v.tensor_scalar(y[:, 0:n], u[:, 0:n], w(1, hp), None, ALU.mult)
                    v.drain()
                    for s0, s1 in SEGS[n]:
                        v.scalar_tensor_tensor(out=y[:, s0 + 1:s1], in0=u[:, s0:s1 - 1], scalar=w(0, hp),
                                               in1=y[:, s0 + 1:s1], op0=ALU.mult, op1=ALU.add)
                    v.drain()
                    for s0, s1 in SEGS[n]:
                        v.scalar_tensor_tensor(out=y[:, s0:s1 - 1], in0=u[:, s0 + 1:s1], scalar=w(2, hp),
                                               in1=y[:, s0:s1 - 1], op0=ALU.mult, op1=ALU.add)
                    v.drain()
                    v.tensor_tensor(y[:, 0:n], y[:, 0:n], cb[:, hp, 0:n], ALU.mult)
                    v.drain()
                    v.tensor_tensor(mix[:, 2 + hp, 0:n], y[:, 0:n], cb[:, 6 + hp, 0:n], ALU.mult)
                    v.drain()
            w_in = t["w_in"][l]
            a = plain(f"conv{l}", w_in, C_CONV, 6, n, (hhi, hlo), to(cb))
            b = plain(f"convz{l}", w_in, C_CONV + 768, 2, n, (hhi, hlo), to(cb[:, 6:8, :], ACT.Silu))
            conv_last[l] = (b["o0"] + 2) // 2
            stream_phase(a, b, before=before, dve=dve)

        conv_last = {}

        def attention(l, full):
            n = TOK if full else SEQ
            w_in = t["w_in"][l]
            q = arena(f"aq{l}", [P, 4, TOK])
            k = arena(f"ak{l}", [P, 4, TOK], off=12 * K1)
            z = arena(f"az{l}", [P, 4, TOK], off=24 * K1)
            vtok = arena(f"avt{l}", [P, NT, 512], off=36 * K1)
            vch = arena(f"avc{l}", [P, 4, TOK], off=48 * K1)
            AT = arena(f"aAT{l}", [P, NT, 512], off=48 * K1)
            prob = [arena(f"apr{l}", [P, 2, TOK], off=60 * K1),
                    [place(f"aprb{l}", [P, TOK], at=at_whi1), place(f"aprc{l}", [P, TOK], at=at_wlo1)]]
            pr = lambda i, j, w: (prob[0][:, j, 0:w] if i % 2 == 0 else prob[1][j][:, 0:w])
            rot = arena(f"arot{l}", [P, 2, SEQ], off=60 * K1)
            st = sm[:, 16:32]

            vtu, vts = Signal("v_turned", NT), Signal("v_tokens", NT)

            def pe_v(e):
                e.wait_ge(S("evac_done0"), (vs["o0"] + 4) // 2)
                e.wait_ge(S("evac_done1"), (vs["o0"] + 4) // 2)
                for T in range(NT):
                    if T >= 2:
                        e.wait_ge(vts.sem, vts.at(T - 1))
                    for h in range(4):
                        ins = e.transpose(bank(4 + T % 2)[:, h * P:(h + 1) * P], vch[:, h, T * P:(T + 1) * P], ident)
                    ins.then_inc(vtu.sem, 1)

            def act_v(a):
                for T in range(NT):
                    a.wait_ge(vtu.sem, vtu.at(T + 1))
                    a.activation(vtok[:, T, :], bank(4 + T % 2), ACT.Copy).then_inc(vts.sem, 1)

            def rope(x, sts):
                def turn_head(v, h):
                    v.wait_ge(S(f"evac_done{h % 2}"), sts["o0"] // 2 + h // 2 + 1)
                    v.stream_shuffle(rot[:, 0, :], x[:, h, 0:SEQ], [j ^ 16 for j in range(32)])
                    v.tensor_tensor(rot[:, 1, :], x[:, h, 0:SEQ], cc("cos"), ALU.mult)
                    v.drain()
                    v.tensor_tensor(rot[:, 0, :], rot[:, 0, :], cc("sin"), ALU.mult)
                    v.drain()
                    v.tensor_tensor(x[:, h, 0:SEQ], rot[:, 0, :], rot[:, 1, :], ALU.add)
                    v.drain()
                return dict(dve=turn_head)
            qs = plain(f"aq{l}", w_in, C_AQ, 4, n, (hhi, hlo), to(q))
            ks = plain(f"ak{l}", w_in, C_AK, 4, TOK, (hhi, hlo), to(k))
            zs = plain(f"az{l}", w_in, C_AZ, 4, n, (hhi, hlo), to(z, ACT.Silu))
            vs = plain(f"av{l}", w_in, C_AV, 4, TOK, (hhi, hlo), to(vch))
            ks["beside"], zs["beside"] = rope(q, qs), rope(k, ks)
            stream_phase(qs, ks, zs, vs, pe=pe_v, act=act_v)

            steps = []
            for h in range(4):
                steps += [(h, qt, 0, 0, NT) for qt in range(4)]
                if full:
                    steps += [(h, qt, SEQ, 4, 2) for qt in (4, 5)]
            finals = []
            for i, (h, qt, c0, kt0, nk) in enumerate(steps):
                if qt in (3, 5):
                    finals.append((i, h, qt == 5))
            fin_at = {i: (f, h, c) for f, (i, h, c) in enumerate(finals)}
            ns, nf = len(steps), len(finals)
            sc_, mx, ex, cb_, tr, at, pv, osq, osum, ort, omix = (
                Signal(f"attn_{nm}", c) for nm, c in (
                    ("scores", 2 * ns), ("max", 2 * ns), ("exps", 2 * ns), ("combined", ns), ("turned", ns), ("AT", ns),
                    ("out", nf), ("out_read", 2 * nf), ("sums", nf), ("root", nf), ("mixed", nf)))
            scale = 64 ** -0.5
            osb = place(f"aosb{l}", [P, 3, 512], at=at_mix)

            def pe_scores(e, i):
                h, qt, c0, kt0, nk = steps[i]
                for j in range(2):
                    if i:
                        e.wait_ge(ex.sem, ex.at(2 * (i - 1) + j + 1))
                    width = nk * P
                    for s0 in range(0, width, 512):
                        s1 = min(width, s0 + 512)
                        ins = e.matmul(PW[j][:, s0:s1], q[64 * j:64 * j + 64, h, qt * P:(qt + 1) * P],
                                       k[64 * j:64 * j + 64, h, c0 + s0:c0 + s1], start=True, stop=True)
                    ins.then_inc(sc_.sem, 1)

            def pe_attn(e):
                pe_scores(e, 0)
                for i in range(ns + 2):
                    if i + 1 < ns:
                        pe_scores(e, i + 1)
                    if i - 1 in fin_at:
                        f, h, is_ctx = fin_at[i - 1]
                        _, _, _, kt0, nk = steps[i - 1]
                        w = 256 if is_ctx else 512
                        e.wait_ge(at.sem, at.at(i))
                        if f:
                            e.wait_ge(osq.sem, osq.at(2 * f))
                        for kt in range(nk):
                            ins = e.matmul(bank(6)[:, 0:w], vtok[:, kt0 + kt, h * P:(h + 1) * P],
                                           AT[:, kt, 0:w], start=kt == 0, stop=kt == nk - 1)
                        ins.then_inc(pv.sem, 1)
                    if i < ns:
                        nk = steps[i][4]
                        e.wait_ge(cb_.sem, cb_.at(i + 1))
                        if i:
                            e.wait_ge(at.sem, at.at(i))
                        for kt in range(nk):
                            ins = e.transpose(PW[2][:, kt * P:(kt + 1) * P], pr(i, 0, nk * P)[:, kt * P:(kt + 1) * P],
                                              ident)
                        ins.then_inc(tr.sem, 1)
                    if i - 2 in fin_at:
                        f, _, is_ctx = fin_at[i - 2]
                        w = 256 if is_ctx else 512
                        e.wait_ge(osq.sem, osq.at(2 * f + 2))
                        if f:
                            e.wait_ge(ort.sem, ort.at(f))
                        e.matmul(bank(7)[:, 0:w], ones, osb[:, 1, 0:w], start=True, stop=True).then_inc(osum.sem, 1)

            def act_attn(a):
                a.preload_act_table_set("natural_log_exp_and_others")
                for i in range(ns + 3):
                    if i < ns:
                        nk = steps[i][4]
                        if i >= 2:
                            a.wait_ge(tr.sem, tr.at(i - 1))
                        for j in range(2):
                            a.wait_ge(mx.sem, mx.at(2 * i + j + 1))
                            a.activation(pr(i, j, nk * P), PW[j][:, 0:nk * P], ACT.Exp, scale=scale,
                                         bias=st[:, 2 + j:3 + j], accum_out=st[:, 4 + j:5 + j]).then_inc(ex.sem, 1)
                    if 1 <= i <= ns:
                        h, qt, _, _, nk = steps[i - 1]
                        is_ctx = qt >= 4
                        a.wait_ge(tr.sem, tr.at(i))
                        if qt in (0, 4) and i > 1:
                            a.wait_ge(pv.sem, pv.at(sum(1 for x in finals if x[0] < i - 1)))
                        qq = (qt - 4 if is_ctx else qt) * P
                        a.activation(AT[:, 0:nk, qq:qq + P], PW[2][:, 0:nk * P].rearrange("p (a b) -> p a b", b=P),
                                     ACT.Copy).then_inc(at.sem, 1)
                    if i - 2 in fin_at:
                        f, _, is_ctx = fin_at[i - 2]
                        w = 256 if is_ctx else 512
                        a.wait_ge(pv.sem, pv.at(f + 1))
                        if f:
                            a.wait_ge(omix.sem, omix.at(f))
                        a.activation(osb[:, 0, 0:w], bank(6)[:, 0:w], ACT.Copy).then_inc(osq.sem, 1)
                        a.activation(osb[:, 1, 0:w], bank(6)[:, 0:w], ACT.Square).then_inc(osq.sem, 1)
                    if i - 3 in fin_at:
                        f, _, is_ctx = fin_at[i - 3]
                        w = 256 if is_ctx else 512
                        a.wait_ge(osum.sem, osum.at(f + 1))
                        inverse_root(a, osb[:, 2, 0:w], osb[:, 2, 0:w], bank(7)[:, 0:w], P, epsc[:, 0:1]) \
                            .then_inc(ort.sem, 1)

            def dve_attn(v):
                def finish(f, h, is_ctx):
                    w, c = (256, SEQ) if is_ctx else (512, 0)
                    v.wait_ge(ort.sem, ort.at(f + 1))
                    v.scalar_tensor_tensor(out=osb[:, 0, 0:w], in0=osb[:, 0, 0:w], scalar=scl[:, 7, l:l + 1],
                                           in1=osb[:, 2, 0:w], op0=ALU.mult, op1=ALU.mult)
                    v.drain()
                    v.tensor_tensor(mix[:, 4 + h, c:c + w], osb[:, 0, 0:w], z[:, h, c:c + w], ALU.mult) \
                     .then_inc(omix.sem, 1)
                for i in range(ns + 3):
                    if i < ns:
                        w = steps[i][4] * P
                        for j in range(2):
                            v.wait_ge(sc_.sem, sc_.at(2 * i + j + 1))
                            v.reduce_max(st[:, j:j + 1], PW[j][:, 0:w], AXX)
                            v.drain()
                            v.tensor_scalar(st[:, 2 + j:3 + j], st[:, j:j + 1], -scale, None, ALU.mult) \
                             .then_inc(mx.sem, 1)
                        v.wait_ge(ex.sem, ex.at(2 * i + 2))
                        v.reciprocal(st[:, 6:8], st[:, 4:6])
                        v.drain()
                        v.tensor_tensor(st[:, 8:9], st[:, 7:8], sm[:, 8 + l:9 + l], ALU.mult)
                        v.drain()
                        v.tensor_scalar(pr(i, 1, w), pr(i, 1, w), st[:, 8:9], None, ALU.mult)
                        v.drain()
                        v.scalar_tensor_tensor(out=pr(i, 0, w), in0=pr(i, 0, w), scalar=st[:, 6:7],
                                               in1=pr(i, 1, w), op0=ALU.mult, op1=ALU.add).then_inc(cb_.sem, 1)
                    if i - 3 in fin_at:
                        finish(*fin_at[i - 3])
            phase("attention", pe=pe_attn, act=act_attn, dve=dve_attn)

        def rwkv(l, full):
            n = TOK if full else SEQ
            w_in = t["w_in"][l]
            col = lambda name, i: VC[:, l, LROW[name] + i:LROW[name] + i + 1]
            r = arena(f"r{l}", [P, 2, TOK])
            k = arena(f"k{l}", [P, 2, TOK], off=6 * K1)
            v_ = arena(f"v{l}", [P, 2, TOK], off=12 * K1)
            z = arena(f"z{l}", [P, 2, TOK], off=18 * K1)
            lora = arena(f"lora{l}", [P, 2, TOK], off=24 * K1)
            kk = arena(f"kk{l}", [P, 2, TOK], off=30 * K1)
            nkk = kk
            icl = arena(f"icl{l}", [P, 2, 2, TOK], off=36 * K1)
            vtok = arena(f"rvt{l}", [P, NT, 256], off=48 * K1)
            wup = arena(f"wup{l}", [P, 2, 256], off=54 * K1)
            cm = arena2(f"cm{l}", [P, 2, 2, TOK])
            cum = arena2(f"cum{l}", [P, 2, 2, TOK], off=12 * K1)
            AR = arena2(f"AR{l}", [P, 2, 2, 3, P], off=24 * K1)
            BK = arena2(f"BK{l}", [P, 2, 2, 4, P], off=30 * K1)
            MB = arena2(f"MB{l}", [P, 8, 3, CH], off=38 * K1)
            MK = arena2(f"MK{l}", [P, 8, 2, CH], off=44 * K1)
            AW = arena(f"AW{l}", [P, 8, 2, CH], off=54 * K1)
            Tt = arena(f"Tt{l}", [P, 8, CH], off=58 * K1)
            X = arena(f"X{l}", [P, 8, CH], off=60 * K1)
            XT = arena(f"XT{l}", [P, 8, CH], off=62 * K1)
            G = arena(f"G{l}", [P, 8, CH], off=64 * K1)
            QT = arena(f"QT{l}", [P, 8, CH], off=66 * K1)
            ST = arena(f"ST{l}", [P, 4, CH], off=24 * K1)
            SH = arena(f"SH{l}", [P, 4, CH], off=25 * K1)
            t1 = arena2(f"t1{l}", [P, 2, TOK], off=24 * K1)
            t2 = arena2(f"t2{l}", [P, 2, TOK], off=30 * K1)

            r_st = plain(f"pr{l}", w_in, C_R, 2, n, (hhi, hlo), to(r))
            k_st = plain(f"pk{l}", w_in, C_K, 2, TOK, (hhi, hlo), to(k))
            v_st = plain(f"pv{l}", w_in, C_V, 2, TOK, (hhi, hlo), to(v_))

            def ev_lora(eng, i, o, acc):
                return eng.activation(lora[:, o, 0:TOK], acc, ACT.Tanh if o == 0 else ACT.Copy)
            l_st = plain(f"pl{l}", w_in, C_LORA, 2, TOK, (hhi, hlo), ev_lora)
            z_st = plain(f"pz{l}", w_in, C_Z, 2, n, (hhi, hlo), to(z, ACT.Silu))
            stream_phase(r_st, k_st, v_st, l_st, z_st)

            lnorm, s_wup, s_vtok, s_vturn = (Signal("kk_squares", 2), Signal("lora_weights", 32), Signal("rwkv_v_tokens", NT),
                                             Signal("rwkv_v_turned", NT))
            s_kksum, s_kkroot = Signal("kk_summed", 2), Signal("kk_root", 2)

            def pool_prep(pool):
                pool.wait_ge(S("phase_end"), 3 * phase_of[f"rprep{l}"])
                pool.dma_start(wup[:, 0, :], t["rwkv_w_up"][l].rearrange("d a n -> (d a) n")).then_inc(s_wup.sem, 16)
                pool.dma_start(wup[:, 1, :], t["rwkv_a_up"][l].rearrange("d a n -> (d a) n")).then_inc(s_wup.sem, 16)

            up, upe = Signal("lora_up", 8), Signal("lora_up_read", 8)

            def pe_prep(e):
                for T in range(NT):
                    if T >= 2:
                        e.wait_ge(s_vtok.sem, s_vtok.at(T - 1))
                    for hp in range(2):
                        ins = e.transpose(bank(6 + T % 2)[:, hp * P:(hp + 1) * P], v_[:, hp, T * P:(T + 1) * P], ident)
                    ins.then_inc(s_vturn.sem, 1)
                e.wait_ge(s_wup.sem, s_wup.at(32))
                i = 0
                for kind in range(2):
                    for d in range(2):
                        for hp in range(2):
                            if i >= 2:
                                e.wait_ge(upe.sem, upe.at(i - 1))
                            for s0, s1 in SEGS[TOK]:
                                ins = e.matmul(PW[i % 2][:, s0:s1], wup[64 * d:64 * d + 64, kind, hp * P:(hp + 1) * P],
                                               lora[64 * d:64 * d + 64, kind, s0:s1], start=True, stop=True)
                            ins.then_inc(up.sem, 1)
                            i += 1
                for hp in range(2):
                    e.wait_ge(lnorm.sem, lnorm.at(hp + 1))
                    if hp == 0:
                        e.wait_ge(upe.sem, upe.at(8))
                    for s0, s1 in SEGS[TOK]:
                        ins = e.matmul(PW[hp][:, s0:s1], headones, t1[:, hp, s0:s1], start=True, stop=True)
                    ins.then_inc(s_kksum.sem, 1)

            def act_prep(a):
                i = 0
                for kind in range(2):
                    for d in range(2):
                        for hp in range(2):
                            a.wait_ge(up.sem, up.at(i + 1))
                            dst = (cm, icl)[kind][:, d, hp, :]
                            a.activation(dst, PW[i % 2][:, 0:TOK], ACT.Sigmoid,
                                         bias=col(("w0", "a0")[kind], 2 * d + hp)).then_inc(upe.sem, 1)
                            i += 1
                for hp in range(2):
                    a.wait_ge(s_kksum.sem, s_kksum.at(hp + 1))
                    a.activation(t2[:, hp, :], PW[hp][:, 0:TOK], ACT.Sqrt).then_inc(s_kkroot.sem, 1)

            def dve_prep(v):
                for hp in range(2):
                    v.tensor_scalar(kk[:, hp, :], k[:, hp, :], col("k_k", hp), None, ALU.mult)
                v.drain()
                for hp in range(2):
                    v.tensor_tensor(t1[:, hp, :], kk[:, hp, :], kk[:, hp, :], ALU.mult).then_inc(lnorm.sem, 1)
                v.memset(mix[:, 0:2, 0:n], 0.0)
                for T in range(NT):
                    v.wait_ge(s_vturn.sem, s_vturn.at(T + 1))
                    v.tensor_copy(vtok[:, T, :], bank(6 + T % 2)[:, 0:256]).then_inc(s_vtok.sem, 1)
                v.wait_ge(upe.sem, upe.at(4))
                v.tensor_scalar(cm[:], cm[:], -math.exp(-0.5), None, ALU.mult)
                v.drain()
                for hp in range(2):
                    v.tensor_tensor_scan(cum[:, 0, hp, :], cc("reset"), cm[:, 0, hp, :], 0.0, ALU.mult, ALU.add)
                    v.tensor_tensor_scan(cum[:, 1, hp, ::-1], cc("reset"), cm[:, 1, hp, ::-1], 0.0, ALU.mult, ALU.add)
                v.drain()
                v.tensor_tensor(cm[:], cum[:], cm[:], ALU.subtract)
                v.wait_ge(s_kkroot.sem, s_kkroot.at(2))
                v.tensor_scalar(t2[:], t2[:], 1e-12, None, ALU.max)
                v.drain()
                v.reciprocal(t2[:], t2[:])
                v.drain()
                v.scalar_tensor_tensor(out=kk[:].rearrange("p a b -> p (a b)"), in0=kk[:].rearrange("p a b -> p (a b)"),
                                       scalar=-1.0, in1=t2[:].rearrange("p a b -> p (a b)"),
                                       op0=ALU.mult, op1=ALU.mult)
                v.tensor_scalar(scl_ka[:, 0:2], VC[:, l, LROW["k_a"]:LROW["k_a"] + 2], -1.0, 1.0, ALU.mult, ALU.add)
                v.tensor_scalar(scl_ka[:, 2:4], VC[:, l, LROW["k_a"]:LROW["k_a"] + 2], -2.0, 2.0, ALU.mult, ALU.add)
            scl_ka = sm[:, 40:44]
            phase_of[f"rprep{l}"] = len(phases)
            phase("rwkv prep", pool=pool_prep, pe=pe_prep, act=act_prep, dve=dve_prep)

            order = [[4, 5, 0, 1, 2, 3], [5, 4, 3, 2, 1, 0]]
            NBATCH = NT

            def has_y(j):
                return full or j >= 2

            per = dict(exps=2, AR=2, BK=2, Lb=2, Lk=2, tA=1, tB=1, tK=1, mb=2, mk=2, aw=1, bh=1, kh=1, w1=1, w1e=1,
                       T=12, Te=12, X=8, Xe=10, XT=10, XTe=12, xa=2, xae=2, gq=2, gqe=1,
                       hy=2, chS=2, che=2)
            sem = {nm: S(f"rw_{nm}") for nm in per}

            def value(nm, j, n):
                return (l * NBATCH + j) * per[nm] + n

            def tiles(j):
                return [slice(order[d][j] * P, order[d][j] * P + P) for d in range(2)]

            def group(d):
                return slice(4 * d, 4 * d + 4)

            a0, a1 = CONST_AT["seen0"][0], CONST_AT["seen1"][0]
            assert a1 == a0 + 2 * CH
            seen_both = const[:, a0:a0 + 4 * CH]
            levels = cc("level").rearrange("p (j d b) -> p j d b", j=6, d=2)
            I4 = ident2.unsqueeze(1).to_broadcast([P, 4, CH])

            def wcol(j, d, pi, hp):
                c = 48 + 8 * (j % 2) + 4 * d + 2 * pi + hp
                return sm[:, c:c + 1]

            def act_exps(a, j):
                if j:
                    a.wait_ge(sem["tK"], value("tK", j - 1, 1))
                for d in range(2):
                    s = tiles(j)[d]
                    a.activation(AR[:, d, :, 0, :], cm[:, d, :, s], ACT.Exp)
                    a.activation(AR[:, d, :, 1 + j % 2, :], cum[:, d, :, s], ACT.Exp)
                    a.activation(BK[:, d, :, 0, :], cum[:, d, :, s], ACT.Exp, scale=-1.0).then_inc(sem["exps"], 1)

            def act_batch(a, j):
                v4 = lambda i: bank(i).rearrange("p (a b) -> p a b", b=CH)
                if j:
                    a.wait_ge(sem["chS"], value("chS", j - 1, 2))
                a.wait_ge(sem["tA"], value("tA", j, 1))
                a.activation(AW[:, :, 0, :], v4(4), ACT.Copy).then_inc(sem["aw"], 1)
                a.wait_ge(sem["tB"], value("tB", j, 1))
                a.activation(MB[:, :, 2, :], v4(5), ACT.Copy).then_inc(sem["bh"], 1)
                a.wait_ge(sem["w1"], value("w1", j, 1))
                a.activation(AW[:, :, 1, :], v4(7), ACT.Copy).then_inc(sem["w1e"], 1)
                a.wait_ge(sem["tK"], value("tK", j, 1))
                a.activation(MK[:, :, 0, :], v4(6), ACT.Copy).then_inc(sem["kh"], 1)
                if j + 1 < NBATCH:
                    act_exps(a, j + 1)
                for d in range(2):
                    a.wait_ge(sem["xa"], value("xa", j, d + 1))
                    src = bank(6 + d).rearrange("p (a c b) -> p a c b", c=2, b=CH)
                    a.activation(AW[:, group(d), 1::-1, :], src, ACT.Copy).then_inc(sem["xae"], 1)

            def pool_batch(g, j):
                for d in range(2):
                    s = tiles(j)[d]
                    A, R = AR[:, d, :, 0, :], AR[:, d, :, 1 + j % 2, :]
                    B, K, Bh = (BK[:, d, :, i, :] for i in range(3))
                    if j:
                        g.wait_ge(sem["tK"], value("tK", j - 1, 1))
                    for hp in range(2):
                        g.tensor_scalar(K[:, hp, :], icl[:, d, hp, s], col("k_a", hp), scl_ka[:, hp:hp + 1],
                                        ALU.mult, ALU.add)
                    g.tensor_tensor(Bh, nkk[:, :, s], icl[:, d, :, s], ALU.mult)
                    g.drain()
                    g.wait_ge(sem["exps"], value("exps", j, d + 1))
                    g.tensor_tensor(A, nkk[:, :, s], A, ALU.mult)
                    g.tensor_tensor(K, K, k[:, :, s], ALU.mult)
                    g.tensor_scalar(Bh, Bh, -1.0, None, ALU.mult)
                    end = CH - 1 if d == 0 else 0
                    c = 48 + 8 * (j % 2) + 4 * d
                    g.tensor_copy(sm[:, c:c + 4].rearrange("p (i h) -> p h i", i=2), R[:, :, end::CH])
                    g.drain()
                    g.tensor_tensor(K, K, B, ALU.mult)
                    if has_y(j):
                        g.tensor_tensor(R, R, r[:, :, s], ALU.mult)
                    g.drain()
                    g.tensor_tensor(B, Bh, B, ALU.mult).then_inc(sem["AR"], 1)
                    g.drain()
                    for hp in range(2):
                        for pi in range(2):
                            g.tensor_scalar(BK[:, d, hp, 2:4, pi * CH:(pi + 1) * CH],
                                            BK[:, d, hp, 0:2, pi * CH:(pi + 1) * CH], wcol(j, d, pi, hp), None,
                                            ALU.mult)
                    g.drain().then_inc(sem["BK"], 1)

            def dve_batch(v, j):
                for bk, M, made, masked in ((0, MB, "Lb", "mb"), (2, MK, "Lk", "mk")):
                    seen = seen_both.rearrange("p (d n) -> p d n", d=2).unsqueeze(2).to_broadcast([P, 2, 2, 2 * CH])
                    for e_ in range(2):
                        v.wait_ge(sem[made], value(made, j, e_ + 1))
                        dst = M[:, :, 0:2, :].rearrange("p (d h e) c b -> p e d h (c b)", d=2, e=2)[:, e_]
                        v.tensor_tensor(dst, bank(bk + e_).rearrange("p (d h n) -> p d h n", d=2, h=2), seen,
                                        ALU.mult).then_inc(sem[masked], 1)
                    if M is MB:
                        v.drain()
                        v.tensor_tensor(XT[:].rearrange("p (d h) b -> p d h b", d=2),
                                        MB[:, :, 0, :].rearrange("p (d h) b -> p d h b", d=2),
                                        levels[:, 0, ::-1, :].unsqueeze(2).to_broadcast([P, 2, 4, CH]), ALU.mult)
                        v.drain()
                        for d in range(2):
                            v.tensor_tensor(XT[:, group(d), :], XT[:, group(d), :], I4, ALU.add) \
                             .then_inc(sem["XTe"], 1)
                for lv in range(6):
                    for d in range(2):
                        v.wait_ge(sem["T"], value("T", j, 2 * lv + d + 1))
                        v.tensor_tensor(Tt[:, group(d), :], bank(d)[:, 0:256].rearrange("p (a b) -> p a b", b=CH),
                                        levels[:, lv, d, :].unsqueeze(1).to_broadcast([P, 4, CH]), ALU.mult) \
                         .then_inc(sem["Te"], 1)
                    if lv == 0:
                        v.drain()
                        for d in range(2):
                            v.tensor_tensor(X[:, group(d), :], Tt[:, group(d), :], I4, ALU.add) \
                             .then_inc(sem["Xe"], 1)
                        continue
                    for d in range(2):
                        if lv < 5:
                            v.wait_ge(sem["X"], value("X", j, 2 * lv + d - 1))
                            v.tensor_tensor(X[:, group(d), :], X[:, group(d), :],
                                            bank(2 + d)[:, 0:256].rearrange("p (a b) -> p a b", b=CH), ALU.add) \
                             .then_inc(sem["Xe"], 1)
                    for d in range(2):
                        v.wait_ge(sem["XT"], value("XT", j, 2 * lv + d - 1))
                        v.tensor_tensor(XT[:, group(d), :], XT[:, group(d), :],
                                        bank(4 + d)[:, 0:256].rearrange("p (a b) -> p a b", b=CH), ALU.add) \
                         .then_inc(sem["XTe"], 1)
                for pi in range(2):
                    v.wait_ge(sem["gq"], value("gq", j, pi + 1))
                    src = bank(pi).rearrange("p (g c b) -> p g c b", g=4, b=CH)
                    v.tensor_copy(G[:].rearrange("p (g c) b -> p c g b", c=2)[:, pi], src[:, :, 0, :])
                    if has_y(j):
                        v.tensor_tensor(QT[:].rearrange("p (g c) b -> p c g b", c=2)[:, pi], src[:, :, 1, :],
                                        AR[:, :, :, 1 + j % 2, pi * CH:(pi + 1) * CH].rearrange("p d h b -> p (d h) b"),
                                        ALU.add)
                v.drain().then_inc(sem["gqe"], 1)

                def add_y(src, pis):
                    for d in range(2):
                        c = tiles(j)[d].start + pis[d] * CH
                        y = mix[:, 0:2, c:c + CH]
                        v.tensor_tensor(y, y, src(d)[:, (4 + 2 * d) * CH:(6 + 2 * d) * CH]
                                        .rearrange("p (a b) -> p a b", b=CH), ALU.add)

                def decayed(step):
                    c = 48 + 8 * (j % 2)
                    wv = sm[:, c:c + 8].rearrange("p (d i h) -> p d i h", d=2, i=2)
                    for d in range(2):
                        v.tensor_tensor(SH[:, 2 * d:2 * d + 2, :], ST[:, 2 * d:2 * d + 2, :],
                                        wv[:, d, (step, 1 - step)[d], :].unsqueeze(2).to_broadcast([P, 2, CH]), ALU.mult)
                    v.drain()

                def add_own(step):
                    for d in range(2):
                        pi = (step, 1 - step)[d]
                        v.tensor_tensor(SH[:, 2 * d:2 * d + 2, :], SH[:, 2 * d:2 * d + 2, :],
                                        bank(2 + pi)[:, 2 * d * CH:(2 * d + 2) * CH].rearrange("p (a b) -> p a b", b=CH),
                                        ALU.add)
                    v.drain()
                for step in range(2):
                    decayed(step)
                    if step == 0:
                        v.wait_ge(sem["hy"], value("hy", j, 2))
                    add_own(step)
                    v.wait_ge(sem["chS"], value("chS", j, step + 1))
                    v.tensor_tensor(ST[:], SH[:], bank(4 + step)[:, 0:4 * CH].rearrange("p (a b) -> p a b", b=CH),
                                    ALU.add)
                    v.drain().then_inc(sem["che"], 1)
                if has_y(j):
                    for step in range(2):
                        add_y(lambda d: bank(2 + (step, 1 - step)[d]), (step, 1 - step))
                    v.drain()
                    for step in range(2):
                        add_y(lambda d: bank(4 + step), (step, 1 - step))
                v.drain().then_inc(S("rw_y_added"), 1)

            def units(d):
                for hp in range(2):
                    for e_ in range(2):
                        for pi in range(2):
                            yield hp, e_, pi, 4 * d + 2 * hp + e_, slice(64 * e_, 64 * e_ + 64), slice(64 * pi, 64 * pi + 64)

            def pe_scores(e, j, i):
                Rk = 1 + j % 2
                bk, made = ((0, "Lb"), (2, "Lk"))[i]
                for d in range(2):
                    e.wait_ge(sem["AR"], value("AR", j, d + 1))
                for half in range(2):
                    for d in range(2):
                        for hp, e_, pi, dh, re, rp in units(d):
                            if e_ == half:
                                a = (2 * d + hp) * 2 * CH
                                ins = e.matmul(bank(bk + e_)[rp, a:a + 2 * CH], BK[re, d, hp, i, rp],
                                               AR[re, d, hp, 0:Rk + 1:Rk, rp], start=True, stop=True)
                    ins.then_inc(sem[made], 1)

            def pe_batch(e, j):
                T = [order[d][j] for d in range(2)]
                if j == 0:
                    pe_scores(e, j, 0)
                if l or j:
                    e.wait_ge(S("rw_y_added"), l * NBATCH + j)
                pe_scores(e, j, 1)
                for d in range(2):
                    e.wait_ge(sem["BK"], value("BK", j, d + 1))
                for i, made in enumerate(("tA", "tB", "tK")):
                    for d in range(2):
                        for hp in range(2):
                            src = AR[:, d, hp, 0, :] if i == 0 else BK[:, d, hp, 1 + i, :]
                            a = (2 * d + hp) * P
                            ins = e.transpose(bank(4 + i)[:, a:a + P], src, ident)
                    ins.then_inc(sem[made], 1)
                e.wait_ge(sem["mb"], value("mb", j, 2))
                for d in range(2):
                    for hp, e_, pi, dh, re, rp in units(d):
                        a = (dh % 4) * CH
                        ins = e.matmul(bank(d)[rp, a:a + CH], MB[rp, dh, 0, :], ident2[rp, :], start=True, stop=True)
                    ins.then_inc(sem["T"], 1)
                e.wait_ge(sem["mk"], value("mk", j, 2))
                for d in range(2):
                    for hp, e_, pi, dh, re, rp in units(d):
                        ins = e.matmul(bank(7)[rp, dh * CH:(dh + 1) * CH], MK[rp, dh, 0, :],
                                       vtok[rp, T[d], (2 * hp + e_) * CH:(2 * hp + e_ + 1) * CH], start=True, stop=True)
                ins.then_inc(sem["w1"], 1)
                e.wait_ge(sem["bh"], value("bh", j, 1))
                for lv in range(1, 6):
                    for d in range(2):
                        e.wait_ge(sem["Xe"], value("Xe", j, 2 * lv - 2 + d + 1))
                        for hp, e_, pi, dh, re, rp in units(d):
                            a = (dh % 4) * CH
                            ins = e.matmul(bank(d)[rp, a:a + CH], MB[rp, dh, 0, :], X[rp, dh, :], start=True, stop=True)
                        ins.then_inc(sem["T"], 1)
                    if lv < 5:
                        for d in range(2):
                            e.wait_ge(sem["Te"], value("Te", j, 2 * lv + d + 1))
                            e.wait_ge(sem["XTe"], value("XTe", j, 2 * lv - 2 + d + 1))
                            for hp, e_, pi, dh, re, rp in units(d):
                                a = (dh % 4) * CH
                                ins = e.matmul(bank(2 + d)[rp, a:a + CH], XT[rp, dh, :], Tt[rp, dh, :],
                                               start=True, stop=True)
                            ins.then_inc(sem["X"], 1)
                    for d in range(2):
                        e.wait_ge(sem["Te"], value("Te", j, 2 * lv + d + 1))
                        e.wait_ge(sem["XTe"], value("XTe", j, 2 * lv - 2 + d + 1))
                        for hp, e_, pi, dh, re, rp in units(d):
                            a = (dh % 4) * CH
                            ins = e.matmul(bank(4 + d)[rp, a:a + CH], Tt[rp, dh, :], XT[rp, dh, :],
                                           start=True, stop=True)
                        ins.then_inc(sem["XT"], 1)
                e.wait_ge(sem["w1e"], value("w1e", j, 1))
                e.wait_ge(sem["kh"], value("kh", j, 1))
                for d in range(2):
                    e.wait_ge(sem["XTe"], value("XTe", j, 10 + d + 1))
                    for hp, e_, pi, dh, re, rp in units(d):
                        a = (dh % 4) * 2 * CH
                        ins = e.matmul(bank(6 + d)[rp, a:a + 2 * CH], XT[rp, dh, :], AW[rp, dh, :, :],
                                       start=True, stop=True)
                    ins.then_inc(sem["xa"], 1)
                e.wait_ge(sem["xae"], value("xae", j, 2))
                for half in range(2):
                    for d in range(2):
                        for hp, e_, pi, dh, re, rp in units(d):
                            if pi == half:
                                a = (2 * d + hp) * 2 * CH
                                ins = e.matmul(bank(pi)[re, a:a + 2 * CH], AW[rp, dh, 1, :], MB[rp, dh, 2:0:-1, :],
                                               start=True, stop=True)
                    ins.then_inc(sem["gq"], 1)
                for half in range(2):
                    for d in range(2):
                        for hp, e_, pi, dh, re, rp in units(d):
                            if pi == half:
                                a = (2 * d + hp) * CH
                                vv = vtok[rp, T[d], (2 * hp + e_) * CH:(2 * hp + e_ + 1) * CH]
                                acc = bank(2 + pi)[re, a:a + CH]
                                e.matmul(acc, MB[rp, dh, 2, :], AW[rp, dh, 0, :], start=True, stop=False)
                                ins = e.matmul(acc, MK[rp, dh, 0, :], vv, start=False, stop=True)
                                if has_y(j):
                                    acc = bank(2 + pi)[re, 4 * CH + a:5 * CH + a]
                                    e.matmul(acc, AW[rp, dh, 0, :], MB[rp, dh, 1, :], start=True, stop=False)
                                    ins = e.matmul(acc, vv, MK[rp, dh, 1, :], start=False, stop=True)
                    ins.then_inc(sem["hy"], 1)
                e.wait_ge(sem["gqe"], value("gqe", j, 1))
                for step in range(2):
                    if step and j + 1 < NBATCH:
                        pe_scores(e, j + 1, 0)
                    if step or j or l:
                        e.wait_ge(sem["che"], value("che", j, step))
                    for d in range(2):
                        pi = step if d == 0 else 1 - step
                        for hp in range(2):
                            for e_ in range(2):
                                re = slice(64 * e_, 64 * e_ + 64)
                                a, g = (2 * d + hp) * CH, 4 * d + 2 * hp + pi
                                ins = e.matmul(bank(4 + step)[re, a:a + CH], G[re, g, :], ST[re, 2 * d + hp, :],
                                               start=True, stop=True)
                                if has_y(j):
                                    ins = e.matmul(bank(4 + step)[re, 4 * CH + a:5 * CH + a], ST[re, 2 * d + hp, :],
                                                   QT[re, g, :], start=True, stop=True)
                    ins.then_inc(sem["chS"], 1)

            def dve_scan(v):
                v.memset(ST[:], 0.0)
                v.drain()
                for j in range(NBATCH):
                    dve_batch(v, j)

            def act_scan(a):
                act_exps(a, 0)
                for j in range(NBATCH):
                    act_batch(a, j)

            def pool_scan(g):
                g.wait_ge(S("phase_end"), 3 * phase_of[f"rscan{l}"])
                for j in range(NBATCH):
                    pool_batch(g, j)
            phase_of[f"rscan{l}"] = len(phases)
            phase("rwkv chunks", pe=lambda e: [pe_batch(e, j) for j in range(NBATCH)], act=act_scan, dve=dve_scan,
                  pool=pool_scan)

            y = mix[:, 0:2, :]
            yc = arena2(f"yc{l}", [P, 2, TOK])
            ysq = arena2(f"ysq{l}", [P, 2, TOK], off=6 * K1)
            bon = arena2(f"bon{l}", [P, 2, TOK], off=12 * K1)
            rs = arena2(f"rs{l}", [P, 2, TOK], off=18 * K1)
            ro = Signal("readout_sums", 3)
            rd = Signal("readout_terms", 2)
            ra = Signal("readout_root", 2)
            segs = SEGS[n]

            def pe_read(e):
                for hp in range(2):
                    for s0, s1 in segs:
                        ins = e.matmul(PW[hp][:, s0:s1], headones, y[:, hp, s0:s1], start=True, stop=True)
                ins.then_inc(ro.sem, 1)
                e.wait_ge(rd.sem, rd.at(1))
                for hp in range(2):
                    for s0, s1 in segs:
                        ins = e.matmul(PW[2 + hp][:, s0:s1], headones, bon[:, hp, s0:s1], start=True, stop=True)
                ins.then_inc(ro.sem, 1)
                e.wait_ge(rd.sem, rd.at(2))
                for hp in range(2):
                    for s0, s1 in segs:
                        ins = e.matmul(PW[hp][:, s0:s1], headones, ysq[:, hp, s0:s1], start=True, stop=True)
                ins.then_inc(ro.sem, 1)

            def act_read(a):
                a.wait_ge(ro.sem, ro.at(3))
                for hp in range(2):
                    a.activation(rs[:, hp, 0:n], PW[hp][:, 0:n], ACT.Sqrt, scale=1.0 / CH, bias=epsc[:, 1:2]) \
                     .then_inc(ra.sem, 1)

            def dve_read(v):
                for hp in range(2):
                    v.tensor_tensor(bon[:, hp, 0:n], icl[:, 0, hp, 0:n], icl[:, 1, hp, 0:n], ALU.add)
                v.drain()
                for hp in range(2):
                    v.tensor_scalar(bon[:, hp, 0:n], bon[:, hp, 0:n], col("k_a", hp), scl_ka[:, 2 + hp:3 + hp],
                                    ALU.mult, ALU.add)
                v.drain()
                v.tensor_tensor(bon[:, :, 0:n], bon[:, :, 0:n], k[:, :, 0:n], ALU.mult)
                v.drain()
                for hp in range(2):
                    ins = v.scalar_tensor_tensor(out=bon[:, hp, 0:n], in0=r[:, hp, 0:n], scalar=col("r_k", hp),
                                                 in1=bon[:, hp, 0:n], op0=ALU.mult, op1=ALU.mult)
                ins.then_inc(rd.sem, 1)
                v.wait_ge(ro.sem, ro.at(1))
                for hp in range(2):
                    v.scalar_tensor_tensor(out=yc[:, hp, 0:n], in0=PW[hp][:, 0:n], scalar=-1.0 / CH,
                                           in1=y[:, hp, 0:n], op0=ALU.mult, op1=ALU.add)
                v.drain()
                v.tensor_tensor(ysq[:, :, 0:n], yc[:, :, 0:n], yc[:, :, 0:n], ALU.mult).then_inc(rd.sem, 1)
                v.wait_ge(ra.sem, ra.at(2))
                v.reciprocal(rs[:, :, 0:n], rs[:, :, 0:n])
                for hp in range(2):
                    v.tensor_tensor(bon[:, hp, 0:n], PW[2 + hp][:, 0:n], v_[:, hp, 0:n], ALU.mult)
                v.drain()
                for hp in range(2):
                    v.scalar_tensor_tensor(out=yc[:, hp, 0:n], in0=yc[:, hp, 0:n], scalar=col("ln_g", hp),
                                           in1=rs[:, hp, 0:n], op0=ALU.mult, op1=ALU.mult)
                v.drain()
                for hp in range(2):
                    v.scalar_tensor_tensor(out=yc[:, hp, 0:n], in0=yc[:, hp, 0:n], scalar=col("ln_b", hp),
                                           in1=bon[:, hp, 0:n], op0=ALU.add, op1=ALU.add)
                v.drain()
                v.tensor_tensor(y[:, :, 0:n], yc[:, :, 0:n], z[:, :, 0:n], ALU.mult)
            phase("rwkv readout", pe=pe_read, act=act_read, dve=dve_read)

        phase_of = {}
        before = []
        in_arena = lambda name, shape, off: arena(name, shape, off=48 * K1 + off)
        for l in range(DEPTH):
            full = l < DEPTH - 1
            n = TOK if full else SEQ
            v = lambda kind, l=l: (lambda b, s: scl[:, 3 * l + kind, 2 * b + s:2 * b + s + 1])
            conv_mixer(l, full, before + [pre_norm(f"{l}", TOK, v(0), v(1), before[0]["xnew"] if before else None)])
            attention(l, full)
            rwkv(l, full)
            m = arena(f"m{l}", [P, NB, TOK], off=24 * K1)
            st, total, zero = squares_beside(f"{l}", m, in_arena,
                                             lambda ev: plain(f"wout{l}", t["w_out"][l], 0, 8, n, (hhi, hlo), ev))
            stream_phase(st, before=[zero, split_mix(n)])
            before = [post_norm(f"{l}", m, total, n, v(2))]

        zero_shift = epsc[:, 2:3]
        b2 = lambda name, base=0: (lambda b, s: VC[:, 2, B2ROW[name] + base + b:B2ROW[name] + base + b + 1])
        noshift = lambda b, s: zero_shift
        LR = SEQ + 127
        revd = nc.dram_tensor("rel_bias_reversed", (8, P, LR), F32, kind="Internal").ap()

        def attn2(part, before=()):
            w = t["attn_w_in_2"][0]
            nm = "AB"[part]
            q = arena(f"q2{nm}", [P, 4, SEQ])
            k = arena(f"k2{nm}", [P, 4, SEQ], off=8 * K1)
            vch = arena(f"vc2{nm}", [P, 4, SEQ], off=16 * K1)
            AT = arena(f"AT2{nm}", [P, 4, SEQ], off=16 * K1)
            vtok = arena(f"vt2{nm}", [P, 4, SEQ], off=24 * K1)
            W = arena(f"wk2{nm}", [P, 4, SEQ], off=32 * K1)
            bias = arena(f"bias2{nm}", [P, 8, SEQ], off=40 * K1)
            rb = arena(f"rb2{nm}", [8, 513], off=56 * K1)
            rev = arena(f"rev2{nm}", [8, LR + 1], off=59 * K1)
            c0 = 1536 * part
            qs = plain(f"q2{nm}", w, c0, 4, SEQ, (hhi, hlo), to(q))
            ks = plain(f"k2{nm}", w, c0 + 512, 4, SEQ, (hhi, hlo), to(k))
            vs = plain(f"v2{nm}", w, c0 + 1024, 4, SEQ, (hhi, hlo), to(vch))

            vtu, vts = Signal("v2_turned", 4), Signal("v2_tokens", 4)

            def pe_v(e):
                e.wait_ge(S("evac_done0"), (vs["o0"] + 4) // 2)
                e.wait_ge(S("evac_done1"), (vs["o0"] + 4) // 2)
                for T in range(4):
                    if T >= 2:
                        e.wait_ge(vts.sem, vts.at(T - 1))
                    for h in range(4):
                        ins = e.transpose(bank(4 + T % 2)[:, h * P:(h + 1) * P], vch[:, h, T * P:(T + 1) * P], ident)
                    ins.then_inc(vtu.sem, 1)

            def act_v(a):
                for T in range(4):
                    a.wait_ge(vtu.sem, vtu.at(T + 1))
                    a.activation(vtok[:, T, :], bank(4 + T % 2), ACT.Copy).then_inc(vts.sem, 1)

            if part == 0:
                def pool_bias(pool):
                    pool.wait_ge(S("phase_end"), 3 * phase_of["bias"])
                    pool.wait_ge(*before[-1]["ready"](NB - 1))
                    pool.dma_start(rb[:, :], t["attn_rel_bias_2"][0]).then_inc(S("rel_bias"), 16)
                    pool.wait_ge(S("rel_bias"), 16)
                    pool.tensor_copy(rev[:, 255:LR], rb[:, 512:512 - (LR - 255):-1])
                    pool.tensor_copy(rev[:, 0:255], rb[:, 512:513].to_broadcast([8, 255]))
                    pool.drain()
                    pool.dma_start(revd, rev[:, 0:LR].unsqueeze(1).to_broadcast([8, P, LR])).then_inc(S("rev_stored"), 16)
                    pool.wait_ge(S("rev_stored"), 16)
                    src = bass.AP(revd.tensor, revd.offset + P - 1, [[LR - 1, P], [P * LR, 8], [1, SEQ]])
                    pool.dma_start(bias[:, :, :], src).then_inc(S("bias_tile"), 16)
                    pool.wait_ge(S("bias_tile"), 16)
                    pool.memset(bias[0:64, :, 448:512], -1e30).then_inc(S("bias_ready"), 1)

                phase_of["bias"] = len(phases)
            stream_phase(qs, ks, vs, before=before, pe=pe_v, act=act_v)
            if part == 0:
                phases[-1]["pool"] = pool_bias

            steps = [(h, qt) for h in range(8) for qt in range(4)]
            sg = {n_: S(f"a2{n_}{nm}") for n_ in ("score", "read", "soft", "exps", "prob", "turn", "AT", "pv", "out", "l")}
            scale = 64 ** -0.5
            st = sm[:, 16:32]

            def rows(h):
                return slice(64 * (h % 2), 64 * (h % 2) + 64)

            def pe_score(e, i):
                h, qt = steps[i]
                if i >= 2:
                    e.wait_ge(sg["read"], i - 1)
                e.matmul(bank(i % 2)[:, 0:(qt + 1) * P], q[rows(h), h // 2, qt * P:(qt + 1) * P],
                         k[rows(h), h // 2, 0:(qt + 1) * P], start=True, stop=True).then_inc(sg["score"], 1)

            def values(e, h):
                e.wait_ge(sg["AT"], 4 * h + 4)
                if h >= 4 and h % 2 == 0:
                    e.wait_ge(sg["out"], h // 2 - 1)
                o = bank(4 + (h // 2) % 2)
                for kt in range(4):
                    ins = e.matmul(o[rows(h), kt * P:SEQ], vtok[:, kt, 64 * h:64 * h + 64],
                                   AT[:, kt, kt * P:SEQ], start=kt == 0, stop=kt == 3)
                ins.then_inc(sg["pv"], 1)

            def pe_main(e):
                pe_score(e, 0)
                pe_score(e, 1)
                for i, (h, qt) in enumerate(steps):
                    if i + 2 < len(steps):
                        pe_score(e, i + 2)
                    e.wait_ge(sg["prob"], i + 1)
                    if i >= 2:
                        e.wait_ge(sg["AT"], i - 1)
                    for kt in range(qt + 1):
                        ins = e.transpose(bank(2 + i % 2)[:, kt * P:(kt + 1) * P],
                                          W[:, i % 4, kt * P:(kt + 1) * P], ident)
                    ins.then_inc(sg["turn"], 1)
                    if qt == 0 and h:
                        values(e, h - 1)
                values(e, 7)

            def act_out(a, pair):
                a.activation(mix[:, 4 * part + pair, 0:SEQ], bank(4 + pair % 2), ACT.Copy).then_inc(sg["out"], 1)

            def act_at(a, i):
                h, qt = steps[i]
                a.wait_ge(sg["turn"], i + 1)
                if qt == 0 and h:
                    a.wait_ge(sg["pv"], h)
                    if h % 2 == 0:
                        act_out(a, h // 2 - 1)
                a.activation(AT[:, 0:qt + 1, qt * P:(qt + 1) * P],
                             bank(2 + i % 2)[:, 0:(qt + 1) * P].rearrange("p (a b) -> p a b", b=P), ACT.Copy) \
                 .then_inc(sg["AT"], 1)
                if i == len(steps) - 1:
                    a.wait_ge(sg["pv"], 8)
                    act_out(a, 3)

            if part == 0:
                def act_main(a):
                    for i, (h, qt) in enumerate(steps):
                        N = (qt + 1) * P
                        a.wait_ge(sg["soft"], i + 1)
                        a.activation(W[:, i % 4, 0:N], W[:, i % 4, 0:N], ACT.Exp, bias=st[:, 2 + i % 2:3 + i % 2],
                                     accum_out=st[:, 4 + i % 2:5 + i % 2]).then_inc(sg["exps"], 1)
                        if i:
                            act_at(a, i - 1)
                    act_at(a, len(steps) - 1)

                def dve_main(v):
                    def logits(i):
                        h, qt = steps[i]
                        N = (qt + 1) * P
                        v.wait_ge(sg["score"], i + 1)
                        if i >= 4:
                            v.wait_ge(sg["turn"], i - 3)
                        v.scalar_tensor_tensor(out=W[:, i % 4, 0:N], in0=bank(i % 2)[:, 0:N], scalar=scale,
                                               in1=bias[:, h, SEQ - N:SEQ], op0=ALU.mult, op1=ALU.add) \
                         .then_inc(sg["read"], 1)
                        v.drain()
                        v.reduce_max(st[:, i % 2:i % 2 + 1], W[:, i % 4, 0:N], AXX)
                        v.drain()
                        v.tensor_scalar(st[:, 2 + i % 2:3 + i % 2], st[:, i % 2:i % 2 + 1], -1.0, None, ALU.mult) \
                         .then_inc(sg["soft"], 1)
                    v.wait_ge(S("bias_ready"), 1)
                    logits(0)
                    for i, (h, qt) in enumerate(steps):
                        N = (qt + 1) * P
                        if i + 1 < len(steps):
                            logits(i + 1)
                        v.wait_ge(sg["exps"], i + 1)
                        v.reciprocal(st[:, 6 + i % 2:7 + i % 2], st[:, 4 + i % 2:5 + i % 2])
                        v.drain()
                        v.tensor_scalar(W[:, i % 4, 0:N], W[:, i % 4, 0:N], st[:, 6 + i % 2:7 + i % 2], None, ALU.mult) \
                         .then_inc(sg["prob"], 1)
            else:
                L = arena(f"l2{nm}", [P, 2, SEQ], off=40 * K1)
                NEG = arena(f"n2{nm}", [P, 2, SEQ], off=44 * K1)
                CS = arena(f"c2{nm}", [P, 2, SEQ], off=48 * K1)
                Zs = arena(f"z2{nm}", [P, 2, SEQ], off=52 * K1)

                def act_main(a):
                    a.preload_act_table_set("natural_log_exp_and_others")

                    def soft(i):
                        h, qt = steps[i]
                        N = (qt + 1) * P
                        a.wait_ge(sg["read"], i + 1)
                        if i >= 2:
                            a.wait_ge(sg["soft"], i - 1)
                        a.activation(L[:, i % 2, 0:N], Zs[:, i % 2, 0:N], ACT.Abs)
                        a.drain()
                        a.activation(L[:, i % 2, 0:N], L[:, i % 2, 0:N], ACT.Exp, scale=-1.0)
                        a.drain()
                        a.activation(L[:, i % 2, 0:N], L[:, i % 2, 0:N], ACT.Ln, bias=1.0).then_inc(sg["l"], 1)
                    soft(0)
                    for i, (h, qt) in enumerate(steps):
                        N = (qt + 1) * P
                        if i + 1 < len(steps):
                            soft(i + 1)
                        if i >= 2:
                            act_at(a, i - 2)
                        a.wait_ge(sg["soft"], i + 1)
                        if i >= 4:
                            a.wait_ge(sg["turn"], i - 3)
                        a.activation(W[:, i % 4, 0:N], CS[:, i % 2, 0:N], ACT.Exp).then_inc(sg["exps"], 1)
                    act_at(a, len(steps) - 2)
                    act_at(a, len(steps) - 1)

                def dve_main(v):
                    def zs(i):
                        h, qt = steps[i]
                        N = (qt + 1) * P
                        v.wait_ge(sg["score"], i + 1)
                        if i >= 2:
                            v.wait_ge(sg["l"], i - 1)
                        v.tensor_scalar(Zs[:, i % 2, 0:N], bank(i % 2)[:, 0:N], scale, None, ALU.mult) \
                         .then_inc(sg["read"], 1)
                        v.drain()
                        v.tensor_scalar(NEG[:, i % 2, 0:N], Zs[:, i % 2, 0:N], -1.0, 0.0, ALU.mult, ALU.min)
                        v.drain()
                        v.tensor_tensor(NEG[:, i % 2, N - P:N], NEG[:, i % 2, N - P:N], cc("strict"), ALU.mult)
                    def weights(i):
                        N = (steps[i][1] + 1) * P
                        v.wait_ge(sg["exps"], i + 1)
                        v.tensor_tensor(W[:, i % 4, N - P:N], W[:, i % 4, N - P:N], cc("strict"), ALU.mult) \
                         .then_inc(sg["prob"], 1)
                    zs(0)
                    for i, (h, qt) in enumerate(steps):
                        N = (qt + 1) * P
                        if i + 1 < len(steps):
                            v.drain()
                            zs(i + 1)
                        v.wait_ge(sg["l"], i + 1)
                        v.tensor_tensor(L[:, i % 2, N - P:N], L[:, i % 2, N - P:N], cc("strict"), ALU.mult)
                        v.drain()
                        v.tensor_tensor_scan(CS[:, i % 2, N - 1::-1],
                                             NEG[:, i % 2, N - 1::-1], L[:, i % 2, N - 1::-1], 0.0,
                                             ALU.add, ALU.subtract)
                        v.drain()
                        v.tensor_tensor(CS[:, i % 2, 0:N], CS[:, i % 2, 0:N], Zs[:, i % 2, 0:N], ALU.add) \
                         .then_inc(sg["soft"], 1)
                        if i:
                            weights(i - 1)
                    weights(len(steps) - 1)
            phase("attention 2" + nm, pe=pe_main, act=act_main, dve=dve_main)

        def ffn(l, post):
            fhi = place(f"fhi{l}", [P, FB, SEQ], F32R, at=at_mix)
            flo = place(f"flo{l}", [P, FB, SEQ], F32R, at=at_mix + FB * SEQ * 4)
            assert at_mix + 2 * FB * SEQ * 4 <= nc.sbuf_usable_end
            gb = place(f"gb{l}", [P, 2, SEQ], at=at_mix + 2 * FB * SEQ * 4)
            wg, wu, wd = (kview(t[n_][l]) for n_ in ("ffn_w_gate_2", "ffn_w_up_2", "ffn_w_down_2"))

            def ev_gate(eng, i, o, acc):
                eng.wait_ge(S("evac_done1"), i + evac_base(st_gu))
                return eng.activation(gb[:, 0, :], acc, ACT.Silu)

            def evac_base(st):
                return st["o0"] // 2

            def ev_up(eng, i, o, acc):
                eng.wait_ge(S("evac_done0"), i + (evac_base(st_gu) + 1))
                eng.tensor_tensor(gb[:, 1, :], gb[:, 0, :], acc, ALU.mult)
                eng.drain()
                hi = fhi[:, bass.ds(i, 1), :].rearrange("p a n -> p (a n)")
                eng.tensor_copy(hi, gb[:, 1, :])
                eng.drain()
                lo = flo[:, bass.ds(i, 1), :].rearrange("p a n -> p (a n)")
                return eng.tensor_tensor(lo, gb[:, 1, :], hi.bitcast(F32), ALU.subtract)
            body = [(wg, 0, 8, 0, P, 0, True, True), (wu, 0, 8, 0, P, 1, True, True)]
            st_gu = add_stage(f"gateup{l}", body, FB, SEQ, (hhi, hlo), [("act", ev_gate), ("dve", ev_up)])
            stream_phase(st_gu, before=[post, pre_norm(f"ffn{l}", SEQ, b2("ffn_pre", 8 * l), noshift, post["xnew"])])
            m = arena2(f"mf{l}", [P, NB, SEQ])
            body = []
            for o in range(2):
                for k0, kb in ((0, 8), (8, 8), (16, 6)):
                    body.append((wd, k0, kb, o * P, 2 * P, o, k0 == 0, k0 == 16))
            in_arena2 = lambda name, shape, off: arena2(name, shape, off=16 * K1 + off)
            st, total, zero = squares_beside(f"f{l}", m, in_arena2, lambda ev: add_stage(
                f"down{l}", body, NB // 2, SEQ, (fhi, flo), [("act", ev)] * 2))
            stream_phase(st, before=[zero])
            return post_norm(f"ffn{l}", m, total, SEQ, b2("ffn_post", 8 * l))

        def recurrent(before):
            w = t["rg_w_in_2"][0]
            gate = arena("rggate", [P, NB, SEQ])
            xr = arena("rgx", [P, NB, SEQ], off=16 * K1)
            xc = arena("rgxc", [P, NB, SEQ], off=32 * K1)
            gs = plain("rggate", w, 0, 8, SEQ, (hhi, hlo), to(gate, ACT.Gelu_apprx_tanh))
            xs = plain("rgxr", w, 1024, 8, SEQ, (hhi, hlo), to(xr))
            stream_phase(gs, xs, before=before)
            wa = arena2("rgwa", [P, 8, 256])
            wi = arena2("rgwi", [P, 8, 256], off=8 * K1)
            WK = arena2("rgwork", [P, 2, 6, SEQ], off=16 * K1)
            col = lambda name, i: VC[:, 2, B2ROW[name] + i:B2ROW[name] + i + 1]

            def pool_w(pool):
                pool.wait_ge(S("phase_end"), 3 * phase_of["rg"])
                pool.dma_start(wa[:], t["rg_w_a_2"][0].rearrange("n (k p) j -> p (n k) j", p=P)).then_inc(S("rg_w"), 16)
                pool.dma_start(wi[:], t["rg_w_i_2"][0].rearrange("n (k p) j -> p (n k) j", p=P)).then_inc(S("rg_w"), 16)
            xcr, gm, ga, rd, rs = S("rg_xc"), S("rg_mm"), S("rg_act"), S("rg_dve"), S("rg_sqrt")

            def dve_conv(v):
                def conv_pair(pair):
                    for b in (2 * pair, 2 * pair + 1):
                        v.tensor_scalar(xc[:, b, :], xr[:, b, :], col("rg_conv_w", 24 + b), col("rg_conv_b", b),
                                        ALU.mult, ALU.add)
                    for j in range(3):
                        v.drain()
                        sh = 3 - j
                        for b in (2 * pair, 2 * pair + 1):
                            v.scalar_tensor_tensor(out=xc[:, b, sh:SEQ], in0=xr[:, b, 0:SEQ - sh],
                                                   scalar=col("rg_conv_w", 8 * j + b), in1=xc[:, b, sh:SEQ],
                                                   op0=ALU.mult, op1=ALU.add)
                    v.drain().then_inc(xcr, 1)
                conv_pair(0)
                for b in range(NB):
                    if b % 2 == 0 and b // 2 + 1 < NB // 2:
                        conv_pair(b // 2 + 1)
                    wk = WK[:, b % 2]
                    A, TH, U, MU, I = (wk[:, i, :] for i in range(5))
                    v.wait_ge(ga, b + 1)
                    v.tensor_scalar(MU, TH, 1.0, None, ALU.add)
                    v.drain()
                    v.reciprocal(MU, MU)
                    v.drain()
                    v.scalar_tensor_tensor(out=MU, in0=TH, scalar=2.0, in1=MU, op0=ALU.mult, op1=ALU.mult) \
                     .then_inc(rd, 1)
                    v.tensor_tensor(U, I, xc[:, b, :], ALU.mult)
                    v.drain()
                    v.wait_ge(rs, b + 1)
                    v.tensor_tensor(U, U, MU, ALU.mult)
                    v.drain()
                    v.tensor_tensor_scan(TH, A, U, 0.0, ALU.mult, ALU.add)
                    v.drain()
                    v.tensor_tensor(mix[:, b, 0:SEQ], TH, gate[:, b, :], ALU.mult).then_inc(rd, 1)

            def pe_g(e):
                e.wait_ge(S("rg_w"), 32)
                for b in range(NB):
                    n_, ob = b // 2, b % 2
                    e.wait_ge(xcr, n_ + 1)
                    if b >= 2:
                        e.wait_ge(ga, b - 1)
                    for i, W_ in enumerate((wa, wi)):
                        for k_ in range(2):
                            ins = e.matmul(bank(2 * (b % 2) + i), W_[:, 2 * n_ + k_, ob * P:(ob + 1) * P],
                                           xc[:, 2 * n_ + k_, :], start=k_ == 0, stop=k_ == 1)
                    ins.then_inc(gm, 1)

            def act_g(a):
                def root(b):
                    wk = WK[:, b % 2]
                    a.wait_ge(rd, 2 * b + 1)
                    a.activation(wk[:, 3, :], wk[:, 3, :], ACT.Sqrt).then_inc(rs, 1)
                for b in range(NB):
                    wk = WK[:, b % 2]
                    A, TH, U, MU, I, Rr = (wk[:, i, :] for i in range(6))
                    a.wait_ge(gm, b + 1)
                    if b >= 2:
                        a.wait_ge(rd, 2 * (b - 1))
                    a.activation(Rr, bank(2 * (b % 2)), ACT.Sigmoid, bias=col("b_a", b))
                    a.activation(I, bank(2 * (b % 2) + 1), ACT.Sigmoid, bias=col("b_i", b))
                    a.drain()
                    a.activation(A, Rr, ACT.Exp, scale=scl[:, 6, 8 + b:9 + b])
                    a.activation(TH, Rr, ACT.Tanh, scale=scl[:, 6, b:b + 1]).then_inc(ga, 1)
                    if b:
                        root(b - 1)
                root(NB - 1)
            phase_of["rg"] = len(phases)
            phase("rg gates", pool=pool_w, pe=pe_g, act=act_g, dve=dve_conv)

        attn2(0, before + [pre_norm("mix0", SEQ, b2("mix_pre"), noshift, before[0]["xnew"])])
        attn2(1)
        m0 = arena("mo0", [P, NB, SEQ])
        st, total, zero = squares_beside("b20", m0, in_arena, lambda ev: plain("wout2", t["attn_w_out_2"][0], 0, 8, SEQ,
                                                                               (hhi, hlo), ev))
        stream_phase(st, before=[zero, split_mix(SEQ)])
        last = ffn(0, post_norm("mix0", m0, total, SEQ, b2("mix_post")))
        recurrent([last, pre_norm("mix1", SEQ, b2("mix_pre", 8), noshift, last["xnew"])])
        m1 = arena("mo1", [P, NB, SEQ])
        st, total, zero = squares_beside("b21", m1, in_arena, lambda ev: plain("wout3", t["rg_w_out_2"][0], 0, 8, SEQ,
                                                                               (hhi, hlo), ev))
        stream_phase(st, before=[zero, split_mix(SEQ)])
        last = ffn(1, post_norm("mix1", m1, total, SEQ, b2("mix_post", 8)))
        phase("last norm", **{e: last[e] for e in ("pe", "act", "dve")})

        otok = arena("otok", [P, 4, D])

        def pe_out(e):
            for T in range(4):
                if T >= 2:
                    e.wait_ge(S("out_rows"), T - 1)
                for b in range(NB):
                    ins = e.transpose(PW[T % 2][:, b * P:(b + 1) * P], xT[:, b, T * P:(T + 1) * P], ident)
                ins.then_inc(S("out_turned"), 1)

        def dve_out(v):
            for T in range(4):
                v.wait_ge(S("out_turned"), T + 1)
                v.tensor_copy(otok[:, T, :], PW[T % 2][:, :]).then_inc(S("out_rows"), 1)

        def sp_out(sp):
            for T in range(4):
                sp.wait_ge(S("out_rows"), T + 1)
                sp.dma_start(out[0, T * P:(T + 1) * P, :], otok[:, T, :]).then_inc(S("out_stored"), 16)
            sp.wait_ge(S("out_stored"), 64)
        phase("output", sp=sp_out, pe=pe_out, dve=dve_out)

        def run(eng, which):
            for i, ph in enumerate(phases):
                if which in ph:
                    ph[which](eng)
                eng.drain().then_inc(S("phase_end"), 1)
                eng.wait_ge(S("phase_end"), 3 * (i + 1))

        block = ctx.enter_context(nc.Block())

        @block.sync
        def _(sp):
            for ph in phases:
                if "sp" in ph:
                    ph["sp"](sp)

        @block.gpsimd
        def _(pool):
            for ph in phases:
                if "pool" in ph:
                    ph["pool"](pool)

        @block.tensor
        def _(pe):
            run(pe, "pe")

        @block.scalar
        def _(act):
            run(act, "act")

        @block.vector
        def _(dve):
            run(dve, "dve")


_INS = ["x", "c", "ctx", "c_ctx", "mod_w", "mod_b", "norm_pre_g", "norm_post_g", "w_in", "w_out", "rwkv_w0",
        "rwkv_w_up", "rwkv_a0", "rwkv_a_up", "rwkv_k_k", "rwkv_k_a", "rwkv_r_k", "rwkv_ln_g", "rwkv_ln_b", "conv_w",
        "diff_lambda", "diff_subln_g", "attn_w_in_2", "attn_rel_bias_2", "attn_w_out_2", "rg_w_in_2", "rg_conv_w_2",
        "rg_conv_b_2", "rg_w_a_2", "rg_b_a_2", "rg_w_i_2", "rg_b_i_2", "rg_lambda_2", "rg_w_out_2", "norm_mix_pre_2",
        "norm_mix_post_2", "norm_ffn_pre_2", "norm_ffn_post_2", "ffn_w_gate_2", "ffn_w_up_2", "ffn_w_down_2"]


def kernel(**inputs):
    from concourse import bacc as _bacc
    from concourse.bass_utils import run_bass_kernel_spmd as _run

    nc = _bacc.Bacc("TRN2", target_bir_lowering=False, num_devices=1)
    arrays, t = {}, {}
    for name in _INS:
        a = np.ascontiguousarray(inputs[name])
        arrays[f"in_{name}"] = a
        t[name] = nc.dram_tensor(f"in_{name}", a.shape, mybir.dt.from_np(a.dtype), kind="ExternalInput").ap()
    _, table = constant_columns()
    arrays["shape_constants"] = table
    t["const"] = nc.dram_tensor("shape_constants", table.shape, F32, kind="ExternalInput").ap()
    out = nc.dram_tensor("out_0", (1, SEQ, D), F32, kind="ExternalOutput").ap()
    build_program(nc, t, out)
    r = _run(nc, [arrays], core_ids=[0])
    return r.results[0]["out_0"]
```
